# Optimizing a Trainium2 kernel written in Bass

```python
import math
import jax, jax.numpy as jnp
from jax import lax
import numpy as np

D_MODEL = 1024
BATCH = 1
SEQ = 512
DEPTH = 2

N_MIXERS = 2
N_SSD_LAYERS = (DEPTH + 1) // 2
N_HGRN_LAYERS = DEPTH // 2

SSD_EXPAND = 2
SSD_D_INNER = SSD_EXPAND * D_MODEL
SSD_HEAD_DIM = 64
SSD_N_HEADS = SSD_D_INNER // SSD_HEAD_DIM
SSD_N_GROUPS = 4
SSD_HEADS_PER_GROUP = SSD_N_HEADS // SSD_N_GROUPS
SSD_D_STATE = 128
SSD_CONV_WIDTH = 4
SSD_CHUNK = 128
SSD_BC_DIM = SSD_N_GROUPS * SSD_D_STATE
SSD_CONV_DIM = SSD_D_INNER + 2 * SSD_BC_DIM
SSD_IN_DIM = SSD_D_INNER + SSD_CONV_DIM + SSD_N_HEADS

HGRN_EXPAND = 128
HGRN_N_HEADS = D_MODEL // HGRN_EXPAND
HGRN_HEAD_V = D_MODEL // HGRN_N_HEADS
HGRN_CHUNK = 64
HGRN_IN_DIM = 4 * D_MODEL

D_FF = 4 * D_MODEL
PLE_DIM = 256
DEEPNORM_ALPHA = (2.0 * DEPTH) ** 0.25
DEEPNORM_BETA = (8.0 * DEPTH) ** -0.25
LN_EPS = 1e-5
RMS_EPS = 1e-5


def layer_norm(x, g, b):
    xf = x.astype(jnp.float32)
    mu = jnp.mean(xf, axis=-1, keepdims=True)
    xc = xf - mu
    var = jnp.mean(xc * xc, axis=-1, keepdims=True)
    y = xc * lax.rsqrt(var + LN_EPS) * g.astype(jnp.float32) + b.astype(jnp.float32)
    return y.astype(x.dtype)

def rms_norm(x, w):
    xf = x.astype(jnp.float32)
    return xf * lax.rsqrt(jnp.mean(xf * xf, axis=-1, keepdims=True) + RMS_EPS) * w.astype(jnp.float32)

def causal_depthwise_conv(u, w, b):
    k, c = w.shape
    out = lax.conv_general_dilated(u, w[:, None, :].astype(u.dtype), window_strides=(1,),
                                   padding=[(k - 1, 0)], dimension_numbers=('NWC', 'WIO', 'NWC'),
                                   feature_group_count=c)
    return out + b

def segsum_exp(a):
    t = a.shape[-1]
    cs = jnp.cumsum(a, axis=-1)
    seg = cs[..., :, None] - cs[..., None, :]
    mask = jnp.tril(jnp.ones((t, t), dtype=bool))
    return jnp.exp(jnp.where(mask, seg, -jnp.inf))

def ssd_mixer(u, w_in, conv_w, conv_b, dt_bias, a_log, d_skip, norm_w, w_out):
    bsz, seq, _ = u.shape
    nc = seq // SSD_CHUNK
    g_, r_, p_, n_ = SSD_N_GROUPS, SSD_HEADS_PER_GROUP, SSD_HEAD_DIM, SSD_D_STATE
    zxbcdt = u @ w_in
    z, xbc, dt = jnp.split(zxbcdt, [SSD_D_INNER, SSD_D_INNER + SSD_CONV_DIM], axis=-1)
    xbc = jax.nn.silu(causal_depthwise_conv(xbc, conv_w, conv_b))
    xs, bm, cm = jnp.split(xbc, [SSD_D_INNER, SSD_D_INNER + SSD_BC_DIM], axis=-1)
    xs = xs.astype(jnp.float32).reshape(bsz, nc, SSD_CHUNK, g_, r_, p_)
    bm = bm.astype(jnp.float32).reshape(bsz, nc, SSD_CHUNK, g_, n_)
    cm = cm.astype(jnp.float32).reshape(bsz, nc, SSD_CHUNK, g_, n_)
    dt = jax.nn.softplus(dt.astype(jnp.float32) + dt_bias.astype(jnp.float32))
    a = -jnp.exp(a_log.astype(jnp.float32))
    dt = dt.reshape(bsz, nc, SSD_CHUNK, g_, r_)
    da = dt * a.reshape(g_, r_)
    xdt = xs * dt[..., None]
    a_cs = jnp.cumsum(da, axis=2)
    decay = segsum_exp(jnp.moveaxis(da, 2, -1))
    cb = jnp.einsum('bclgn,bcsgn->bcgls', cm, bm)
    y_diag = jnp.einsum('bcgls,bcgrls,bcsgrp->bclgrp', cb, decay, xdt)
    decay_to_end = jnp.exp(a_cs[:, :, -1:] - a_cs)
    states = jnp.einsum('bclgn,bclgr,bclgrp->bcgrpn', bm, decay_to_end, xdt)
    chunk_decay = jnp.exp(a_cs[:, :, -1])

    def step(h, inp):
        st, dec = inp
        return h * dec[..., None, None] + st, h

    h0 = jnp.zeros((bsz, g_, r_, p_, n_), jnp.float32)
    _, prev = lax.scan(step, h0, (jnp.moveaxis(states, 1, 0), jnp.moveaxis(chunk_decay, 1, 0)))
    prev = jnp.moveaxis(prev, 0, 1)
    y_off = jnp.einsum('bclgn,bcgrpn,bclgr->bclgrp', cm, prev, jnp.exp(a_cs))
    y = y_diag + y_off + d_skip.astype(jnp.float32).reshape(g_, r_)[:, :, None] * xs
    y = y.reshape(bsz, seq, SSD_D_INNER) * jax.nn.silu(z.astype(jnp.float32))
    y = rms_norm(y.reshape(bsz, seq, g_, SSD_D_INNER // g_), norm_w.reshape(g_, SSD_D_INNER // g_))
    y = y.reshape(bsz, seq, SSD_D_INNER).astype(u.dtype)
    return y @ w_out

def hgrn2_mixer(u, w_in, lb, norm_w, w_out):
    bsz, seq, _ = u.shape
    nc = seq // HGRN_CHUNK
    h_, k_dim, v_dim, c_ = HGRN_N_HEADS, HGRN_EXPAND, HGRN_HEAD_V, HGRN_CHUNK
    q, fz, v, g = jnp.split(u @ w_in, 4, axis=-1)
    fz = fz.astype(jnp.float32)
    lb = lb.astype(jnp.float32)
    log_f = jnp.logaddexp(jnp.log(lb), jnp.log1p(-lb) + jax.nn.log_sigmoid(fz))
    k = (1.0 - lb) * jax.nn.sigmoid(-fz)

    def chunked(t, d):
        return jnp.moveaxis(t.astype(jnp.float32).reshape(bsz, nc, c_, h_, d), 1, 0)

    qc, kc, vc = chunked(q, k_dim), chunked(k, k_dim), chunked(v, v_dim)
    b_cs = jnp.cumsum(chunked(log_f, k_dim), axis=2)
    mask = jnp.tril(jnp.ones((c_, c_), dtype=bool))[None, :, :, None, None]

    def step(s_prev, inp):
        q_, kk, v_, b_ = inp
        diff = b_[:, :, None] - b_[:, None, :]
        dec = jnp.exp(jnp.where(mask, diff, -jnp.inf))
        scores = jnp.einsum('blhk,bshk,blshk->bhls', q_, kk, dec)
        o = jnp.einsum('bhls,bshv->blhv', scores, v_) + jnp.einsum('blhk,bhkv->blhv', q_ * jnp.exp(b_), s_prev)
        b_last = b_[:, -1]
        s_new = jnp.exp(b_last)[..., None] * s_prev + jnp.einsum(
            'bshk,bshv->bhkv', kk * jnp.exp(b_last[:, None] - b_), v_)
        return s_new, o

    s0 = jnp.zeros((bsz, h_, k_dim, v_dim), jnp.float32)
    _, o = lax.scan(step, s0, (qc, kc, vc, b_cs))
    o = jnp.moveaxis(o, 0, 1).reshape(bsz, seq, h_, v_dim)
    o = rms_norm(o, norm_w).reshape(bsz, seq, D_MODEL) * jax.nn.silu(g.astype(jnp.float32))
    return o.astype(u.dtype) @ w_out

def sq_relu_mlp(h, w1, w2):
    a = jax.nn.relu(h @ w1)
    return (a * a) @ w2

def first_inputs(seed: int = 0) -> dict:
    key = jax.random.key(seed)
    ks = jax.random.split(key, 20)
    f32 = jnp.float32
    nrm = lambda k, shape, s: jax.random.normal(k, shape, f32) * s
    x = jax.random.normal(ks[0], (BATCH, SEQ, D_MODEL), f32)
    p = jax.random.normal(ks[1], (DEPTH, BATCH, SEQ, PLE_DIM), f32)
    ssd_w_in = nrm(ks[2], (N_SSD_LAYERS, D_MODEL, SSD_IN_DIM), D_MODEL ** -0.5)
    ssd_conv_w = nrm(ks[3], (N_SSD_LAYERS, SSD_CONV_WIDTH, SSD_CONV_DIM), SSD_CONV_WIDTH ** -0.5)
    ssd_conv_b = nrm(ks[4], (N_SSD_LAYERS, SSD_CONV_DIM), 0.02)
    dt0 = jnp.exp(jax.random.uniform(ks[5], (N_SSD_LAYERS, SSD_N_HEADS), f32,
                                     math.log(1e-3), math.log(1e-1)))
    ssd_dt_bias = dt0 + jnp.log(-jnp.expm1(-dt0))
    ssd_a_log = jnp.log(jax.random.uniform(ks[6], (N_SSD_LAYERS, SSD_N_HEADS), f32, 1.0, 16.0))
    ssd_d = 1.0 + nrm(ks[7], (N_SSD_LAYERS, SSD_N_HEADS), 0.02)
    ssd_norm_w = 1.0 + nrm(ks[8], (N_SSD_LAYERS, SSD_D_INNER), 0.02)
    ssd_w_out = nrm(ks[9], (N_SSD_LAYERS, SSD_D_INNER, D_MODEL), SSD_D_INNER ** -0.5 * DEEPNORM_BETA)
    hgrn_w_in = nrm(ks[10], (N_HGRN_LAYERS, D_MODEL, HGRN_IN_DIM), D_MODEL ** -0.5)
    hgrn_lower_bounds = nrm(ks[11], (N_HGRN_LAYERS, D_MODEL), 0.1)
    hgrn_norm_w = 1.0 + nrm(ks[12], (N_HGRN_LAYERS, HGRN_HEAD_V), 0.02)
    hgrn_w_out = nrm(ks[13], (N_HGRN_LAYERS, D_MODEL, D_MODEL), D_MODEL ** -0.5 * DEEPNORM_BETA)
    ln_g = 1.0 + nrm(ks[14], (DEPTH, 2, D_MODEL), 0.02)
    ln_b = nrm(ks[15], (DEPTH, 2, D_MODEL), 0.02)
    mlp_w1 = nrm(ks[16], (DEPTH, D_MODEL, D_FF), D_MODEL ** -0.5)
    mlp_w2 = nrm(ks[17], (DEPTH, D_FF, D_MODEL), D_FF ** -0.5 * DEEPNORM_BETA)
    ple_w_proj = nrm(ks[18], (DEPTH, PLE_DIM, D_MODEL), PLE_DIM ** -0.5)
    ple_w_gate = nrm(ks[19], (DEPTH, D_MODEL, D_MODEL), D_MODEL ** -0.5)
    return {"x": x, "p": p, "ssd_w_in": ssd_w_in, "ssd_conv_w": ssd_conv_w, "ssd_conv_b": ssd_conv_b,
            "ssd_dt_bias": ssd_dt_bias, "ssd_a_log": ssd_a_log, "ssd_d": ssd_d, "ssd_norm_w": ssd_norm_w,
            "ssd_w_out": ssd_w_out, "hgrn_w_in": hgrn_w_in, "hgrn_lower_bounds": hgrn_lower_bounds,
            "hgrn_norm_w": hgrn_norm_w, "hgrn_w_out": hgrn_w_out, "ln_g": ln_g, "ln_b": ln_b,
            "mlp_w1": mlp_w1, "mlp_w2": mlp_w2, "ple_w_proj": ple_w_proj, "ple_w_gate": ple_w_gate}

def first_block(x, p, ssd_w_in, ssd_conv_w, ssd_conv_b, ssd_dt_bias, ssd_a_log, ssd_d, ssd_norm_w,
              ssd_w_out, hgrn_w_in, hgrn_lower_bounds, hgrn_norm_w, hgrn_w_out, ln_g, ln_b,
              mlp_w1, mlp_w2, ple_w_proj, ple_w_gate):
    lbs = jnp.cumsum(jax.nn.softmax(hgrn_lower_bounds.astype(jnp.float32), axis=0), axis=0)
    lbs = lbs - lbs[0:1]
    for i in range(DEPTH):
        j = i // N_MIXERS
        if i % N_MIXERS == 0:
            mix = ssd_mixer(x, ssd_w_in[j], ssd_conv_w[j], ssd_conv_b[j], ssd_dt_bias[j], ssd_a_log[j],
                            ssd_d[j], ssd_norm_w[j], ssd_w_out[j])
        else:
            mix = hgrn2_mixer(x, hgrn_w_in[j], lbs[j], hgrn_norm_w[j], hgrn_w_out[j])
        h = layer_norm(DEEPNORM_ALPHA * x + mix, ln_g[i, 0], ln_b[i, 0])
        h = layer_norm(DEEPNORM_ALPHA * h + sq_relu_mlp(h, mlp_w1[i], mlp_w2[i]), ln_g[i, 1], ln_b[i, 1])
        x = h + jax.nn.sigmoid(h @ ple_w_gate[i]) * (p[i] @ ple_w_proj[i])
    return x


DEPTH_2 = 1

N_MEM = 256
MIX_WIDTH = D_MODEL
MEM_HEADS = 4
MEM_WIDTH = MIX_WIDTH // 4
MEM_HEAD_DIM = MEM_WIDTH // MEM_HEADS
MAIN_WIDTH = MIX_WIDTH - MEM_WIDTH
MLA_HEADS = 12
QK_NOPE = 64
QK_ROPE = 32
V_HEAD = MAIN_WIDTH // MLA_HEADS
Q_LORA = (3 * D_MODEL) // 8
KV_LORA = D_MODEL // 4
ROPE_THETA = 10000.0
Q_BLOCK = 128
FNET_GROUPS = 4
FNET_GROUP_DIM = MAIN_WIDTH // FNET_GROUPS
EPS = 1e-6

MLA_IN = Q_LORA + KV_LORA + QK_ROPE + MEM_WIDTH + MIX_WIDTH
FNET_IN = MAIN_WIDTH + MEM_WIDTH + MIX_WIDTH


def rmsnorm(x, g):
    xf = x.astype(jnp.float32)
    y = xf * lax.rsqrt(jnp.mean(xf * xf, axis=-1, keepdims=True) + EPS)
    return (y * g.astype(jnp.float32)).astype(x.dtype)

def rope_tables(positions):
    inv_freq = 1.0 / (ROPE_THETA ** (jnp.arange(0, QK_ROPE, 2, dtype=jnp.float32) / QK_ROPE))
    ang = positions.astype(jnp.float32)[..., None] * inv_freq
    return jnp.cos(ang), jnp.sin(ang)

def apply_rope(t, cos, sin):
    tf = t.astype(jnp.float32)
    t1, t2 = tf[..., : QK_ROPE // 2], tf[..., QK_ROPE // 2:]
    return jnp.concatenate([t1 * cos - t2 * sin, t2 * cos + t1 * sin], axis=-1).astype(t.dtype)

def mla_attention(q_nope, q_rope, k_nope, k_rope, v):
    B, S, H, _ = q_nope.shape
    nb = S // Q_BLOCK
    scale = 1.0 / float(np.sqrt(QK_NOPE + QK_ROPE))

    def to_blocks(t):
        return jnp.moveaxis(t.reshape((B, nb, Q_BLOCK) + t.shape[2:]), 1, 0)

    def one_block(args):
        qn, qr = args
        s = (jnp.einsum('bqhd,bkhd->bhqk', qn, k_nope)
             + jnp.einsum('bqhr,bkr->bhqk', qr, k_rope)).astype(jnp.float32) * scale
        p = jax.nn.softmax(s, axis=-1).astype(v.dtype)
        return jnp.einsum('bhqk,bkhd->bqhd', p, v)

    out = lax.map(one_block, (to_blocks(q_nope), to_blocks(q_rope)))
    return jnp.moveaxis(out, 0, 1).reshape(B, S, H * V_HEAD)

def memory_cross_attention(q_mem, mem, mem_norm_g, w_mem_kv):
    B, S, _ = q_mem.shape
    q = q_mem.reshape(B, S, MEM_HEADS, MEM_HEAD_DIM)
    kv = (rmsnorm(mem, mem_norm_g) @ w_mem_kv).reshape(B, mem.shape[1], 2, MEM_HEADS, MEM_HEAD_DIM)
    k, v = kv[:, :, 0], kv[:, :, 1]
    s = jnp.einsum('bshd,bmhd->bhsm', q, k).astype(jnp.float32) * (1.0 / float(np.sqrt(MEM_HEAD_DIM)))
    p = jax.nn.softmax(s, axis=-1).astype(v.dtype)
    return jnp.einsum('bhsm,bmhd->bshd', p, v).reshape(B, S, MEM_WIDTH)

def mla_layer(x, mem, cos, sin, norm_g, w_in, q_norm_g, kv_norm_g, w_uq, w_ukv,
              mem_norm_g, w_mem_kv, w_out):
    B, S, _ = x.shape
    h = rmsnorm(x, norm_g)
    proj = h @ w_in
    o1 = Q_LORA
    o2 = o1 + KV_LORA
    o3 = o2 + QK_ROPE
    o4 = o3 + MEM_WIDTH
    c_q, c_kv, k_rope = proj[..., :o1], proj[..., o1:o2], proj[..., o2:o3]
    q_mem, gate = proj[..., o3:o4], proj[..., o4:]
    q = (rmsnorm(c_q, q_norm_g) @ w_uq).reshape(B, S, MLA_HEADS, QK_NOPE + QK_ROPE)
    kv = (rmsnorm(c_kv, kv_norm_g) @ w_ukv).reshape(B, S, MLA_HEADS, QK_NOPE + V_HEAD)
    q_nope = q[..., :QK_NOPE]
    q_rope = apply_rope(q[..., QK_NOPE:], cos[:, :, None, :], sin[:, :, None, :])
    k_nope, v = kv[..., :QK_NOPE], kv[..., QK_NOPE:]
    k_rope = apply_rope(k_rope, cos, sin)
    attn = mla_attention(q_nope, q_rope, k_nope, k_rope, v)
    mem_out = memory_cross_attention(q_mem, mem, mem_norm_g, w_mem_kv)
    branch = jnp.concatenate([attn, mem_out], axis=-1) * jax.nn.silu(gate)
    return x + branch @ w_out

def fnet_layer(x, mem, norm_g, w_in, w_fnet, mem_norm_g, w_mem_kv, w_out):
    B, S, _ = x.shape
    h = rmsnorm(x, norm_g)
    proj = h @ w_in
    f = proj[..., :MAIN_WIDTH].reshape(B, S, FNET_GROUPS, FNET_GROUP_DIM).astype(jnp.float32)
    q_mem = proj[..., MAIN_WIDTH:MAIN_WIDTH + MEM_WIDTH]
    gate = proj[..., MAIN_WIDTH + MEM_WIDTH:]
    spec = jnp.fft.fft2(f, axes=(1, 3), norm='ortho').real
    mixed = jnp.einsum('bsgc,gcd->bsgd', spec, w_fnet.astype(jnp.float32))
    mixed = mixed.reshape(B, S, MAIN_WIDTH).astype(x.dtype)
    mem_out = memory_cross_attention(q_mem, mem, mem_norm_g, w_mem_kv)
    branch = jnp.concatenate([mixed, mem_out], axis=-1) * jax.nn.silu(gate)
    return x + branch @ w_out

def second_inputs(seed: int = 0) -> dict:
    key = jax.random.key(seed)
    ks = jax.random.split(key, 24)
    f32 = jnp.float32

    def w(k, shape, fan_in):
        return jax.random.normal(k, shape, f32) * (fan_in ** -0.5)

    def gain(k, n):
        return 1.0 + 0.02 * jax.random.normal(k, (n,), f32)

    x = jax.random.normal(ks[0], (BATCH, SEQ, D_MODEL), f32)
    mem = jax.random.normal(ks[1], (BATCH, N_MEM, D_MODEL), f32)
    offsets = jax.random.randint(ks[2], (BATCH, 1), 0, 1024, dtype=jnp.int32)
    positions = (jnp.arange(SEQ, dtype=jnp.int32)[None, :] + offsets).astype(jnp.int32)
    return {
        "x": x,
        "mem": mem,
        "positions": positions,
        "norm_g_l0": gain(ks[3], D_MODEL),
        "w_in_l0": w(ks[4], (D_MODEL, MLA_IN), D_MODEL),
        "q_norm_g_l0": gain(ks[5], Q_LORA),
        "kv_norm_g_l0": gain(ks[6], KV_LORA),
        "w_uq_l0": w(ks[7], (Q_LORA, MLA_HEADS * (QK_NOPE + QK_ROPE)), Q_LORA),
        "w_ukv_l0": w(ks[8], (KV_LORA, MLA_HEADS * (QK_NOPE + V_HEAD)), KV_LORA),
        "mem_norm_g_l0": gain(ks[9], D_MODEL),
        "w_mem_kv_l0": w(ks[10], (D_MODEL, 2 * MEM_WIDTH), D_MODEL),
        "w_out_l0": w(ks[11], (MIX_WIDTH, D_MODEL), MIX_WIDTH),
        "norm_g_l1": gain(ks[12], D_MODEL),
        "w_in_l1": w(ks[13], (D_MODEL, FNET_IN), D_MODEL),
        "w_fnet_l1": w(ks[14], (FNET_GROUPS, FNET_GROUP_DIM, FNET_GROUP_DIM), FNET_GROUP_DIM),
        "mem_norm_g_l1": gain(ks[15], D_MODEL),
        "w_mem_kv_l1": w(ks[16], (D_MODEL, 2 * MEM_WIDTH), D_MODEL),
        "w_out_l1": w(ks[17], (MIX_WIDTH, D_MODEL), MIX_WIDTH),
        "final_norm_g": gain(ks[18], D_MODEL),
    }

def second_block(x, mem, positions,
              norm_g_l0, w_in_l0, q_norm_g_l0, kv_norm_g_l0, w_uq_l0, w_ukv_l0,
              mem_norm_g_l0, w_mem_kv_l0, w_out_l0,
              norm_g_l1, w_in_l1, w_fnet_l1, mem_norm_g_l1, w_mem_kv_l1, w_out_l1,
              final_norm_g):
    cos, sin = rope_tables(positions)
    for i in range(DEPTH_2):
        if i % N_MIXERS == 0:
            x = mla_layer(x, mem, cos, sin, norm_g_l0, w_in_l0, q_norm_g_l0, kv_norm_g_l0,
                          w_uq_l0, w_ukv_l0, mem_norm_g_l0, w_mem_kv_l0, w_out_l0)
        else:
            x = fnet_layer(x, mem, norm_g_l1, w_in_l1, w_fnet_l1,
                           mem_norm_g_l1, w_mem_kv_l1, w_out_l1)
    return rmsnorm(x, final_norm_g)


def setup_inputs(seed=0):
    out = dict(first_inputs(seed))
    for name, value in second_inputs(seed + 1).items():
        if name != "x":
            out[name + "_2"] = value
    return out


def reference(
    x, p, ssd_w_in, ssd_conv_w, ssd_conv_b, ssd_dt_bias, ssd_a_log, ssd_d, ssd_norm_w,
    ssd_w_out, hgrn_w_in, hgrn_lower_bounds, hgrn_norm_w, hgrn_w_out, ln_g, ln_b, mlp_w1,
    mlp_w2, ple_w_proj, ple_w_gate, mem_2, positions_2, norm_g_l0_2, w_in_l0_2, q_norm_g_l0_2,
    kv_norm_g_l0_2, w_uq_l0_2, w_ukv_l0_2, mem_norm_g_l0_2, w_mem_kv_l0_2, w_out_l0_2,
    norm_g_l1_2, w_in_l1_2, w_fnet_l1_2, mem_norm_g_l1_2, w_mem_kv_l1_2, w_out_l1_2,
    final_norm_g_2,
):
    x = first_block(
        x, p, ssd_w_in, ssd_conv_w, ssd_conv_b, ssd_dt_bias, ssd_a_log, ssd_d, ssd_norm_w,
        ssd_w_out, hgrn_w_in, hgrn_lower_bounds, hgrn_norm_w, hgrn_w_out, ln_g, ln_b, mlp_w1,
        mlp_w2, ple_w_proj, ple_w_gate,
    )
    return second_block(
        x, mem_2, positions_2, norm_g_l0_2, w_in_l0_2, q_norm_g_l0_2, kv_norm_g_l0_2, w_uq_l0_2,
        w_ukv_l0_2, mem_norm_g_l0_2, w_mem_kv_l0_2, w_out_l0_2, norm_g_l1_2, w_in_l1_2,
        w_fnet_l1_2, mem_norm_g_l1_2, w_mem_kv_l1_2, w_out_l1_2, final_norm_g_2,
    )


_drawn_inputs = setup_inputs


def setup_inputs(seed=0):
    import zlib

    import numpy as np

    out = dict(_drawn_inputs(seed))
    spreads = {}
    factors = {'ssd_conv_b': 6.378,
     'ssd_d': 8.0,
     'ssd_norm_w': 8.0,
     'hgrn_norm_w': 8.0,
     'norm_g_l0_2': 8.0,
     'q_norm_g_l0_2': 8.0,
     'kv_norm_g_l0_2': 8.0,
     'mem_norm_g_l0_2': 8.0,
     'final_norm_g_2': 2.785}
    for name, (base, spread) in spreads.items():
        noise = np.random.default_rng([zlib.crc32(name.encode()), seed]).standard_normal(out[name].shape)
        drawn = base * np.exp(spread * noise) if base else spread * noise
        out[name] = __import__('jax').numpy.asarray(drawn.astype(out[name].dtype))
    for name, factor in factors.items():
        out[name] = (out[name] * factor).astype(out[name].dtype)
    return out
```

```python
from contextlib import ExitStack

import numpy as np

import concourse.bass as bass
from concourse import mybir

ALU = mybir.AluOpType
ACT = mybir.ActivationFunctionType
AX = mybir.AxisListType
F32 = mybir.dt.float32
I32 = mybir.dt.int32
ds = bass.ds

P = 128
T = 512
NT = T // P
D = 1024
KD = D // P
HALF = 512
NHALF = D // HALF
DEPTH = 2
ALPHA = (2.0 * DEPTH) ** 0.25
LN_EPS = 1e-5
RMS_EPS = 1e-5
EPS = 1e-6
ARENA = 26000
DFF = 4 * D
KF = DFF // P
PLE = 256
KP = PLE // P

S_IN = 2 * D
S_HEADS, S_P, S_GROUPS, S_N = 32, 64, 4, 128
S_HPG = S_HEADS // S_GROUPS
S_Z, S_X, S_B = 0, S_IN, 2 * S_IN
S_C = S_B + S_GROUPS * S_N
S_DT = S_C + S_GROUPS * S_N
KS = S_IN // P
CONV_BLOCKS = 24
TAPS = 4

H_HEADS = 8
LEVELS = 7

NMEM = 256
MT = NMEM // P
Q_LORA, KV_LORA, ROPE = 384, 256, 32
HR = ROPE // 2
NOPE, V_HEAD = 64, 64
QK = NOPE + ROPE
A_HEADS, M_HEADS, M_HEAD = 12, 4, 64
MEM_W = 256
KQ, KKV = Q_LORA // P, KV_LORA // P
A_SCALE = 1.0 / float(np.sqrt(QK))
M_SCALE = 1.0 / float(np.sqrt(M_HEAD))
O_KV, O_QM, O_GATE = Q_LORA, Q_LORA + KV_LORA + ROPE, Q_LORA + KV_LORA + ROPE + MEM_W

C_ID, C_TRI, C_ONE, C_MASK = 0, P, 2 * P, 3 * P
C_FREQ = C_MASK + (LEVELS + 1) * P
C_ALL = C_FREQ + HR
A_CW, A_CB, A_ROWS = 0, TAPS * CONV_BLOCKS, (TAPS + 1) * CONV_BLOCKS
B_G, B_B, B_SN, B_NG, B_MG, B_QG, B_KG, B_HG = 0, 32, 64, 80, 88, 96, 99, 101
B_ROWS = 102

TWO_PI = 2.0 * np.pi
PI_A = 6.28125
PI_B = float(np.float32(TWO_PI - PI_A))
PI_C = float(TWO_PI - PI_A - PI_B)
MAGIC = 1.5 * 2.0 ** 23
PI_CAP = 3.1415925


def shape_constants():
    c = np.zeros((P, C_ALL), np.float32)
    r = np.arange(P)
    c[:, C_ID:C_ID + P] = np.eye(P)
    c[:, C_TRI:C_TRI + P] = r[:, None] <= r[None, :]
    c[:, C_ONE:C_ONE + P] = 1.0
    for n in range(LEVELS):
        h = 64 >> n
        s, l = r[:, None], r[None, :]
        c[:, C_MASK + n * P:C_MASK + (n + 1) * P] = (s // (2 * h) == l // (2 * h)) & (s % (2 * h) < h) & (l % (2 * h) >= h)
    c[:, C_MASK + LEVELS * P:C_MASK + (LEVELS + 1) * P] = np.eye(P)
    c[:, C_FREQ:] = (1.0 / (10000.0 ** (np.arange(0, ROPE, 2, dtype=np.float32) / np.float32(ROPE)))).astype(np.float32)
    return c


class Banks:

    def __init__(self):
        self.before = [0] * 8
        self.table = {}

    def stage(self, stage, uses, turns=1):
        per = [0] * 8
        for name, b in uses:
            self.table[stage, name] = (b, self.before[b] + per[b], b)
            per[b] += 1
        for name, b in uses:
            bank, first, _ = self.table[stage, name]
            self.table[stage, name] = (bank, first, per[bank])
        for b in range(8):
            self.before[b] += per[b] * turns

    def at(self, stage, name, i=0):
        bank, first, per = self.table[stage, name]
        return bank, first + i * per


def first_and_last(k, n):
    return {"start": k == 0, "stop": k == n - 1}


def build(nc, x, p, cst, par_a, par_b, w_ssd, w_dt, dt_bias, a_log, d_skip, w_ssd_out, w_hgrn, w_hgrn_out,
          ln_g, ln_b, w_mlp1, w_mlp2, w_gate, w_proj, mem, pos, w_mla, w_uq, w_ukv, w_mem, w_mla_out, fin_g, out):
    with ExitStack() as ctx:
        def sb(name, shape, dt=F32):
            return ctx.enter_context(nc.sbuf_tensor(name, shape, dt))

        def sem(name):
            return ctx.enter_context(nc.semaphore(name))

        slots = [sb(f"slot{s}", [P, 4096]) for s in range(2)]
        res = sb("res", [P, NT, D])
        rn = sb("rn", [P, NT, D])
        fT = sb("fT", [P, KD, T])
        gb = sb("gb", [P, 2, D])
        con = sb("con", [P, C_ALL])
        col_a = sb("col_a", [P, A_ROWS])
        col_b = sb("col_b", [P, B_ROWS])
        eps_h = sb("eps_h", [P, 1])
        pT = sb("pT", [P, DEPTH, KP, T])
        st6 = sb("st6", [P, NT, 2, 6])
        mv = sb("mv", [P, NT, 2])
        ms = sb("ms", [P, NT, 3])
        arena = sb("arena", [P, ARENA])
        psum = ctx.enter_context(nc.psum_tensor("psum", [P, 8, HALF], F32))
        ident = con[:, C_ID:C_ID + P]
        tri = con[:, C_TRI:C_TRI + P]
        ones = con[:, C_ONE:C_ONE + P]

        at = [0]

        def carve(*shape):
            n = int(np.prod(shape))
            assert at[0] + n <= ARENA, (at[0], n)
            v = arena[:, at[0]:at[0] + n]
            at[0] += n
            if len(shape) == 2:
                v = v.rearrange("p (a b) -> p a b", a=shape[0])
            if len(shape) == 3:
                v = v.rearrange("p (a b c) -> p a b c", a=shape[0], b=shape[1])
            return v

        s_par = carve(2, P)
        s_p = carve(DEPTH * NT, PLE)
        at[0] = 0
        BT = carve(T)
        CT = carve(T)
        Btok = carve(NT, P)
        CBm = carve(NT, P)
        cv = carve(3, T)
        xr = carve(NT, HALF)
        xdt = carve(NT, HALF)
        xw = carve(NT, HALF)
        Mh = carve(S_HPG, T)
        zs = carve(NT, HALF)
        prev = carve(NT - 1, HALF)
        rows = carve(2, T)
        ybuf = carve(HALF)
        yoff = carve(HALF)
        y_hi = carve(2, S_IN)
        wdt = carve(KD, S_HEADS)
        small = carve(5, S_HEADS)
        dbias, aneg, dskip, dtmp, _ = [small[:, n, :] for n in range(5)]
        dt_all = carve(NT, S_HEADS)
        da = carve(NT, S_HEADS)
        acs = carve(NT, S_HEADS)
        tot = carve(NT, S_HEADS)
        decay_end = carve(NT, S_HEADS)
        ecs = carve(NT, S_HEADS)
        edec = carve(NT, S_HEADS)
        sp1 = carve(NT, S_HEADS)
        sp2 = carve(NT, S_HEADS)
        acsT = carve(T)
        ssq = carve(NT, S_GROUPS)
        srs = carve(2, NT * S_GROUPS)
        y_lo = rn[:].rearrange("p t d -> p (t d)").rearrange("p (t d) -> p t d", t=2)
        ys = [y_lo[:, 0, :], y_lo[:, 1, :], y_hi[:, 0, :], y_hi[:, 1, :]]
        bc_w = gb[:].rearrange("p a b -> p (a b)").rearrange("p (k n) -> p k n", k=KD)
        yT = [Mh[:].rearrange("p a b -> p (a b)")[:, 0:KS * P].rearrange("p (k l) -> p k l", k=KS),
              Mh[:].rearrange("p a b -> p (a b)")[:, KS * P:2 * KS * P].rearrange("p (k l) -> p k l", k=KS),
              arena[:, 0:2048].rearrange("p (k l) -> p k l", k=KS),
              arena[:, 3584:3584 + 2048].rearrange("p (k l) -> p k l", k=KS)]
        at[0] = 0
        hid = carve(KF, T)
        sg = arena[:, 16384:16384 + 4096].rearrange("p (t d) -> p t d", t=NT)
        at[0] = 0
        oT = carve(H_HEADS, T)
        f_q = carve(2, T)
        f_k = carve(2, T)
        f_b = carve(2, T)
        f_v = carve(2, NT, P)
        f_g = carve(2, NT, P)
        f_t = carve(2, T)
        dif = carve(2, T)
        lev = carve(2, T)
        scT = carve(2, T)
        kend = carve(T)
        ktok = carve(NT, P)
        qe = carve(T)
        elast = carve(NT)
        state = carve(NT - 1, P)
        o_s = carve(NT, P)
        hsq = carve(2, NT)
        junk_h = carve(NT, P)
        at[0] = 0
        q_tok = carve(NT, A_HEADS * QK)
        k_tok = carve(NT, A_HEADS * QK)
        v_tok = carve(NT, A_HEADS * V_HEAD)
        branch = carve(NT, D)
        at_pre = at[0]
        cq_n = carve(NT, Q_LORA)
        ckv_n = carve(NT, KV_LORA)
        cqT = carve(KQ, T)
        ckvT = carve(KKV, T)
        at_post = at[0]
        at[0] = at_pre
        hq = carve(2, NT, QK)
        hk = carve(2, NT, QK)
        qhT = carve(2, T)
        khT = carve(2, T)
        prob = carve(2, T)
        probT = carve(2, T)
        smx = carve(2, 4, NT)
        assert at[0] <= at_post + 2000
        at[0] = max(at[0], at_post)
        qmT = carve(2, T)
        kmT = carve(2, NMEM)
        v_mem = carve(MT, MEM_W)
        krope = carve(NT, ROPE)
        cosn = carve(NT, HR)
        sinn = carve(NT, HR)
        ang = carve(NT, HR)
        turns = carve(NT, HR)
        posf = carve(NT)
        posi = carve(NT)
        rstat = carve(2, NT, 12)
        rt = carve(4, A_HEADS * HR)
        mem_tok = q_tok[:].rearrange("p a b -> p (a b)")[:, 0:MT * D].rearrange("p (a b) -> p a b", a=MT)
        memT = k_tok[:].rearrange("p a b -> p (a b)")[:, 0:KD * NMEM].rearrange("p (a b) -> p a b", a=KD)
        gate = rn

        units_landed = [sem(f"units_landed{s}") for s in range(2)]
        units_begun = sem("units_begun")
        bank_full = [sem(f"bank_full{b}") for b in range(8)]
        bank_free = [sem(f"bank_free{b}") for b in range(8)]
        con_in = sem("con_in")
        x_in = [sem(f"x_in{t}") for t in range(NT)]
        p_in = sem("p_in")
        par_in = sem("par_in")
        gb_in = sem("gb_in")
        var_ready = sem("var_ready")
        root_ready = sem("root_ready")
        norm_ready = sem("norm_ready")
        res_ready = sem("res_ready")
        ssd_small_in = sem("ssd_small_in")
        bc_in = sem("bc_in")
        out_done = sem("out_done")
        named = {}

        def sig(name):
            if name not in named:
                named[name] = sem(name)
            return named[name]

        banks = Banks()
        banks.stage("start", [("par", 0), ("par_b", 1)] + [(("x", t, h), 2 + (2 * t + h) % 4) for t in range(NT) for h in range(2)]
                    + [(("p", i, k), 6 + k) for i in range(DEPTH) for k in range(KP)])
        banks.stage("dt", [("dt", 0), ("acs", 1), ("tot", 2), ("acsT", 3)])
        banks.stage("ssd", [("B", 0), ("C", 1), (("acs", 0), 4), (("acs", 1), 5), (("acs", 2), 6), (("acs", 3), 7),
                            (("x", 0), 2), (("acs", 4), 4), (("acs", 5), 5), (("acs", 6), 6), (("acs", 7), 7),
                            (("x", 1), 3), (("xt", 0), 4), (("x", 2), 0), ("CB", 2), ("BT", 3), (("xt", 1), 5),
                            (("x", 3), 1), (("xt", 2), 6), (("z", 0), 0), (("xt", 3), 7), (("z", 1), 1),
                            (("z", 2), 2), (("z", 3), 3), (("st", 0), 4), (("st", 1), 5), (("st", 2), 6),
                            (("yd", 0), 7), (("yd", 1), 4), (("yo", 1), 7), (("yd", 2), 5), (("yo", 2), 4),
                            (("yd", 3), 6), (("yo", 3), 5)], S_GROUPS)
        banks.stage("yT", [((t, g), 4 + g) for t in range(NT) for g in range(S_GROUPS)])

        def norm_banks(stage):
            banks.stage(stage, [((t, h), 4 + (2 * t + h) % 4) for t in range(NT) for h in range(2)])

        def out_banks(stage):
            banks.stage(stage, [(t, t) for t in range(NT)], NHALF)

        def mlp_banks(i):
            banks.stage(f"up{i}", [((s, m), m) for s in range(2) for m in range(4)], 4)
            out_banks(f"down{i}")
            norm_banks(f"norm{i}1")

        def ple_banks(i):
            banks.stage(f"gate{i}", [((h, t), 4 * h + t) for h in range(NHALF) for t in range(NT)])
            banks.stage(f"proj{i}", [((h, t), 4 * h + t) for t in range(NT) for h in range(NHALF)])

        out_banks("ssd_out")
        norm_banks("norm00")
        mlp_banks(0)
        ple_banks(0)
        norm_banks("turn0")
        banks.stage("hgrn", [(n, b) for n, b in (("q", 0), ("f", 1), ("vg0", 2), ("vg1", 3))]
                    + [(("lev", n), 4 + n % 2) for n in range(LEVELS + 1)]
                    + [("kt", 6), (("st", 0), 7), (("st", 1), 6), (("st", 2), 7), ("o", 6), ("ot", 7)], H_HEADS)
        out_banks("hgrn_out")
        norm_banks("norm10")
        mlp_banks(1)
        ple_banks(1)
        banks.stage("memT", [((m, h), 2 * m + h) for m in range(MT) for h in range(2)])
        banks.stage("memkv", [(("k", c), c) for c in range(2)] + [(("v", m), 2 + m) for m in range(MT)])
        norm_banks("norm_mla")
        banks.stage("cq", [(t, t) for t in range(NT)])
        banks.stage("ckv", [(t, t) for t in range(NT)])
        banks.stage("lora", [(("q", t), 4 + t) for t in range(NT)] + [(("kv", t), 4 + t) for t in range(NT)])
        banks.stage("qm", [(c, c) for c in range(2)])
        banks.stage("mgate", [((h, t), t) for h in range(NHALF) for t in range(NT)])
        banks.stage("uq", [((n, t), t) for n in range(3) for t in range(NT)])
        banks.stage("ukv", [((n, t), 4 + t) for n in range(3) for t in range(NT)])

        def head_banks(name, turn_next):
            return [(name("s", t), t) for t in range(NT)] + ([(name("qt"), 5), (name("kt"), 4)] if turn_next else []) \
                + [(name("pt", t), 6 + t % 2) for t in range(NT)] + [(name("o"), 4)]

        banks.stage("mheads", head_banks(lambda *n: n, False), M_HEADS)
        banks.stage("first_turn", [(("qt",), 5), (("kt",), 4)])
        banks.stage("heads", head_banks(lambda *n: (0,) + n, True) + head_banks(lambda *n: (1,) + n, True), A_HEADS // 2 - 1)
        banks.stage("last_heads", head_banks(lambda *n: (0,) + n, True) + head_banks(lambda *n: (1,) + n, False))
        norm_banks("branchT")
        out_banks("mla_out")

        order = [("ssd", 2 * S_GROUPS), ("ssd_out", 4), ("up0", 8), ("down0", 8), ("ple0", 3), ("hgrn", H_HEADS),
                 ("hgrn_out", 2), ("up1", 8), ("down1", 8), ("ple1", 3), ("mem", 1), ("cq", 1), ("ckv", 1), ("qm", 1),
                 ("mgate", 2), ("uq", 1), ("ukv", 1), ("mla_out", 2)]
        unit0, n_units = {}, 0
        for name, n in order:
            unit0[name] = n_units
            n_units += n

        def slot_of(stage, n=0):
            return slots[(unit0[stage] + n) % 2]

        def as_k(s, cols=HALF):
            return s[:, 0:4096 // cols * cols].rearrange("p (k n) -> p k n", n=cols)

        LAND = 4 * 16

        def landed(pe, stage, n=0, i=0, per=0):
            u = unit0[stage] + n
            pe.wait_ge(units_landed[u % 2], LAND * (u // 2 + 1) + i * (LAND * (per // 2)))

        def wait_taken(eng, stage, name, i=0):
            b, n = banks.at(stage, name, i)
            eng.wait_ge(bank_free[b], n + 1)

        def wait_full(eng, stage, name, i=0):
            b, n = banks.at(stage, name, i)
            eng.wait_ge(bank_full[b], n + 1)
            return b

        def wait_filled_before(eng, stage, name, i=0):
            b, n = banks.at(stage, name, i)
            if not isinstance(n, int) or n > 0:
                eng.wait_ge(bank_full[b], n)

        def by_block(ap, t=NT):
            return ap.rearrange("p (t l) -> p t l", t=t)

        block = ctx.enter_context(nc.Block())

        @block.sync
        def _(sp):
            def slot_free(stage, n=0, i=0, per=0):
                u = unit0[stage] + n
                if u >= 2:
                    sp.wait_ge(units_begun, u + i * per)
                    sp.sem_inc(sig("slot_given"), 1)
                return slots[u % 2], units_landed[u % 2]

            def load(view, w, stage, n=0, i=0, per=0):
                s, done = slot_free(stage, n, i, per)
                nk = view[1]
                dst = s[:, 0:nk * view[2]].rearrange("p (k n) -> p k n", k=nk)
                step = nk // 4
                for c in range(4):
                    sp.dma_start(dst[:, c * step:(c + 1) * step, :], w(c * step, step)).then_inc(done, 16)

            def rows_cols(w2, row0, col0, cols):
                def pick(k, n):
                    return w2[ds(row0 + k * P, n * P) if not isinstance(row0, int) else slice(row0 + k * P, row0 + (k + n) * P),
                              ds(col0, cols) if not isinstance(col0, int) else slice(col0, col0 + cols)
                              ].rearrange("(k p) n -> p k n", p=P)
                return pick

            sp.dma_start(con[:], cst).then_inc(con_in, 16)
            for t in range(NT):
                sp.dma_start(res[:, t, :], x[t * P:(t + 1) * P, :]).then_inc(x_in[t], 16)
            sp.dma_start(s_par[0:A_ROWS, 0, :], par_a).then_inc(par_in, 16)
            sp.dma_start(s_par[0:B_ROWS, 1, :], par_b).then_inc(par_in, 16)
            for i in range(DEPTH):
                sp.dma_start(s_p[:, i * NT:(i + 1) * NT, :], p[i].rearrange("(t p) n -> p t n", p=P)).then_inc(p_in, 16)

            sp.dma_start(wdt, w_dt.rearrange("(k p) n -> p k n", p=P)).then_inc(ssd_small_in, 16)
            for dst, src in ((dbias, dt_bias), (aneg, a_log), (dskip, d_skip)):
                sp.dma_start(dst, src.partition_broadcast(P)).then_inc(ssd_small_in, 16)
            w3 = w_ssd.rearrange("(k p) n -> p k n", p=P)
            def load_group(g, first):
                if not first:
                    sp.wait_ge(units_begun, 2 * g)
                    sp.sem_inc(sig("slot_given"), 1)
                for n, c0 in enumerate((S_B, S_C)):
                    sp.dma_start(bc_w[:, :, n * P:(n + 1) * P], w3[:, :, ds(g * S_N + c0, S_N)]).then_inc(bc_in, 16)
                for c in range(4):
                    sp.dma_start(as_k(slots[0])[:, 2 * c:2 * c + 2, :],
                                 w3[:, 2 * c:2 * c + 2, ds(g * HALF + S_X, HALF)]).then_inc(units_landed[0], 16)
                if not first:
                    sp.wait_ge(units_begun, 2 * g + 1)
                    sp.sem_inc(sig("slot_given"), 1)
                for c in range(4):
                    sp.dma_start(as_k(slots[1])[:, 2 * c:2 * c + 2, :],
                                 w3[:, 2 * c:2 * c + 2, ds(g * HALF + S_Z, HALF)]).then_inc(units_landed[1], 16)

            load_group(0, True)
            with sp.Fori(1, S_GROUPS) as g:
                load_group(g, False)
            with sp.Fori(0, NHALF) as h:
                for n in range(2):
                    load((P, KD, HALF), rows_cols(w_ssd_out, n * D, h * HALF, HALF), "ssd_out", n, h, 2)

            def load_mlp(i):
                with sp.Fori(0, 4) as j:
                    for n in range(2):
                        load((P, KD, HALF), rows_cols(w_mlp1[i], 0, j * (2 * HALF) + n * HALF, HALF), f"up{i}", n, j, 2)
                with sp.Fori(0, NHALF) as h:
                    for n in range(4):
                        load((P, KD, HALF), rows_cols(w_mlp2[i], n * D, h * HALF, HALF), f"down{i}", n, h, 4)

            def load_ple(i):
                for h in range(NHALF):
                    load((P, KD, HALF), rows_cols(w_gate[i], 0, h * HALF, HALF), f"ple{i}", h)
                s, done = slot_free(f"ple{i}", 2)
                dst = s[:, 0:KP * D].rearrange("p (k n) -> p k n", k=KP)
                src = w_proj[i].rearrange("(k p) n -> p k n", p=P)
                for c in range(4):
                    sp.dma_start(dst[:, :, c * 256:(c + 1) * 256], src[:, :, c * 256:(c + 1) * 256]).then_inc(done, 16)

            load_mlp(0)
            load_ple(0)
            wh = w_hgrn.rearrange("(k p) n -> p k n", p=P)
            with sp.Fori(0, H_HEADS // 2) as j:
                for n in range(2):
                    s, done = slot_free("hgrn", n, j, 2)
                    for c in range(4):
                        sp.dma_start(as_k(s)[:, :, c * P:(c + 1) * P],
                                     wh[:, :, ds(j * (2 * P) + (c * D + n * P), P)]).then_inc(done, 16)
            for h in range(NHALF):
                load((P, KD, HALF), rows_cols(w_hgrn_out, 0, h * HALF, HALF), "hgrn_out", h)
            load_mlp(1)
            load_ple(1)
            sp.dma_start(mem_tok, mem.rearrange("(t p) n -> p t n", p=P)).then_inc(sig("mem_in"), 16)
            sp.dma_start(posi[:].bitcast(I32), pos.rearrange("(t p) -> p t", p=P),
                         allow_slow_non_contiguous=True).then_inc(sig("pos_in"), 16)
            load((P, KD, 2 * MEM_W), rows_cols(w_mem, 0, 0, 2 * MEM_W), "mem")
            load((P, KD, Q_LORA), rows_cols(w_mla, 0, 0, Q_LORA), "cq")
            load((P, KD, KV_LORA + ROPE), rows_cols(w_mla, 0, O_KV, KV_LORA + ROPE), "ckv")
            load((P, KD, MEM_W), rows_cols(w_mla, 0, O_QM, MEM_W), "qm")
            for h in range(NHALF):
                load((P, KD, HALF), rows_cols(w_mla, 0, O_GATE + h * HALF, HALF), "mgate", h)
            for name, w, nk, width in (("uq", w_uq, KQ, A_HEADS * QK), ("ukv", w_ukv, KKV, A_HEADS * 2 * NOPE)):
                s, done = slot_free(name)
                dst = s[:, 0:nk * width].rearrange("p (k n) -> p k n", k=nk)
                src = w.rearrange("(k p) n -> p k n", p=P)
                q = width // 4
                for c in range(4):
                    sp.dma_start(dst[:, :, c * q:(c + 1) * q], src[:, :, c * q:(c + 1) * q]).then_inc(done, 16)
            for h in range(NHALF):
                load((P, KD, HALF), rows_cols(w_mla_out, 0, h * HALF, HALF), "mla_out", h)
            for t in range(NT):
                sp.wait_ge(sig("out_ready"), t + 1)
                sp.dma_start(out[t * P:(t + 1) * P, :], res[:, t, :]).then_inc(out_done, 16)
            sp.wait_ge(out_done, 16 * NT)

        @block.tensor
        def _(pe):
            def claim(stage, name, i=0):
                b, n = banks.at(stage, name, i)
                if not isinstance(n, int) or n > 0:
                    pe.wait_ge(bank_free[b], n)
                return b

            def turn(b, cols, src, kp=P, mp=P):
                return pe.transpose(psum[0:mp, b, cols:cols + kp], src, con[0:kp, C_ID:C_ID + kp])

            def turn_rows(stage, src, t, wait_sem, n):
                pe.wait_ge(wait_sem, n)
                for h in range(2):
                    b = claim(stage, (t, h))
                    for c in range(4):
                        m = turn(b, c * P, src[:, t, (4 * h + c) * P:(4 * h + c + 1) * P])
                    m.then_inc(bank_full[b], 1)

            norms = [0]

            def norm_turns(stage, after):
                n = norms[0]
                norms[0] += 1
                for t in range(NT + 1):
                    if t < NT and after is not None:
                        after(t)
                    if t > 0:
                        turn_rows(stage, rn, t - 1, norm_ready, NT * n + t)

            def wait_features(stage, name=lambda t, h: (t, h)):
                for t in range(NT):
                    for h in range(2):
                        wait_taken(pe, stage, name(t, h))

            pe.wait_ge(con_in, 16)
            for t in range(NT):
                pe.wait_ge(x_in[t], 16)
                for h in range(2):
                    b = claim("start", ("x", t, h))
                    for c in range(4):
                        m = turn(b, c * P, res[:, t, (4 * h + c) * P:(4 * h + c + 1) * P])
                    m.then_inc(bank_full[b], 1)
            pe.wait_ge(par_in, 32)
            b = claim("start", "par")
            turn(b, 0, s_par[0:A_ROWS, 0, :], A_ROWS).then_inc(bank_full[b], 1)
            b = claim("start", "par_b")
            turn(b, 0, s_par[0:B_ROWS, 1, :], B_ROWS).then_inc(bank_full[b], 1)
            pe.wait_ge(p_in, 16 * DEPTH)
            for i in range(DEPTH):
                for k in range(KP):
                    b = claim("start", ("p", i, k))
                    for t in range(NT):
                        m = turn(b, t * P, s_p[:, i * NT + t, k * P:(k + 1) * P])
                    m.then_inc(bank_full[b], 1)
            wait_features("start", lambda t, h: ("x", t, h))

            pe.wait_ge(ssd_small_in, 64)
            b = claim("dt", "dt")
            for t in range(NT):
                for k in range(KD):
                    m = pe.matmul(psum[:, b, t * S_HEADS:(t + 1) * S_HEADS], fT[:, k, t * P:(t + 1) * P], wdt[:, k, :],
                                  **first_and_last(k, KD))
            m.then_inc(bank_full[b], 1)
            pe.wait_ge(sig("da_ready"), 1)
            for name, left in (("acs", tri), ("tot", ones)):
                b = claim("dt", name)
                for t in range(NT):
                    m = pe.matmul(psum[:, b, t * S_HEADS:(t + 1) * S_HEADS], left, da[:, t, :], start=True, stop=True)
                m.then_inc(bank_full[b], 1)
            b = claim("dt", "acsT")
            for t in range(NT):
                m = pe.matmul(psum[0:S_HEADS, b, t * P:(t + 1) * P], da[:, t, :], tri, start=True, stop=True)
            m.then_inc(bank_full[b], 1)

            with pe.Fori(0, S_GROUPS) as g:
                wx, wz = as_k(slots[0]), as_k(slots[1])
                pe.wait_ge(bc_in, 32 + g * 32)
                for n, name in enumerate(("B", "C")):
                    b = claim("ssd", name, g)
                    for k in range(KD):
                        m = pe.matmul(psum[:, b, :], bc_w[:, k, n * P:(n + 1) * P], fT[:, k, :], **first_and_last(k, KD))
                    m.then_inc(bank_full[b], 1)

                def spread_sums(j):
                    pe.wait_ge(sig("row_ready"), g * S_HPG + (j + 1))
                    b = claim("ssd", ("acs", j), g)
                    pe.matmul(psum[:, b, :], con[0:S_HEADS, C_ONE:C_ONE + P], rows[0:S_HEADS, j % 2, :],
                              start=True, stop=True).then_inc(bank_full[b], 1)

                def x_block(mm_):
                    b = claim("ssd", ("x", mm_), g)
                    for k in range(KD):
                        m = pe.matmul(psum[:, b, :], wx[:, k, mm_ * P:(mm_ + 1) * P], fT[:, k, :], **first_and_last(k, KD))
                        if mm_ == 0 and k == 0:
                            m.then_inc(units_begun, 1)
                    m.then_inc(bank_full[b], 1)

                def x_turn(mm_):
                    pe.wait_ge(sig("conv_silu"), g * 6 + (3 + mm_))
                    b = claim("ssd", ("xt", mm_), g)
                    for t in range(NT):
                        m = turn(b, t * P, cv[:, (mm_ + 2) % 3, t * P:(t + 1) * P])
                    m.then_inc(bank_full[b], 1)

                def z_tile(t):
                    b = claim("ssd", ("z", t), g)
                    for k in range(KD):
                        m = pe.matmul(psum[:, b, :], fT[:, k, t * P:(t + 1) * P], wz[:, k, :], **first_and_last(k, KD))
                        if t == 0 and k == 0:
                            m.then_inc(units_begun, 1)
                    m.then_inc(bank_full[b], 1)

                for j in range(4):
                    spread_sums(j)
                pe.wait_ge(units_landed[0], LAND + g * LAND)
                x_block(0)
                for j in range(4, S_HPG):
                    spread_sums(j)
                x_block(1)
                x_turn(0)
                x_block(2)
                b = claim("ssd", "CB", g)
                for t in range(NT):
                    m = pe.matmul(psum[:, b, t * P:(t + 1) * P], BT[:, t * P:(t + 1) * P], CT[:, t * P:(t + 1) * P],
                                  start=True, stop=True)
                m.then_inc(bank_full[b], 1)
                b = claim("ssd", "BT", g)
                for t in range(NT):
                    m = turn(b, t * P, BT[:, t * P:(t + 1) * P])
                m.then_inc(bank_full[b], 1)
                x_turn(1)
                x_block(3)
                x_turn(2)
                pe.wait_ge(units_landed[1], LAND + g * LAND)
                z_tile(0)
                x_turn(3)
                for t in range(1, NT):
                    z_tile(t)
                wait_taken(pe, "ssd", "BT", g)
                for c in range(NT - 1):
                    if c == 0:
                        pe.wait_ge(sig("xw_ready"), g * 4 + 4)
                    b = claim("ssd", ("st", c), g)
                    pe.matmul(psum[:, b, :], Btok[:, c, :], xw[:, c, :], start=True, stop=True).then_inc(bank_full[b], 1)

                def y_in(c):
                    b = claim("ssd", ("yd", c), g)
                    for j in range(S_HPG):
                        m = pe.matmul(psum[:, b, j * S_P:(j + 1) * S_P], Mh[:, j, c * P:(c + 1) * P],
                                      xdt[:, c, j * S_P:(j + 1) * S_P], start=True, stop=True)
                    m.then_inc(bank_full[b], 1)

                def y_before(c):
                    wait_taken(pe, "ssd", ("st", c - 1), g)
                    b = claim("ssd", ("yo", c), g)
                    pe.matmul(psum[:, b, :], CT[:, c * P:(c + 1) * P], prev[:, c - 1, :],
                              start=True, stop=True).then_inc(bank_full[b], 1)

                pe.wait_ge(sig("M_ready"), g * S_HPG + S_HPG)
                pe.wait_ge(sig("xdt_ready"), g * 4 + 4)
                y_in(0)
                for c in range(1, NT):
                    y_in(c)
                    y_before(c)

            for t in range(NT):
                pe.wait_ge(sig("y_normed"), t + 1)
                for g in range(S_GROUPS):
                    b = claim("yT", (t, g))
                    for c in range(4):
                        m = turn(b, c * P, ys[t][:, (4 * g + c) * P:(4 * g + c + 1) * P])
                    m.then_inc(bank_full[b], 1)
            for t in range(NT):
                for g in range(S_GROUPS):
                    wait_taken(pe, "yT", (t, g))

            def times_out(stage, left, n_units_, h, static=False):
                for n in range(n_units_):
                    last = n == n_units_ - 1
                    landed(pe, stage, h * n_units_ + n)
                    w = as_k(slot_of(stage, h * n_units_ + n))

                    def tile(t, n=n, last=last, w=w):
                        b = t if n else claim(stage, t, h)
                        for k in range(KD):
                            m = pe.matmul(psum[:, b, :], left(n * KD + k, t), w[:, k, :],
                                          start=(n == 0 and k == 0), stop=(last and k == KD - 1))
                            if t == 0 and k == 0:
                                m.then_inc(units_begun, 1)
                        if last:
                            m.then_inc(bank_full[b], 1)
                    if last:
                        return tile
                    for t in range(NT):
                        tile(t)

            def out_and_norm(stage, norm, left, n_units_):
                tile = times_out(stage, left, n_units_, 0)
                for t in range(NT):
                    tile(t)
                norm_turns(norm, times_out(stage, left, n_units_, 1))

            out_and_norm("ssd_out", "norm00", lambda k, t: yT[t][:, k, :], 2)

            def mlp(i):
                wait_features(f"norm{i}0")
                with pe.Fori(0, 4) as j:
                    for n in range(2):
                        landed(pe, f"up{i}", n, j, 2)
                        w = as_k(slot_of(f"up{i}", n))
                        for c in range(4):
                            b = claim(f"up{i}", (n, c), j)
                            for k in range(KD):
                                m = pe.matmul(psum[:, b, :], w[:, k, c * P:(c + 1) * P], fT[:, k, :], **first_and_last(k, KD))
                                if c == 0 and k == 0:
                                    m.then_inc(units_begun, 1)
                            m.then_inc(bank_full[b], 1)
                pe.wait_ge(sig("hidden"), 32 * (i + 1))
                out_and_norm(f"down{i}", f"norm{i}1", lambda k, t: hid[:, k, t * P:(t + 1) * P], 4)

            def ple(i):
                wait_features(f"norm{i}1")
                for h in range(NHALF):
                    landed(pe, f"ple{i}", h)
                    w = as_k(slot_of(f"ple{i}", h))
                    for t in range(NT):
                        b = claim(f"gate{i}", (h, t))
                        for k in range(KD):
                            m = pe.matmul(psum[:, b, :], fT[:, k, t * P:(t + 1) * P], w[:, k, :], **first_and_last(k, KD))
                            if t == 0 and k == 0:
                                m.then_inc(units_begun, 1)
                        m.then_inc(bank_full[b], 1)
                landed(pe, f"ple{i}", 2)
                w = slot_of(f"ple{i}", 2)[:, 0:KP * D].rearrange("p (k n) -> p k n", k=KP)
                for t in range(NT):
                    for h in range(NHALF):
                        b = claim(f"proj{i}", (h, t))
                        for k in range(KP):
                            m = pe.matmul(psum[:, b, :], pT[:, i, k, t * P:(t + 1) * P], w[:, k, h * HALF:(h + 1) * HALF],
                                          **first_and_last(k, KP))
                            if t == 0 and h == 0 and k == 0:
                                m.then_inc(units_begun, 1)
                        m.then_inc(bank_full[b], 1)

            mlp(0)
            ple(0)
            for t in range(NT):
                turn_rows("turn0", res, t, sig("ple_done0"), t + 1)
            wait_features("turn0")

            def hgrn_project(par, i, n):
                w = as_k(slot_of("hgrn", par))
                if n == 0:
                    landed(pe, "hgrn", par, i, 2)
                if n < 2:
                    b = claim("hgrn", "qf"[n], 2 * i + par)
                    for k in range(KD):
                        m = pe.matmul(psum[:, b, :], w[:, k, n * P:(n + 1) * P], fT[:, k, :], **first_and_last(k, KD))
                        if n == 0 and k == 0:
                            m.then_inc(units_begun, 1)
                    m.then_inc(bank_full[b], 1)
                else:
                    b = claim("hgrn", f"vg{n - 2}", 2 * i + par)
                    for tt in range(2):
                        t = 2 * (n - 2) + tt
                        for k in range(KD):
                            m = pe.matmul(psum[:, b, tt * 256:(tt + 1) * 256], fT[:, k, t * P:(t + 1) * P],
                                          w[:, k, 2 * P:4 * P], **first_and_last(k, KD))
                    m.then_inc(bank_full[b], 1)

            def hgrn_level(par, i, n):
                h = 2 * i + par
                if n < LEVELS:
                    pe.wait_ge(sig("level_ready"), h * LEVELS + (n + 1))
                else:
                    pe.wait_ge(sig("k_ready"), h + 1)
                b = claim("hgrn", ("lev", n), h)
                for c in range(NT):
                    if n < LEVELS:
                        a = lev[:, n % 2, c * P:(c + 1) * P]
                        m = pe.matmul(psum[:, b, c * P:(c + 1) * P], a, a, start=True, stop=True)
                    else:
                        m = pe.matmul(psum[:, b, c * P:(c + 1) * P], f_k[:, par, c * P:(c + 1) * P],
                                      f_q[:, par, c * P:(c + 1) * P], start=True, stop=True)
                m.then_inc(bank_full[b], 1)

            def hgrn_turn(h):
                wait_taken(pe, "hgrn", "o", h)
                b = claim("hgrn", "ot", h)
                for c in range(NT):
                    m = turn(b, c * P, o_s[:, c, :])
                m.then_inc(bank_full[b], 1)

            def hgrn_core(par, i, fill, before=None):
                h = 2 * i + par
                for n in range(LEVELS + 1):
                    hgrn_level(par, i, n)
                    if n == 1 and before is not None:
                        hgrn_turn(before)
                    if n % 2 == 1 and fill:
                        fill(n // 2)
                    if n == 3:
                        pe.wait_ge(sig("kend_ready"), h + 1)
                        b = claim("hgrn", "kt", h)
                        for c in range(NT):
                            m = turn(b, c * P, kend[:, c * P:(c + 1) * P])
                        m.then_inc(bank_full[b], 1)
                    if n == 5:
                        wait_taken(pe, "hgrn", "kt", h)
                        for c in range(NT - 1):
                            b = claim("hgrn", ("st", c), h)
                            pe.matmul(psum[:, b, 0:P], ktok[:, c, :], f_v[:, par, c, :],
                                      start=True, stop=True).then_inc(bank_full[b], 1)
                wait_taken(pe, "hgrn", ("lev", LEVELS), h)
                wait_taken(pe, "hgrn", ("st", NT - 2), h)
                wait_taken(pe, "hgrn", "vg1", h)
                b = claim("hgrn", "o", h)
                for c in range(NT):
                    m = pe.matmul(psum[:, b, c * P:(c + 1) * P], scT[:, par, c * P:(c + 1) * P], f_v[:, par, c, :],
                                  start=True, stop=(c == 0))
                    if c:
                        m = pe.matmul(psum[:, b, c * P:(c + 1) * P], qe[:, c * P:(c + 1) * P], state[:, c - 1, :],
                                      start=False, stop=True)
                m.then_inc(bank_full[b], 1)

            for n in range(4):
                hgrn_project(0, 0, n)
            hgrn_core(0, 0, lambda n: hgrn_project(1, 0, n))
            with pe.Fori(0, H_HEADS // 2 - 1) as i:
                hgrn_core(1, i, lambda n: hgrn_project(0, i + 1, n), 2 * i)
                hgrn_core(0, i + 1, lambda n: hgrn_project(1, i + 1, n), 2 * i + 1)
            hgrn_core(1, H_HEADS // 2 - 1, None, H_HEADS - 2)
            hgrn_turn(H_HEADS - 1)
            wait_taken(pe, "hgrn", "ot", H_HEADS - 1)
            out_and_norm("hgrn_out", "norm10", lambda k, t: oT[:, k, t * P:(t + 1) * P], 1)
            mlp(1)
            ple(1)

            for m_ in range(MT):
                pe.wait_ge(sig("mem_normed"), m_ + 1)
                for h in range(2):
                    b = claim("memT", (m_, h))
                    for c in range(4):
                        m = turn(b, c * P, mem_tok[:, m_, (4 * h + c) * P:(4 * h + c + 1) * P])
                    m.then_inc(bank_full[b], 1)
            for m_ in range(MT):
                for h in range(2):
                    wait_taken(pe, "memT", (m_, h))
            landed(pe, "mem")
            w = as_k(slot_of("mem"))
            for c in range(2):
                b = claim("memkv", ("k", c))
                for k in range(KD):
                    m = pe.matmul(psum[:, b, 0:NMEM], w[:, k, c * P:(c + 1) * P], memT[:, k, :], **first_and_last(k, KD))
                    if c == 0 and k == 0:
                        m.then_inc(units_begun, 1)
                m.then_inc(bank_full[b], 1)
            for m_ in range(MT):
                b = claim("memkv", ("v", m_))
                for k in range(KD):
                    m = pe.matmul(psum[:, b, 0:MEM_W], memT[:, k, m_ * P:(m_ + 1) * P], w[:, k, MEM_W:2 * MEM_W],
                                  **first_and_last(k, KD))
                m.then_inc(bank_full[b], 1)
            norm_turns("norm_mla", None)
            wait_features("norm_mla")

            def by_tokens(stage, unit, cols, n=0, name=lambda t: t):
                landed(pe, unit, n)
                w = slot_of(unit, n)[:, 0:KD * cols].rearrange("p (k n) -> p k n", k=KD)
                for t in range(NT):
                    b = claim(stage, name(t))
                    for k in range(KD):
                        m = pe.matmul(psum[:, b, 0:cols], fT[:, k, t * P:(t + 1) * P], w[:, k, :], **first_and_last(k, KD))
                        if t == 0 and k == 0:
                            m.then_inc(units_begun, 1)
                    m.then_inc(bank_full[b], 1)

            by_tokens("cq", "cq", Q_LORA)
            by_tokens("ckv", "ckv", KV_LORA + ROPE)
            landed(pe, "qm")
            w = slot_of("qm")[:, 0:KD * MEM_W].rearrange("p (k n) -> p k n", k=KD)
            for c in range(2):
                b = claim("qm", c)
                for k in range(KD):
                    m = pe.matmul(psum[:, b, :], w[:, k, c * P:(c + 1) * P], fT[:, k, :], **first_and_last(k, KD))
                    if c == 0 and k == 0:
                        m.then_inc(units_begun, 1)
                m.then_inc(bank_full[b], 1)
            for h in range(NHALF):
                by_tokens("mgate", "mgate", HALF, h, lambda t: (h, t))
            for name, src, nk in (("q", cq_n, KQ), ("kv", ckv_n, KKV)):
                for t in range(NT):
                    wait_taken(pe, f"c{name}", t)
                    b = claim("lora", (name, t))
                    for c in range(nk):
                        m = turn(b, c * P, src[:, t, c * P:(c + 1) * P])
                    m.then_inc(bank_full[b], 1)
            for stage, left, nk, cols in (("uq", cqT, KQ, Q_LORA), ("ukv", ckvT, KKV, HALF)):
                for t in range(NT):
                    wait_taken(pe, "lora", (stage[1:], t))
                landed(pe, stage)
                w = slot_of(stage)[:, 0:nk * 3 * cols].rearrange("p (k n) -> p k n", k=nk)
                for n in range(3):
                    for t in range(NT):
                        b = claim(stage, (n, t))
                        for k in range(nk):
                            m = pe.matmul(psum[:, b, 0:cols], left[:, k, t * P:(t + 1) * P],
                                          w[:, k, n * cols:(n + 1) * cols], **first_and_last(k, nk))
                            if n == 0 and t == 0 and k == 0:
                                m.then_inc(units_begun, 1)
                        m.then_inc(bank_full[b], 1)

            def scores(stage, name, i, q, k, width):
                for t in range(NT):
                    b = claim(stage, name("s", t), i)
                    pe.matmul(psum[:, b, 0:width], q[:, t * P:(t + 1) * P], k, start=True, stop=True)\
                        .then_inc(bank_full[b], 1)

            def weigh(stage, name, i, nk, values):
                for t in range(NT + 1):
                    if t < NT:
                        wait_taken(pe, stage, name("s", t), i)
                        b = claim(stage, name("pt", t), i)
                        for c in range(nk):
                            m = turn(b, c * P, prob[:, t % 2, c * P:(c + 1) * P])
                        m.then_inc(bank_full[b], 1)
                    if t > 0:
                        wait_taken(pe, stage, name("pt", t - 1), i)
                        b = claim(stage, name("o"), i) if t == 1 else banks.at(stage, name("o"))[0]
                        for c in range(nk):
                            m = pe.matmul(psum[:, b, (t - 1) * V_HEAD:t * V_HEAD], probT[:, (t - 1) % 2, c * P:(c + 1) * P],
                                          values(c), **first_and_last(c, nk))
                        m.then_inc(sig("tile_weighed") if t < NT else bank_full[b], 1)

            for c in range(2):
                wait_taken(pe, "memkv", ("k", c))
                wait_taken(pe, "memkv", ("v", c))
                wait_taken(pe, "qm", c)
            for h in range(M_HEADS):
                r0 = M_HEAD * (h % 2)
                scores("mheads", lambda *n: n, h, qmT[r0:r0 + M_HEAD, h // 2, :], kmT[r0:r0 + M_HEAD, h // 2, :], NMEM)
                weigh("mheads", lambda *n: n, h, MT, lambda c: v_mem[:, c, h * M_HEAD:(h + 1) * M_HEAD])

            def turn_head(stage, name, i, par, nth):
                pe.wait_ge(sig("head_rows"), nth + 1)
                for src, n in ((hq, "qt"), (hk, "kt")):
                    b = claim(stage, name(n), i)
                    for t in range(NT):
                        m = turn(b, t * P, src[:, par, t, :], P, QK)
                    m.then_inc(bank_full[b], 1)

            def head(stage, par, i, nth, turned_by, nxt=True):
                for n in ("qt", "kt"):
                    wait_taken(pe, turned_by[0], turned_by[1] + (n,), turned_by[2])
                scores(stage, lambda *n: (par,) + n, i, qhT[0:QK, par, :], khT[0:QK, par, :], T)
                if nxt:
                    turn_head(stage, lambda n: (par, n), i, 1 - par, nth + 1)
                weigh(stage, lambda *n: (par,) + n, i, NT, lambda c: v_tok[:, c, ds(nth * V_HEAD, V_HEAD)]
                      if not isinstance(nth, int) else v_tok[:, c, nth * V_HEAD:(nth + 1) * V_HEAD])

            turn_head("first_turn", lambda n: (n,), 0, 0, 0)
            for n in ("qt", "kt"):
                wait_taken(pe, "first_turn", (n,))
            with pe.Fori(0, A_HEADS // 2 - 1) as i:
                scores("heads", lambda *n: (0,) + n, i, qhT[0:QK, 0, :], khT[0:QK, 0, :], T)
                turn_head("heads", lambda n: (0, n), i, 1, 2 * i + 1)
                weigh("heads", lambda *n: (0,) + n, i, NT, lambda c: v_tok[:, c, ds(i * (2 * V_HEAD), V_HEAD)])
                head("heads", 1, i, 2 * i + 1, ("heads", (0,), i))
                for n in ("qt", "kt"):
                    wait_taken(pe, "heads", (1, n), i)
            head("last_heads", 0, 0, A_HEADS - 2, ("heads", (1,), A_HEADS // 2 - 2))
            head("last_heads", 1, 0, A_HEADS - 1, ("last_heads", (0,), 0), False)
            for t in range(NT):
                turn_rows("branchT", branch, t, sig("branch_gated"), M_HEADS + A_HEADS)
            wait_features("branchT")
            for h in range(NHALF):
                tile = times_out("mla_out", lambda k, t: fT[:, k, t * P:(t + 1) * P], 1, h)
                for t in range(NT):
                    tile(t)

        @block.scalar
        def _(act):
            def full(stage, name, i=0):
                return wait_full(act, stage, name, i)

            def turned_out(stage, t, gain=None, bias=None, name=lambda t, h: (t, h)):
                b = full(stage, name(t, 0))
                if gain is None:
                    act.copy(fT[:, 0:4, t * P:(t + 1) * P], by_block(psum[:, b, :])).then_inc(bank_free[b], 1)
                    return
                for c in range(4):
                    src, dst, g = psum[:, b, c * P:(c + 1) * P], fT[:, c, t * P:(t + 1) * P], col_b[:, gain + c:gain + c + 1]
                    if bias is None:
                        m = act.mul(dst, src, g)
                    else:
                        m = act.activation(dst, src, ACT.Identity, scale=g, bias=col_b[:, bias + c:bias + c + 1])
                m.then_inc(bank_free[b], 1)

            for t in range(NT):
                turned_out("start", t, name=lambda t, h: ("x", t, h))
            wait_taken(act, "start", "par")
            wait_taken(act, "start", "par_b")

            wait_taken(act, "dt", "dt")
            act.activation(sp2, sp1, ACT.Abs)
            act.drain()
            act.activation(sp2, sp2, ACT.Exp, scale=-1.0)
            act.drain()
            act.activation(sp2, sp2, ACT.Ln, bias=1.0)
            act.wait_ge(ssd_small_in, 64)
            act.activation(aneg, aneg, ACT.Exp).then_inc(sig("softplus_ln"), 1)
            act.wait_ge(sig("sums_ready"), 1)
            act.activation(decay_end, decay_end, ACT.Exp)
            act.activation(ecs, acs, ACT.Exp)
            act.activation(edec, tot, ACT.Exp).then_inc(sig("decays"), 1)

            with act.Fori(0, S_GROUPS) as g:
                def row(j):
                    if j >= 2:
                        full("ssd", ("acs", j - 2), g)
                    act.mul(rows[0:S_HEADS, j % 2, :], acsT[0:S_HEADS, :], con[0:S_HEADS, ds(g * S_HPG + (C_ID + j), 1)])\
                        .then_inc(sig("row_ready"), 1)

                def conv_start(n, name, blk):
                    act.drain()
                    b = full("ssd", name, g)
                    act.activation(cv[:, n % 3, :], psum[:, b, :], ACT.Identity, scale=col_a[:, ds(blk + (A_CW + 3 * CONV_BLOCKS), 1)],
                                   bias=col_a[:, ds(blk + A_CB, 1)]).then_inc(sig("conv_begun"), 1)

                def silu(n, name, dst):
                    wait_taken(act, "ssd", name, g)
                    act.activation(dst, cv[:, n % 3, :], ACT.Silu).then_inc(sig("conv_silu"), 1)

                def exp_diff(j):
                    act.wait_ge(sig("diff_ready"), g * S_HPG + (j + 1))
                    act.activation(Mh[:, j, :], Mh[:, j, :], ACT.Exp).then_inc(sig("exp_ready"), 1)

                def x_out(m):
                    b = full("ssd", ("xt", m), g)
                    act.copy(xr[:, :, m * P:(m + 1) * P], by_block(psum[:, b, :])).then_inc(bank_free[b], 1)

                row(0)
                row(1)
                conv_start(0, "B", g + 16)
                conv_start(1, "C", g + 20)
                row(2)
                row(3)
                silu(0, "B", BT)
                silu(1, "C", CT)
                row(4)
                row(5)
                conv_start(2, ("x", 0), 4 * g)
                row(6)
                row(7)
                silu(2, ("x", 0), cv[:, 2, :])
                for j in range(4):
                    exp_diff(j)
                conv_start(3, ("x", 1), 4 * g + 1)
                for j in range(4, S_HPG):
                    exp_diff(j)
                silu(3, ("x", 1), cv[:, 0, :])
                x_out(0)
                conv_start(4, ("x", 2), 4 * g + 2)
                silu(4, ("x", 2), cv[:, 1, :])
                b = full("ssd", "BT", g)
                act.copy(Btok, by_block(psum[:, b, :])).then_inc(bank_free[b], 1)
                x_out(1)
                conv_start(5, ("x", 3), 4 * g + 3)
                silu(5, ("x", 3), cv[:, 2, :])
                x_out(2)
                b = full("ssd", ("z", 0), g)
                act.activation(zs[:, 0, :], psum[:, b, :], ACT.Silu).then_inc(bank_free[b], 1)
                x_out(3)
                for t in range(1, NT):
                    b = full("ssd", ("z", t), g)
                    act.activation(zs[:, t, :], psum[:, b, :], ACT.Silu).then_inc(bank_free[b], 1)
                for c in range(NT):
                    act.wait_ge(sig("y_gated"), g * NT + (c + 1))
                    act.activation(zs[:, c, :], ys[c][:, ds(g * HALF, HALF)], ACT.Square,
                                   accum_out=ssq[:, c, ds(g, 1)]).then_inc(sig("ssq_ready"), 1)
            act.wait_ge(sig("sms_ready"), 1)
            act.activation(srs[:, 1, :], srs[:, 0, :], ACT.Sqrt).then_inc(sig("srs_ready"), 1)
            for t in range(NT):
                for g in (0, 2):
                    b = full("yT", (t, g))
                    for c in range(4):
                        k = 4 * g + c
                        m = act.mul(yT[t][:, k, :], psum[:, b, c * P:(c + 1) * P], col_b[:, B_SN + k:B_SN + k + 1])
                    m.then_inc(bank_free[b], 1)

            norms = [0]

            def norm(stage=None, gain=None, bias=None):
                n = norms[0]
                norms[0] += 1
                for t in range(NT + 1):
                    if t < NT:
                        act.wait_ge(var_ready, NT * n + t + 1)
                        act.activation(ms[:, t, 1:2], ms[:, t, 0:1], ACT.Sqrt).then_inc(root_ready, 1)
                    if t > 0 and stage:
                        turned_out(stage, t - 1, gain, bias)

            def mlp(i):
                with act.Fori(0, 4) as j:
                    for n in range(2):
                        for c in range(4):
                            b = full(f"up{i}", (n, c), j)
                            act.activation(hid[:, ds(j * 8 + (n * 4 + c), 1), :].rearrange("p a l -> p (a l)"), psum[:, b, :],
                                           ACT.Relu).then_inc(bank_free[b], 1)
                norm(f"norm{i}1", B_G + 16 * i + 8, B_B + 16 * i + 8)

            def ple(i):
                for h in range(NHALF):
                    for t in range(NT):
                        b = full(f"gate{i}", (h, t))
                        act.activation(sg[:, t, h * HALF:(h + 1) * HALF], psum[:, b, :], ACT.Sigmoid).then_inc(bank_free[b], 1)

            norm("norm00", B_G, B_B)
            mlp(0)
            ple(0)
            for t in range(NT):
                turned_out("turn0", t)

            def gates(par, h):
                b = full("hgrn", "q", h)
                act.copy(f_q[:, par, :], psum[:, b, :]).then_inc(bank_free[b], 1)
                act.drain()
                b = full("hgrn", "f", h)
                act.activation(f_t[:, 0, :], psum[:, b, :], ACT.Abs)
                act.drain()
                act.activation(f_t[:, 0, :], f_t[:, 0, :], ACT.Exp, scale=-1.0)
                act.drain()
                act.activation(f_t[:, 1, :], f_t[:, 0, :], ACT.Ln, bias=1.0).then_inc(sig("ln_ready"), 1)
                wait_taken(act, "hgrn", "f", h)
                act.activation(f_k[:, par, :], f_t[:, 0, :], ACT.Exp).then_inc(sig("k_ready"), 1)

            def values(par, h):
                for n in range(2):
                    b = full("hgrn", f"vg{n}", h)
                    v = psum[:, b, :].rearrange("p (t s l) -> p t s l", t=2, s=2)
                    act.copy(f_v[:, par, 2 * n:2 * n + 2, :], v[:, :, 0, :])
                    act.activation(f_g[:, par, 2 * n:2 * n + 2, :], v[:, :, 1, :], ACT.Silu).then_inc(bank_free[b], 1)

            def exps(par, h):
                act.wait_ge(sig("b_ready"), h + 1)
                b3 = by_block(f_b[:, par, :])
                act.activation(qe, f_b[:, par, :], ACT.Exp)
                for c in range(NT):
                    act.activation(kend[:, c * P:(c + 1) * P], b3[:, c, :], ACT.Exp, scale=-1.0, bias=b3[:, c, P - 1:P])
                act.activation(elast, b3[:, :, P - 1:P].rearrange("p c l -> p (c l)"), ACT.Exp).then_inc(sig("ends_ready"), 1)
                for n in range(LEVELS):
                    act.wait_ge(sig("dif_ready"), h * LEVELS + (n + 1))
                    v = dif[:, n % 2, :].rearrange("p (a s l) -> p a s l", s=2, l=64 >> n)
                    act.activation(v[:, :, 0, :], v[:, :, 0, :], ACT.Exp, scale=-1.0)
                    act.activation(v[:, :, 1, :], v[:, :, 1, :], ACT.Exp).then_inc(sig("dexp_ready"), 1)

            def out_turned(h):
                b = full("hgrn", "ot", h)
                act.mul(oT[:, ds(h, 1), :].rearrange("p a l -> p (a l)") if not isinstance(h, int) else oT[:, h, :],
                        psum[:, b, :], col_b[:, B_HG:B_HG + 1]).then_inc(bank_free[b], 1)

            def out_root(h):
                b = full("hgrn", "o", h)
                for c in range(NT):
                    act.activation(junk_h[:, c, :], psum[:, b, c * P:(c + 1) * P], ACT.Square, accum_out=hsq[:, 0, c:c + 1])
                act.drain()
                act.activation(hsq[:, 1, :], hsq[:, 0, :], ACT.Sqrt, scale=1.0 / P, bias=eps_h[:, 0:1]).then_inc(sig("oroot_ready"), 1)

            def hgrn_head(par, h, last=False, first=False):
                values(par, h)
                exps(par, h)
                if not first:
                    out_turned(h - 1)
                if not last:
                    gates(1 - par, h + 1)
                out_root(h)

            act.wait_ge(sig("eps_set"), 1)
            gates(0, 0)
            hgrn_head(0, 0, first=True)
            with act.Fori(0, H_HEADS // 2 - 1) as i:
                hgrn_head(1, 2 * i + 1)
                hgrn_head(0, 2 * i + 2)
            hgrn_head(1, H_HEADS - 1, last=True)
            out_turned(H_HEADS - 1)
            norm("norm10", B_G + 16, B_B + 16)
            mlp(1)
            ple(1)

            act.wait_ge(sig("angles_ready"), 1)
            act.activation(sinn, sinn, ACT.Sin)
            act.activation(cosn, cosn, ACT.Sin).then_inc(sig("trig_ready"), 1)
            for m_ in range(MT):
                act.wait_ge(sig("mem_ms"), m_ + 1)
                act.activation(ms[:, m_, 1:2], ms[:, m_, 0:1], ACT.Sqrt).then_inc(sig("mem_root"), 1)
            for m_ in range(MT):
                b = full("memT", (m_, 0))
                for c in range(4):
                    m = act.mul(memT[:, c, m_ * P:(m_ + 1) * P], psum[:, b, c * P:(c + 1) * P], col_b[:, B_MG + c:B_MG + c + 1])
                m.then_inc(bank_free[b], 1)
            for c in range(2):
                b = full("memkv", ("k", c))
                act.copy(kmT[:, c, :], psum[:, b, 0:NMEM]).then_inc(bank_free[b], 1)
            for m_ in range(MT):
                b = full("memkv", ("v", m_))
                act.copy(v_mem[:, m_, :], psum[:, b, 0:MEM_W]).then_inc(bank_free[b], 1)
            norm("norm_mla", B_NG)
            for name, s in (("cq", 0), ("ckv", 1)):
                for t in range(NT):
                    act.wait_ge(sig(f"{name}_ms"), t + 1)
                    act.activation(rstat[:, s, t, 9:10], rstat[:, s, t, 8:9], ACT.Sqrt).then_inc(sig(f"{name}_root"), 1)
            for c in range(2):
                b = full("qm", c)
                act.copy(qmT[:, c, :], psum[:, b, :]).then_inc(bank_free[b], 1)
            for h in range(NHALF):
                for t in range(NT):
                    b = full("mgate", (h, t))
                    act.activation(gate[:, t, h * HALF:(h + 1) * HALF], psum[:, b, :], ACT.Silu).then_inc(bank_free[b], 1)
            for t in range(NT):
                b = full("lora", ("kv", t))
                for c in range(KKV):
                    m = act.mul(ckvT[:, c, t * P:(t + 1) * P], psum[:, b, c * P:(c + 1) * P], col_b[:, B_KG + c:B_KG + c + 1])
                m.then_inc(bank_free[b], 1)
            for n in range(3):
                for t in range(NT):
                    b = full("uq", (n, t))
                    act.copy(q_tok[:, t, n * Q_LORA:(n + 1) * Q_LORA], psum[:, b, 0:Q_LORA]).then_inc(bank_free[b], 1)

            def softmax(stage, name, i, nth, width, scale, par, turned):
                def exp(t):
                    act.wait_ge(sig("max_ready"), nth * NT + (t + 1))
                    wait_filled_before(act, stage, name("pt", t), i)
                    b = banks.at(stage, name("s", t))[0]
                    act.activation(prob[:, t % 2, 0:width], psum[:, b, 0:width], ACT.Exp, scale=scale,
                                   bias=smx[:, par, 1, t:t + 1], accum_out=smx[:, par, 2, t:t + 1])\
                        .then_inc(bank_free[b], 1)

                def prob_turned(t):
                    b = full(stage, name("pt", t), i)
                    if t == 1:
                        wait_filled_before(act, stage, name("o"), i)
                    else:
                        act.wait_ge(sig("tile_weighed"), nth * (NT - 1) + (t - 1))
                    act.copy(probT[:, t % 2, 0:width], psum[:, b, 0:width]).then_inc(bank_free[b], 1)

                exp(0)
                if turned:
                    b = full(stage, name("kt"), i)
                    act.copy(khT[0:QK, 1 - par, :], psum[0:QK, b, :]).then_inc(bank_free[b], 1)
                exp(1)
                exp(2)
                prob_turned(1)
                exp(3)
                prob_turned(3)

            for h in range(M_HEADS):
                softmax("mheads", lambda *n: n, h, h, NMEM, M_SCALE, h % 2, False)
            b = full("first_turn", ("kt",))
            act.copy(khT[0:QK, 0, :], psum[0:QK, b, :]).then_inc(bank_free[b], 1)
            with act.Fori(0, A_HEADS // 2 - 1) as i:
                for par in range(2):
                    softmax("heads", lambda *n, par=par: (par,) + n, i, 2 * i + (par + M_HEADS), T, A_SCALE, par, True)
            for par in range(2):
                softmax("last_heads", lambda *n, par=par: (par,) + n, 0, M_HEADS + A_HEADS - 2 + par, T, A_SCALE, par, par == 0)
            for t in range(NT):
                turned_out("branchT", t)
            norm()

        @block.vector
        def _(dve):
            def full(stage, name, i=0):
                return wait_full(dve, stage, name, i)

            def turned_out(stage, t, gain=None, bias=None, name=lambda t, h: (t, h)):
                b = full(stage, name(t, 1))
                if gain is None:
                    dve.tensor_copy(fT[:, 4:8, t * P:(t + 1) * P], by_block(psum[:, b, :])).then_inc(bank_free[b], 1)
                    return
                for c in range(4, 8):
                    src, dst = psum[:, b, (c - 4) * P:(c - 3) * P], fT[:, c, t * P:(t + 1) * P]
                    m = dve.tensor_scalar(dst, src, col_b[:, gain + c:gain + c + 1],
                                          0.0 if bias is None else col_b[:, bias + c:bias + c + 1], ALU.mult, ALU.add)
                m.then_inc(bank_free[b], 1)

            dve.memset(eps_h[:], RMS_EPS).then_inc(sig("eps_set"), 1)
            for t in range(NT):
                turned_out("start", t, name=lambda t, h: ("x", t, h))
            b = full("start", "par")
            dve.tensor_copy(col_a[:], psum[:, b, 0:A_ROWS]).then_inc(bank_free[b], 1)
            b = full("start", "par_b")
            dve.tensor_copy(col_b[:], psum[:, b, 0:B_ROWS]).then_inc(bank_free[b], 1)
            for i in range(DEPTH):
                for k in range(KP):
                    b = full("start", ("p", i, k))
                    dve.tensor_copy(pT[:, i, k, :], psum[:, b, :]).then_inc(bank_free[b], 1)

            def heads_on_all(v):
                return v.unsqueeze(1).broadcast_to([P, NT, S_HEADS])

            def chunk_heads(b):
                return psum[:, b, 0:NT * S_HEADS].rearrange("p (t h) -> p t h", t=NT)

            dve.wait_ge(ssd_small_in, 64)
            b = full("dt", "dt")
            dve.tensor_tensor(sp1, chunk_heads(b), heads_on_all(dbias), ALU.add).then_inc(bank_free[b], 1)
            dve.wait_ge(sig("softplus_ln"), 1)
            dve.scalar_tensor_tensor(dt_all, sp1, 0.0, sp2, ALU.max, ALU.add)
            dve.tensor_scalar(aneg, aneg, -1.0, None, ALU.mult)
            dve.drain()
            dve.tensor_tensor(da, dt_all, heads_on_all(aneg), ALU.mult).then_inc(sig("da_ready"), 1)
            b = full("dt", "acs")
            dve.tensor_copy(acs, chunk_heads(b)).then_inc(bank_free[b], 1)
            b = full("dt", "tot")
            dve.tensor_copy(tot, chunk_heads(b)).then_inc(bank_free[b], 1)
            b = full("dt", "acsT")
            dve.tensor_copy(acsT[0:S_HEADS, :], psum[0:S_HEADS, b, :]).then_inc(bank_free[b], 1)
            dve.drain()
            dve.tensor_tensor(decay_end, tot, acs, ALU.subtract).then_inc(sig("sums_ready"), 1)

            def by_head(ap, nh):
                return ap.rearrange("p (h d) -> p h d", h=nh)

            with dve.Fori(0, S_GROUPS) as g:
                def taps(n, name, blk):
                    dve.wait_ge(sig("conv_begun"), g * 6 + (n + 1))
                    b = banks.at("ssd", name)[0]
                    for back in range(1, TAPS):
                        m = dve.scalar_tensor_tensor(cv[:, n % 3, back:T], psum[:, b, 0:T - back],
                                                     col_a[:, ds(blk + (A_CW + (3 - back) * CONV_BLOCKS), 1)],
                                                     cv[:, n % 3, back:T], ALU.mult, ALU.add)
                        if back < TAPS - 1:
                            dve.drain()
                    m.then_inc(bank_free[b], 1)

                def diff(j):
                    b = full("ssd", ("acs", j), g)
                    dve.tensor_tensor(by_block(Mh[:, j, :]), by_block(psum[:, b, :]),
                                      acs[:, :, ds(g * S_HPG + j, 1)].broadcast_to([P, NT, P]), ALU.subtract)\
                        .then_inc(bank_free[b], 1)
                    dve.drain()
                    dve.tensor_scalar(Mh[:, j, :], Mh[:, j, :], 0.0, None, ALU.min).then_inc(sig("diff_ready"), 1)

                def weights(j):
                    dve.wait_ge(sig("exp_ready"), g * S_HPG + (j + 1))
                    dve.tensor_tensor(Mh[:, j, :], Mh[:, j, :], CBm[:].rearrange("p t l -> p (t l)"),
                                      ALU.mult).then_inc(sig("M_ready"), 1)

                def x_dt(m):
                    wait_taken(dve, "ssd", ("xt", m), g)
                    dst = xdt[:, :, m * P:(m + 1) * P].rearrange("p t (h d) -> p t h d", h=2)
                    src = xr[:, :, m * P:(m + 1) * P].rearrange("p t (h d) -> p t h d", h=2)
                    dve.tensor_tensor(dst, src, dt_all[:, :, ds(g * S_HPG + 2 * m, 2)].unsqueeze(3)
                                      .broadcast_to([P, NT, 2, S_P]), ALU.mult).then_inc(sig("xdt_ready"), 1)

                taps(0, "B", g + 16)
                taps(1, "C", g + 20)
                for j in range(4):
                    diff(j)
                taps(2, ("x", 0), 4 * g)
                for j in range(4, S_HPG):
                    diff(j)
                taps(3, ("x", 1), 4 * g + 1)
                x_dt(0)
                taps(4, ("x", 2), 4 * g + 2)
                b = full("ssd", "CB", g)
                dve.tensor_tensor(CBm, by_block(psum[:, b, :]), tri.unsqueeze(1).broadcast_to([P, NT, P]), ALU.mult)\
                    .then_inc(bank_free[b], 1)
                dve.drain()
                x_dt(1)
                for j in range(4):
                    weights(j)
                taps(5, ("x", 3), 4 * g + 3)
                x_dt(2)
                for j in range(4, S_HPG):
                    weights(j)
                x_dt(3)
                dve.wait_ge(sig("decays"), 1)
                for c in range(NT - 1):
                    if c:
                        dve.tensor_tensor(by_head(prev[:, c, :], S_HPG), by_head(prev[:, c - 1, :], S_HPG),
                                          edec[:, c, ds(g * S_HPG, S_HPG)].unsqueeze(2).broadcast_to([P, S_HPG, S_P]), ALU.mult)
                        dve.drain()
                    b = full("ssd", ("st", c), g)
                    if c:
                        dve.tensor_tensor(prev[:, c, :], prev[:, c, :], psum[:, b, :], ALU.add).then_inc(bank_free[b], 1)
                    else:
                        dve.tensor_copy(prev[:, c, :], psum[:, b, :]).then_inc(bank_free[b], 1)
                    dve.drain()
                dve.wait_ge(sig("xD_ready"), g * 4 + 4)
                for c in range(NT):
                    if c:
                        dve.drain()
                    b = full("ssd", ("yd", c), g)
                    dve.tensor_tensor(ybuf, psum[:, b, :], xr[:, c, :], ALU.add).then_inc(bank_free[b], 1)
                    if c:
                        b = full("ssd", ("yo", c), g)
                        dve.tensor_tensor(by_head(yoff, S_HPG), by_head(psum[:, b, :], S_HPG),
                                          ecs[:, c, ds(g * S_HPG, S_HPG)].unsqueeze(2).broadcast_to([P, S_HPG, S_P]), ALU.mult)\
                            .then_inc(bank_free[b], 1)
                        dve.drain()
                        dve.tensor_tensor(ybuf, ybuf, yoff, ALU.add)
                    dve.drain()
                    wait_taken(dve, "ssd", ("z", c), g)
                    dve.tensor_tensor(ys[c][:, ds(g * HALF, HALF)], ybuf, zs[:, c, :], ALU.mult).then_inc(sig("y_gated"), 1)
            dve.wait_ge(sig("ssq_ready"), NT * S_GROUPS)
            dve.tensor_scalar(srs[:, 0, :], ssq[:].rearrange("p t g -> p (t g)"), 1.0 / HALF, RMS_EPS, ALU.mult, ALU.add)\
                .then_inc(sig("sms_ready"), 1)
            dve.wait_ge(sig("srs_ready"), 1)
            dve.reciprocal(srs[:, 0, :], srs[:, 1, :])
            dve.drain()

            def y_turned(t):
                for g in (1, 3):
                    b = full("yT", (t, g))
                    for c in range(4):
                        k = 4 * g + c
                        m = dve.tensor_scalar(yT[t][:, k, :], psum[:, b, c * P:(c + 1) * P], col_b[:, B_SN + k:B_SN + k + 1],
                                              None, ALU.mult)
                    m.then_inc(bank_free[b], 1)

            for t in range(NT):
                for g in range(S_GROUPS):
                    n = t * S_GROUPS + g
                    m = dve.tensor_scalar(ys[t][:, g * HALF:(g + 1) * HALF], ys[t][:, g * HALF:(g + 1) * HALF],
                                          srs[:, 0, n:n + 1], None, ALU.mult)
                m.then_inc(sig("y_normed"), 1)
                if t:
                    y_turned(t - 1)
            y_turned(NT - 1)

            norms = [0]

            def stats(src, t, eps, centred):
                for h in range(2):
                    dve.bn_stats(st6[:, t, h, :], src[:, h * HALF:(h + 1) * HALF])
                dve.drain()
                dve.bn_aggr(mv[:, t, :], st6[:, t, :, :].rearrange("p h s -> p (h s)"))
                dve.drain()
                if not centred:
                    dve.scalar_tensor_tensor(mv[:, t, 1:2], mv[:, t, 0:1], mv[:, t, 0:1], mv[:, t, 1:2], ALU.mult, ALU.add)
                    dve.drain()
                return dve.tensor_scalar(ms[:, t, 0:1], mv[:, t, 1:2], eps, None, ALU.add)

            def norm(t, src, dst, eps, centred, gain=None):
                n = NT * norms[0] + t + 1
                stats(src, t, eps, centred).then_inc(var_ready, 1)
                dve.wait_ge(root_ready, n)
                dve.reciprocal(ms[:, t, 2:3], ms[:, t, 1:2])
                dve.drain()
                if centred:
                    return dve.tensor_scalar(dst, src, mv[:, t, 0:1], ms[:, t, 2:3], ALU.subtract, ALU.mult)
                if gain is None:
                    return dve.tensor_scalar(dst, src, ms[:, t, 2:3], None, ALU.mult)
                return dve.scalar_tensor_tensor(dst, src, ms[:, t, 2:3], gain, ALU.mult, ALU.mult)

            def add_and_norm(out_stage, norm_stage, gain, bias, res_from):
                for h in range(NHALF):
                    for t in range(NT):
                        if h == 0 and res_from:
                            dve.wait_ge(res_ready, res_from)
                        b = full(out_stage, t, h)
                        cols = slice(h * HALF, (h + 1) * HALF)
                        dve.scalar_tensor_tensor(rn[:, t, cols], res[:, t, cols], ALPHA, psum[:, b, :], ALU.mult, ALU.add)\
                            .then_inc(bank_free[b], 1)
                        if h == 1:
                            dve.drain()
                            norm(t, rn[:, t, :], rn[:, t, :], LN_EPS, True).then_inc(norm_ready, 1)
                            if t:
                                turned_out(norm_stage, t - 1, gain, bias)
                turned_out(norm_stage, NT - 1, gain, bias)
                norms[0] += 1

            def mlp(i):
                with dve.Fori(0, 4) as j:
                    for n in range(2):
                        for c in range(4):
                            wait_taken(dve, f"up{i}", (n, c), j)
                            a = hid[:, ds(j * 8 + (n * 4 + c), 1), :].rearrange("p a l -> p (a l)")
                            dve.tensor_tensor(a, a, a, ALU.mult).then_inc(sig("hidden"), 1)
                add_and_norm(f"down{i}", f"norm{i}1", B_G + 16 * i + 8, B_B + 16 * i + 8, NT * (2 * i + 1))

            def ple(i):
                dve.wait_ge(res_ready, NT * (2 * i + 2))
                for t in range(NT):
                    for h in range(NHALF):
                        cols = slice(h * HALF, (h + 1) * HALF)
                        b = full(f"proj{i}", (h, t))
                        wait_taken(dve, f"gate{i}", (h, t))
                        dve.tensor_tensor(sg[:, t, cols], sg[:, t, cols], psum[:, b, :], ALU.mult).then_inc(bank_free[b], 1)
                    dve.drain()
                    dve.tensor_tensor(res[:, t, :], res[:, t, :], sg[:, t, :], ALU.add).then_inc(sig(f"ple_done{i}"), 1)

            add_and_norm("ssd_out", "norm00", B_G, B_B, 0)
            mlp(0)
            ple(0)
            for t in range(NT):
                turned_out("turn0", t)

            def head_gates(par, h):
                dve.wait_ge(sig("ln_ready"), h + 1)
                b = banks.at("hgrn", "f")[0]
                dve.scalar_tensor_tensor(f_t[:, 1, :], psum[:, b, :], 0.0, f_t[:, 1, :], ALU.min, ALU.subtract)
                dve.drain()
                dve.tensor_tensor(f_t[:, 0, :], f_t[:, 1, :], psum[:, b, :], ALU.subtract).then_inc(bank_free[b], 1)
                for c in range(NT):
                    m = dve.tensor_tensor_scan(f_b[:, par, c * P:(c + 1) * P], ones, f_t[:, 1, c * P:(c + 1) * P], 0.0,
                                               ALU.mult, ALU.add)
                m.then_inc(sig("b_ready"), 1)

            def head_core(par, h):
                def from_middle(n):
                    half = 64 >> n
                    v = dif[:, n % 2, :].rearrange("p (a l) -> p a l", l=2 * half)
                    w = f_b[:, par, :].rearrange("p (a l) -> p a l", l=2 * half)
                    dve.tensor_tensor(v, w, w[:, :, half - 1:half].broadcast_to([P, T // (2 * half), 2 * half]), ALU.subtract)\
                        .then_inc(sig("dif_ready"), 1)

                def level(n):
                    dve.wait_ge(sig("dexp_ready"), h * LEVELS + (n + 1))

                    def halves(ap):
                        return ap.rearrange("p (a s l) -> p a s l", s=2, l=64 >> n)
                    e, o = halves(dif[:, n % 2, :]), halves(lev[:, n % 2, :])
                    if n == 0:
                        dve.wait_ge(sig("k_ready"), h + 1)
                    dve.tensor_tensor(o[:, :, 0, :], e[:, :, 0, :], halves(f_k[:, par, :])[:, :, 0, :], ALU.mult)
                    dve.tensor_tensor(o[:, :, 1, :], e[:, :, 1, :], halves(f_q[:, par, :])[:, :, 1, :], ALU.mult)\
                        .then_inc(sig("level_ready"), 1)

                def take(n):
                    b = full("hgrn", ("lev", n), h)
                    dve.sem_inc(sig("level_filled"), 1)
                    mask = con[:, C_MASK + n * P:C_MASK + (n + 1) * P].bitcast(I32)
                    dve.copy_predicated(by_block(scT[:, par, :]), mask.unsqueeze(1).broadcast_to([P, NT, P]),
                                        by_block(psum[:, b, :])).then_inc(bank_free[b], 1)

                dve.drain()
                from_middle(0)
                from_middle(1)
                for n in range(LEVELS):
                    level(n)
                    dve.drain()
                    if n + 2 < LEVELS:
                        from_middle(n + 2)
                    if n:
                        take(n - 1)
                    if n == 5:
                        b = full("hgrn", "kt", h)
                        dve.tensor_copy(ktok, by_block(psum[:, b, :])).then_inc(bank_free[b], 1)
                for c in range(NT - 1):
                    b = full("hgrn", ("st", c), h)
                    if c:
                        dve.scalar_tensor_tensor(state[:, c, :], state[:, c - 1, :], elast[:, c:c + 1], psum[:, b, 0:P],
                                                 ALU.mult, ALU.add).then_inc(bank_free[b], 1)
                    else:
                        dve.tensor_copy(state[:, 0, :], psum[:, b, 0:P]).then_inc(bank_free[b], 1)
                    dve.drain()
                take(LEVELS - 1)
                dve.drain()
                take(LEVELS)

            def head_out(par, h):
                dve.wait_ge(sig("oroot_ready"), h + 1)
                dve.reciprocal(hsq[:, 0, :], hsq[:, 1, :])
                dve.drain()
                b = banks.at("hgrn", "o")[0]
                for c in range(NT):
                    m = dve.scalar_tensor_tensor(o_s[:, c, :], psum[:, b, c * P:(c + 1) * P], hsq[:, 0, c:c + 1],
                                                 f_g[:, par, c, :], ALU.mult, ALU.mult)
                m.then_inc(bank_free[b], 1)

            dve.memset(scT[:, 0, :], 0.0)
            dve.memset(scT[:, 1, :], 0.0)
            dve.drain()
            head_gates(0, 0)
            head_core(0, 0)
            head_gates(1, 1)
            head_out(0, 0)
            with dve.Fori(0, H_HEADS // 2 - 1) as i:
                head_core(1, 2 * i + 1)
                head_gates(0, 2 * i + 2)
                head_out(1, 2 * i + 1)
                head_core(0, 2 * i + 2)
                head_gates(1, 2 * i + 3)
                head_out(0, 2 * i + 2)
            head_core(1, H_HEADS - 1)
            head_out(1, H_HEADS - 1)
            add_and_norm("hgrn_out", "norm10", B_G + 16, B_B + 16, 0)
            mlp(1)
            ple(1)

            dve.wait_ge(sig("pos_in"), 16)
            dve.tensor_copy(posf, posi.bitcast(I32))
            dve.drain()
            freq = con[:, C_FREQ:C_FREQ + HR].unsqueeze(1).broadcast_to([P, NT, HR])
            dve.tensor_tensor(ang, posf.unsqueeze(2).broadcast_to([P, NT, HR]), freq, ALU.mult)
            dve.drain()
            for dst, quarter in ((sinn, 0.0), (cosn, 0.25)):
                dve.tensor_scalar(turns, ang, 1.0 / TWO_PI, quarter, ALU.mult, ALU.add)
                dve.drain()
                dve.tensor_scalar(turns, turns, MAGIC, None, ALU.add)
                dve.drain()
                dve.tensor_scalar(turns, turns, -MAGIC, None, ALU.add)
                dve.drain()
                dve.scalar_tensor_tensor(dst, turns, -PI_A, ang, ALU.mult, ALU.add)
                dve.drain()
                dve.scalar_tensor_tensor(dst, turns, -PI_B, dst, ALU.mult, ALU.add)
                dve.drain()
                dve.scalar_tensor_tensor(dst, turns, -PI_C, dst, ALU.mult, ALU.add)
                dve.drain()
                dve.tensor_scalar(dst, dst, quarter * TWO_PI, None, ALU.add)
                dve.drain()
                m = dve.tensor_scalar(dst, dst, PI_CAP, -PI_CAP, ALU.min, ALU.max)
                if not quarter:
                    dve.drain()
            m.then_inc(sig("angles_ready"), 1)

            dve.wait_ge(sig("mem_in"), 16)
            for m_ in range(MT):
                stats(mem_tok[:, m_, :], m_, EPS, False).then_inc(sig("mem_ms"), 1)
                dve.wait_ge(sig("mem_root"), m_ + 1)
                dve.reciprocal(ms[:, m_, 2:3], ms[:, m_, 1:2])
                dve.drain()
                dve.tensor_scalar(mem_tok[:, m_, :], mem_tok[:, m_, :], ms[:, m_, 2:3], None, ALU.mult)\
                    .then_inc(sig("mem_normed"), 1)
            for m_ in range(MT):
                b = full("memT", (m_, 1))
                for c in range(4, 8):
                    m = dve.tensor_scalar(memT[:, c, m_ * P:(m_ + 1) * P], psum[:, b, (c - 4) * P:(c - 3) * P],
                                          col_b[:, B_MG + c:B_MG + c + 1], None, ALU.mult)
                m.then_inc(bank_free[b], 1)
            for t in range(NT):
                norm(t, res[:, t, :], rn[:, t, :], EPS, False).then_inc(norm_ready, 1)
                if t:
                    turned_out("norm_mla", t - 1, B_NG)
            turned_out("norm_mla", NT - 1, B_NG)
            norms[0] += 1

            def rotate(x1, x2, y1, y2, cos, sin, width):
                shape = list(x1.shape)
                tmp = [rt[:, n, 0:width] if len(shape) == 2 else rt[:, n, 0:width].rearrange("p (h d) -> p h d", d=HR)
                       for n in range(4)]
                for dst, a, w in zip(tmp, (x1, x2, x2, x1), (cos, sin, cos, sin)):
                    dve.tensor_tensor(dst, a, w, ALU.mult)
                dve.drain()
                dve.tensor_tensor(y1, tmp[0], tmp[1], ALU.subtract)
                return dve.tensor_tensor(y2, tmp[2], tmp[3], ALU.add)

            dve.wait_ge(sig("trig_ready"), 1)
            for name, s, width, dst in (("cq", 0, Q_LORA, cq_n), ("ckv", 1, KV_LORA, ckv_n)):
                for t in range(NT):
                    b = full(name, t)
                    r = rstat[:, s, t, :]
                    dve.bn_stats(r[:, 0:6], psum[:, b, 0:width])
                    dve.drain()
                    dve.bn_aggr(r[:, 6:8], r[:, 0:6])
                    dve.drain()
                    dve.scalar_tensor_tensor(r[:, 7:8], r[:, 6:7], r[:, 6:7], r[:, 7:8], ALU.mult, ALU.add)
                    dve.drain()
                    dve.tensor_scalar(r[:, 8:9], r[:, 7:8], EPS, None, ALU.add).then_inc(sig(f"{name}_ms"), 1)
                    if s:
                        m = rotate(psum[:, b, width:width + HR], psum[:, b, width + HR:width + ROPE],
                                   krope[:, t, 0:HR], krope[:, t, HR:ROPE], cosn[:, t, :], sinn[:, t, :], HR)
                        m.then_inc(sig("krope_ready"), 1)
                    dve.wait_ge(sig(f"{name}_root"), t + 1)
                    dve.reciprocal(r[:, 10:11], r[:, 9:10])
                    dve.drain()
                    dve.tensor_scalar(dst[:, t, :], psum[:, b, 0:width], r[:, 10:11], None, ALU.mult).then_inc(bank_free[b], 1)
            for t in range(NT):
                b = full("lora", ("q", t))
                for c in range(KQ):
                    m = dve.tensor_scalar(cqT[:, c, t * P:(t + 1) * P], psum[:, b, c * P:(c + 1) * P],
                                          col_b[:, B_QG + c:B_QG + c + 1], None, ALU.mult)
                m.then_inc(bank_free[b], 1)
            for n in range(3):
                for t in range(NT):
                    b = full("ukv", (n, t))
                    kv = psum[:, b, :].rearrange("p (h s d) -> p h s d", h=4, s=2)
                    k4 = k_tok[:, t, n * 4 * QK:(n + 1) * 4 * QK].rearrange("p (h d) -> p h d", h=4)
                    dve.tensor_copy(k4[:, :, 0:NOPE], kv[:, :, 0, :])
                    dve.tensor_copy(v_tok[:, t, n * 256:(n + 1) * 256].rearrange("p (h d) -> p h d", h=4), kv[:, :, 1, :])\
                        .then_inc(bank_free[b], 1)
            for t in range(NT):
                for n in range(3):
                    wait_taken(dve, "uq", (n, t))
                q3 = q_tok[:, t, :].rearrange("p (h d) -> p h d", h=A_HEADS)
                x1, x2 = q3[:, :, NOPE:NOPE + HR], q3[:, :, NOPE + HR:QK]
                bc = [v[:, t, :].unsqueeze(1).broadcast_to([P, A_HEADS, HR]) for v in (cosn, sinn)]
                rotate(x1, x2, x1, x2, bc[0], bc[1], A_HEADS * HR).then_inc(sig("q_roped"), 1)
                dve.drain()

            def softmax(stage, name, i, nth, width, scale, par, turned, col):
                def row_max(t):
                    b = full(stage, name("s", t), i)
                    dve.tensor_reduce(smx[:, par, 0, t:t + 1], psum[:, b, 0:width], AX.X, ALU.max)
                    dve.drain()
                    dve.tensor_scalar(smx[:, par, 1, t:t + 1], smx[:, par, 0, t:t + 1], -scale, None, ALU.mult)\
                        .then_inc(sig("max_ready"), 1)

                def prob_turned(t):
                    b = full(stage, name("pt", t), i)
                    weighed = nth * (NT - 1) + (0 if t == 0 else t - 1)
                    if not isinstance(weighed, int) or weighed > 0:
                        dve.wait_ge(sig("tile_weighed"), weighed)
                    dve.tensor_copy(probT[:, t % 2, 0:width], psum[:, b, 0:width]).then_inc(bank_free[b], 1)

                row_max(0)
                row_max(1)
                if turned:
                    b = full(stage, name("qt"), i)
                    dve.tensor_copy(qhT[0:QK, 1 - par, :], psum[0:QK, b, :]).then_inc(bank_free[b], 1)
                row_max(2)
                prob_turned(0)
                row_max(3)
                prob_turned(2)
                wait_taken(dve, stage, name("s", NT - 1), i)
                dve.reciprocal(smx[:, par, 3, :], smx[:, par, 2, :])
                dve.drain()
                b = full(stage, name("o"), i)
                dve.tensor_tensor(branch[:, :, col], psum[:, b, 0:NT * V_HEAD].rearrange("p (t d) -> p t d", t=NT),
                                  smx[:, par, 3, :].unsqueeze(2).broadcast_to([P, NT, V_HEAD]), ALU.mult)\
                    .then_inc(bank_free[b], 1)

            for h in range(M_HEADS):
                c0 = A_HEADS * V_HEAD + h * V_HEAD
                softmax("mheads", lambda *n: n, h, h, NMEM, M_SCALE, h % 2, False, slice(c0, c0 + V_HEAD))
            b = full("first_turn", ("qt",))
            dve.tensor_copy(qhT[0:QK, 0, :], psum[0:QK, b, :]).then_inc(bank_free[b], 1)
            with dve.Fori(0, A_HEADS // 2 - 1) as i:
                for par in range(2):
                    softmax("heads", lambda *n, par=par: (par,) + n, i, 2 * i + (par + M_HEADS), T, A_SCALE, par, True,
                            ds(i * (2 * V_HEAD) + par * V_HEAD, V_HEAD))
            for par in range(2):
                h = A_HEADS - 2 + par
                softmax("last_heads", lambda *n, par=par: (par,) + n, 0, M_HEADS + h, T, A_SCALE, par, par == 0,
                        slice(h * V_HEAD, (h + 1) * V_HEAD))
            for t in range(NT):
                turned_out("branchT", t)
            dve.wait_ge(gb_in, 16 * 9)
            for h in range(NHALF):
                for t in range(NT):
                    b = full("mla_out", t, h)
                    cols = slice(h * HALF, (h + 1) * HALF)
                    dve.tensor_tensor(rn[:, t, cols], res[:, t, cols], psum[:, b, :], ALU.add).then_inc(bank_free[b], 1)
                    if h == 1:
                        dve.drain()
                        norm(t, rn[:, t, :], res[:, t, :], EPS, False, gb[:, 0, :]).then_inc(sig("out_ready"), 1)

        @block.gpsimd
        def _(pool):
            pool.wait_ge(ssd_small_in, 64)
            pool.wait_ge(sig("decays"), 1)
            with pool.Fori(0, S_GROUPS) as g:
                for m in range(4):
                    pool.wait_ge(sig("xdt_ready"), g * 4 + (m + 1))

                    def heads(ap):
                        return ap[:, :, m * P:(m + 1) * P].rearrange("p t (h d) -> p t h d", h=2)
                    pool.tensor_tensor(heads(xw), heads(xdt), decay_end[:, :, ds(g * S_HPG + 2 * m, 2)].unsqueeze(3)
                                       .broadcast_to([P, NT, 2, S_P]), ALU.mult).then_inc(sig("xw_ready"), 1)
                    pool.tensor_tensor(heads(xr), heads(xr), dskip[:, ds(g * S_HPG + 2 * m, 2)].unsqueeze(1).unsqueeze(3)
                                       .broadcast_to([P, NT, 2, S_P]), ALU.mult).then_inc(sig("xD_ready"), 1)

            def load_gb(n, g, b=None):
                pool.dma_start(gb[:, 0, :], g.partition_broadcast(P)).then_inc(gb_in, 16)
                if b is not None:
                    pool.dma_start(gb[:, 1, :], b.partition_broadcast(P)).then_inc(gb_in, 16)

            def residual(n):
                pool.wait_ge(gb_in, 32 * (n + 1))
                for t in range(NT):
                    pool.wait_ge(norm_ready, NT * n + t + 1)
                    pool.tensor_tensor(res[:, t, :], rn[:, t, :], gb[:, 0, :], ALU.mult).then_inc(sig("res_scaled"), 1)
                    pool.wait_ge(sig("res_scaled"), NT * n + t + 1)
                    pool.tensor_tensor(res[:, t, :], res[:, t, :], gb[:, 1, :], ALU.add).then_inc(res_ready, 1)

            pool.wait_ge(units_begun, 2 * S_GROUPS)
            for n in range(2 * DEPTH):
                if n == 2:
                    with pool.Fori(0, H_HEADS // 2) as i:
                        for par in range(2):
                            h = 2 * i + par
                            pool.wait_ge(sig("ends_ready"), h + 1)
                            pool.wait_ge(sig("k_ready"), h + 1)
                            pool.tensor_tensor(qe, qe, f_q[:, par, :], ALU.mult).then_inc(sig("qe_ready"), 1)
                            pool.tensor_tensor(kend, kend, f_k[:, par, :], ALU.mult).then_inc(sig("kend_ready"), 1)
                if n:
                    pool.wait_ge(res_ready, NT * n)
                load_gb(n, ln_g[n // 2, n % 2], ln_b[n // 2, n % 2])
                residual(n)
            pool.wait_ge(res_ready, NT * 2 * DEPTH)
            load_gb(2 * DEPTH, fin_g)

            for t in range(NT):
                pool.wait_ge(sig("krope_ready"), t + 1)
                k3 = k_tok[:, t, :].rearrange("p (h d) -> p h d", h=A_HEADS)
                pool.tensor_copy(k3[:, :, NOPE:QK], krope[:, t, :].unsqueeze(1).broadcast_to([P, A_HEADS, ROPE]))\
                    .then_inc(sig("k_roped"), 1)
            pool.wait_ge(sig("k_roped"), NT)
            pool.wait_ge(sig("q_roped"), NT)
            for n in range(3):
                for t in range(NT):
                    wait_taken(pool, "ukv", (n, t))

            def head_rows(par, h):
                cols = slice(h * QK, (h + 1) * QK) if isinstance(h, int) else ds(h * QK, QK)
                pool.tensor_copy(hq[:, par, :, :], q_tok[:, :, cols]).then_inc(sig("hq_copied"), 1)
                pool.tensor_copy(hk[:, par, :, :], k_tok[:, :, cols]).then_inc(sig("head_rows"), 1)

            def gated(stage, name, i, col):
                wait_taken(pool, stage, name, i)
                pool.tensor_tensor(branch[:, :, col], branch[:, :, col], gate[:, :, col], ALU.mult)\
                    .then_inc(sig("branch_gated"), 1)

            head_rows(0, 0)
            head_rows(1, 1)
            for h in range(NHALF):
                for t in range(NT):
                    wait_taken(pool, "mgate", (h, t))
            for h in range(M_HEADS):
                c0 = A_HEADS * V_HEAD + h * V_HEAD
                gated("mheads", ("o",), h, slice(c0, c0 + V_HEAD))
            with pool.Fori(0, A_HEADS // 2 - 1) as i:
                for par in range(2):
                    gated("heads", (par, "o"), i, ds(i * (2 * V_HEAD) + par * V_HEAD, V_HEAD))
                    head_rows(par, 2 * i + (2 + par))
            for par in range(2):
                h = A_HEADS - 2 + par
                gated("last_heads", (par, "o"), 0, slice(h * V_HEAD, (h + 1) * V_HEAD))


def kernel(**inputs):
    import concourse.bacc as bacc
    from concourse.bass_utils import run_bass_kernel_spmd

    a = {k: np.asarray(v) for k, v in inputs.items()}
    conv = np.concatenate([a["ssd_conv_w"].reshape(-1, P), a["ssd_conv_b"].reshape(-1, P)])
    par_b = np.concatenate([a[k].reshape(-1, P) for k in
                            ("ln_g", "ln_b", "ssd_norm_w", "norm_g_l0_2", "mem_norm_g_l0_2", "q_norm_g_l0_2",
                             "kv_norm_g_l0_2", "hgrn_norm_w")])
    data = {
        "x": a["x"][0], "p": a["p"][:, 0], "cst": shape_constants(), "par_a": conv, "par_b": par_b,
        "w_ssd": a["ssd_w_in"][0], "w_dt": a["ssd_w_in"][0][:, S_DT:], "dt_bias": a["ssd_dt_bias"][0],
        "a_log": a["ssd_a_log"][0], "d_skip": a["ssd_d"][0], "w_ssd_out": a["ssd_w_out"][0], "w_hgrn": a["hgrn_w_in"][0],
        "w_hgrn_out": a["hgrn_w_out"][0], "ln_g": a["ln_g"], "ln_b": a["ln_b"], "w_mlp1": a["mlp_w1"], "w_mlp2": a["mlp_w2"],
        "w_gate": a["ple_w_gate"], "w_proj": a["ple_w_proj"], "mem": a["mem_2"][0], "pos": a["positions_2"][0],
        "w_mla": a["w_in_l0_2"], "w_uq": a["w_uq_l0_2"], "w_ukv": a["w_ukv_l0_2"], "w_mem": a["w_mem_kv_l0_2"],
        "w_mla_out": a["w_out_l0_2"], "fin_g": a["final_norm_g_2"],
    }
    data = {k: np.ascontiguousarray(v) for k, v in data.items()}
    nc = bacc.Bacc("TRN2", target_bir_lowering=False, num_devices=1)
    args = {k: nc.dram_tensor(f"in_{k}", v.shape, mybir.dt.from_np(v.dtype), kind="ExternalInput").ap() for k, v in data.items()}
    out = nc.dram_tensor("out_rows", (T, D), F32, kind="ExternalOutput").ap()
    build(nc, **args, out=out)
    r = run_bass_kernel_spmd(nc, [{f"in_{k}": v for k, v in data.items()}], core_ids=[0])
    return r.results[0]["out_rows"].reshape(1, T, D)
```

```python
from contextlib import ExitStack

import numpy as np

import concourse.bass as bass
from concourse import mybir

ALU = mybir.AluOpType
ACT = mybir.ActivationFunctionType
AX = mybir.AxisListType
F32 = mybir.dt.float32
I32 = mybir.dt.int32
F32R = mybir.dt.float32r
ds = bass.ds

P = 128
T = 512
NT = T // P
D = 1024
KD = D // P
HALF = 512
NHALF = D // HALF
DEPTH = 2
ALPHA = (2.0 * DEPTH) ** 0.25
LN_EPS = 1e-5
RMS_EPS = 1e-5
EPS = 1e-6
ARENA = 26112
DFF = 4 * D
KF = DFF // P
PLE = 256
KP = PLE // P

S_IN = 2 * D
S_HEADS, S_P, S_GROUPS, S_N = 32, 64, 4, 128
S_HPG = S_HEADS // S_GROUPS
S_Z, S_X, S_B = 0, S_IN, 2 * S_IN
S_C = S_B + S_GROUPS * S_N
S_DT = S_C + S_GROUPS * S_N
KS = S_IN // P
CONV_BLOCKS = 24
TAPS = 4

H_HEADS = 8
LEVELS = 7

NMEM = 256
MT = NMEM // P
Q_LORA, KV_LORA, ROPE = 384, 256, 32
HR = ROPE // 2
NOPE, V_HEAD = 64, 64
QK = NOPE + ROPE
A_HEADS, M_HEADS, M_HEAD = 12, 4, 64
MEM_W = 256
KQ, KKV = Q_LORA // P, KV_LORA // P
A_SCALE = 1.0 / float(np.sqrt(QK))
M_SCALE = 1.0 / float(np.sqrt(M_HEAD))
O_KV, O_QM, O_GATE = Q_LORA, Q_LORA + KV_LORA + ROPE, Q_LORA + KV_LORA + ROPE + MEM_W

C_ID, C_TRI, C_ONE, C_MASK = 0, P, 2 * P, 3 * P
C_FREQ = C_MASK + (LEVELS + 1) * P
C_ALL = C_FREQ + HR
A_CW, A_CB, A_ROWS = 0, TAPS * CONV_BLOCKS, (TAPS + 1) * CONV_BLOCKS
B_G, B_B, B_SN, B_NG, B_MG, B_QG, B_KG, B_HG = 0, 32, 64, 80, 88, 96, 99, 101
B_ROWS = 102

QUARTERS = 4
MLP_UNITS = ("up0", "up1", "down0", "down1")

TWO_PI = 2.0 * np.pi
PI_A = 6.28125
PI_B = float(np.float32(TWO_PI - PI_A))
PI_C = float(TWO_PI - PI_A - PI_B)
MAGIC = 1.5 * 2.0 ** 23
PI_CAP = 3.1415925


def shape_constants():
    c = np.zeros((P, C_ALL), np.float32)
    r = np.arange(P)
    c[:, C_ID:C_ID + P] = np.eye(P)
    c[:, C_TRI:C_TRI + P] = r[:, None] <= r[None, :]
    c[:, C_ONE:C_ONE + P] = 1.0
    for n in range(LEVELS):
        h = 64 >> n
        s, l = r[:, None], r[None, :]
        c[:, C_MASK + n * P:C_MASK + (n + 1) * P] = (s // (2 * h) == l // (2 * h)) & (s % (2 * h) < h) & (l % (2 * h) >= h)
    c[:, C_MASK + LEVELS * P:C_MASK + (LEVELS + 1) * P] = np.eye(P)
    c[:, C_FREQ:] = (1.0 / (10000.0 ** (np.arange(0, ROPE, 2, dtype=np.float32) / np.float32(ROPE)))).astype(np.float32)
    return c


class Banks:

    def __init__(self):
        self.before = [0] * 8
        self.table = {}

    def stage(self, stage, uses, turns=1):
        per = [0] * 8
        for name, b in uses:
            self.table[stage, name] = (b, self.before[b] + per[b], b)
            per[b] += 1
        for name, b in uses:
            bank, first, _ = self.table[stage, name]
            self.table[stage, name] = (bank, first, per[bank])
        for b in range(8):
            self.before[b] += per[b] * turns

    def at(self, stage, name, i=0):
        bank, first, per = self.table[stage, name]
        return bank, first + i * per


def first_and_last(k, n):
    return {"start": k == 0, "stop": k == n - 1}


def build(nc, x, p, cst, par_a, par_b, w_ssd, w_dt, dt_bias, a_log, d_skip, w_ssd_out, w_hgrn, w_hgrn_out,
          ln_g, ln_b, w_mlp1, w_mlp2, w_gate, w_proj, mem, pos, w_mla, w_uq, w_ukv, w_mem, w_mla_out, fin_g, out):
    with ExitStack() as ctx:
        def sb(name, shape, dt=F32):
            return ctx.enter_context(nc.sbuf_tensor(name, shape, dt))

        def sem(name):
            return ctx.enter_context(nc.semaphore(name))

        slots = [sb(f"slot{s}", [P, 4096]) for s in range(2)]
        res = sb("res", [P, NT, D])
        rn = sb("rn", [P, NT, D])
        fT = sb("fT", [P, KD, T])
        gb = sb("gb", [P, 2, D])
        con = sb("con", [P, C_ALL])
        col_a = sb("col_a", [P, A_ROWS])
        col_b = sb("col_b", [P, B_ROWS])
        eps_h = sb("eps_h", [P, 1])
        pT = sb("pT", [P, DEPTH, KP, T])
        posi = sb("posi", [P, NT])
        st6 = sb("st6", [P, NT, 2, 6])
        mv = sb("mv", [P, NT, 2])
        ms = sb("ms", [P, NT, 3])
        arena = sb("arena", [P, ARENA])
        arena_base = nc.sbuf_base - 4 * ARENA
        psum = ctx.enter_context(nc.psum_tensor("psum", [P, 8, HALF], F32))
        tri = con[:, C_TRI:C_TRI + P]
        ones = con[:, C_ONE:C_ONE + P]

        at = [0]

        def carve(*shape):
            n = int(np.prod(shape))
            assert at[0] + n <= ARENA, (at[0], n)
            v = arena[:, at[0]:at[0] + n]
            at[0] += n
            if len(shape) == 2:
                v = v.rearrange("p (a b) -> p a b", a=shape[0])
            if len(shape) == 3:
                v = v.rearrange("p (a b c) -> p a b c", a=shape[0], b=shape[1])
            return v

        s_par = carve(2, P)
        s_p = carve(DEPTH * NT, PLE)
        at[0] = 0
        BT = carve(T)
        CT = carve(T)
        Btok = carve(NT, P)
        CBm = carve(NT, P)
        cv = carve(3, T)
        xr = carve(NT, HALF)
        xdt = carve(NT, HALF)
        xw = carve(NT, HALF)
        Mh = carve(S_HPG, T)
        zs = carve(NT, HALF)
        prev = carve(NT - 1, HALF)
        rows = carve(2, T)
        ybuf = carve(HALF)
        yoff = carve(HALF)
        y_hi = carve(2, S_IN)
        wdt = carve(KD, S_HEADS)
        small = carve(5, S_HEADS)
        dbias, aneg, dskip, dtmp, _ = [small[:, n, :] for n in range(5)]
        dt_all = carve(NT, S_HEADS)
        da = carve(NT, S_HEADS)
        acs = carve(NT, S_HEADS)
        tot = carve(NT, S_HEADS)
        decay_end = carve(NT, S_HEADS)
        ecs = carve(NT, S_HEADS)
        edec = carve(NT, S_HEADS)
        sp1 = carve(NT, S_HEADS)
        sp2 = carve(NT, S_HEADS)
        acsT = carve(T)
        ssq = carve(NT, S_GROUPS)
        srs = carve(2, NT * S_GROUPS)
        y_lo = rn[:].rearrange("p t d -> p (t d)").rearrange("p (t d) -> p t d", t=2)
        ys = [y_lo[:, 0, :], y_lo[:, 1, :], y_hi[:, 0, :], y_hi[:, 1, :]]
        bc_w = gb[:].rearrange("p a b -> p (a b)").rearrange("p (k n) -> p k n", k=KD)
        yT = [Mh[:].rearrange("p a b -> p (a b)")[:, 0:KS * P].rearrange("p (k l) -> p k l", k=KS),
              Mh[:].rearrange("p a b -> p (a b)")[:, KS * P:2 * KS * P].rearrange("p (k l) -> p k l", k=KS),
              arena[:, 0:2048].rearrange("p (k l) -> p k l", k=KS),
              arena[:, 3584:3584 + 2048].rearrange("p (k l) -> p k l", k=KS)]
        def part(name, first, *shape):
            return nc.alloc_sbuf_tensor_at(name, [P, *shape], F32R, offset=arena_base + 4 * first)

        f_hi, f_lo = part("f_hi", 5632, KD, T), part("f_lo", 13824, KD, T)
        w_hi, w_lo = part("w_hi", 17920, KD, HALF), part("w_lo", 22016, KD, HALF)
        hid_hi, hid_lo = part("hid_hi", 0, KD, T), part("hid_lo", 9728, KD, T)
        sq = arena[:, 4096:4096 + 3 * T].rearrange("p (a l) -> p a l", a=3)
        sg = arena[:, 9728:9728 + 4096].rearrange("p (t d) -> p t d", t=NT)
        at[0] = 0
        f_q = carve(2, T)
        f_k = carve(2, T)
        f_b = carve(2, T)
        f_v = carve(2, NT, P)
        f_g = carve(2, NT, P)
        kend = carve(T)
        assert at[0] <= 5632
        at[0] = 9728
        f_t = carve(2, T)
        dif = carve(2, T)
        lev = carve(2, T)
        scT = carve(2, T)
        assert at[0] <= 13824
        oT = rn[:].rearrange("p t d -> p (t d)").rearrange("p (h l) -> p h l", h=H_HEADS)
        o_hi, o_lo = part("o_hi", 5632, H_HEADS, T), part("o_lo", 13824, H_HEADS, T)
        ktok = fT[:, 0, :].rearrange("p (c l) -> p c l", c=NT)
        qe = fT[:, 1, :]
        o_s = fT[:, 2, :].rearrange("p (c l) -> p c l", c=NT)
        junk_h = fT[:, 3, :].rearrange("p (c l) -> p c l", c=NT)
        state = fT[:, 4, 0:(NT - 1) * P].rearrange("p (c l) -> p c l", c=NT - 1)
        elast = fT[:, 5, 0:NT]
        hsq = fT[:, 6, 0:2 * NT].rearrange("p (a c) -> p a c", a=2)
        at[0] = 0
        q_tok = carve(NT, A_HEADS * QK)
        k_tok = carve(NT, A_HEADS * QK)
        v_tok = carve(NT, A_HEADS * V_HEAD)
        branch = carve(NT, D)
        at_pre = at[0]
        cq_n = carve(NT, Q_LORA)
        ckv_n = carve(NT, KV_LORA)
        cqT = carve(KQ, T)
        ckvT = carve(KKV, T)
        at_post = at[0]
        at[0] = at_pre
        hq = carve(2, NT, QK)
        hk = carve(2, NT, QK)
        qhT = carve(2, T)
        khT = carve(2, T)
        prob = carve(2, T)
        probT = carve(2, T)
        smx = carve(2, 4, NT)
        assert at[0] <= at_post + 2000
        at[0] = max(at[0], at_post)
        qmT = carve(2, T)
        kmT = carve(2, NMEM)
        v_mem = carve(MT, MEM_W)
        krope = carve(NT, ROPE)
        cosn = carve(NT, HR)
        sinn = carve(NT, HR)
        ang = carve(NT, HR)
        turns = carve(NT, HR)
        posf = carve(NT)
        rstat = carve(2, NT, 12)
        rt = carve(4, A_HEADS * HR)
        mem_tok = q_tok[:].rearrange("p a b -> p (a b)")[:, 0:MT * D].rearrange("p (a b) -> p a b", a=MT)
        memT = k_tok[:].rearrange("p a b -> p (a b)")[:, 0:KD * NMEM].rearrange("p (a b) -> p a b", a=KD)
        gate = rn

        units_landed = [sem(f"units_landed{s}") for s in range(2)]
        units_begun = sem("units_begun")
        blocks_begun = sem("blocks_begun")
        high_made = sem("high_made")
        low_made = sem("low_made")
        input_high = sem("input_high")
        input_low = sem("input_low")
        bank_full = [sem(f"bank_full{b}") for b in range(8)]
        bank_free = [sem(f"bank_free{b}") for b in range(8)]
        con_in = sem("con_in")
        x_in = [sem(f"x_in{t}") for t in range(NT)]
        p_in = sem("p_in")
        par_in = sem("par_in")
        gb_in = sem("gb_in")
        var_ready = sem("var_ready")
        root_ready = sem("root_ready")
        norm_ready = sem("norm_ready")
        res_ready = sem("res_ready")
        ssd_small_in = sem("ssd_small_in")
        bc_in = sem("bc_in")
        out_done = sem("out_done")
        named = {}

        def sig(name):
            if name not in named:
                named[name] = sem(name)
            return named[name]

        banks = Banks()
        banks.stage("start", [("par", 0), ("par_b", 1)] + [(("x", t, h), 2 + (2 * t + h) % 4) for t in range(NT) for h in range(2)]
                    + [(("p", i, k), 6 + k) for i in range(DEPTH) for k in range(KP)])
        banks.stage("dt", [("dt", 0), ("acs", 1), ("tot", 2), ("acsT", 3)])
        banks.stage("ssd", [("B", 0), ("C", 1), (("acs", 0), 4), (("acs", 1), 5), (("acs", 2), 6), (("acs", 3), 7),
                            (("x", 0), 2), (("acs", 4), 4), (("acs", 5), 5), (("acs", 6), 6), (("acs", 7), 7),
                            (("x", 1), 3), (("xt", 0), 4), (("x", 2), 0), ("CB", 2), ("BT", 3), (("xt", 1), 5),
                            (("x", 3), 1), (("xt", 2), 6), (("z", 0), 0), (("xt", 3), 7), (("z", 1), 1),
                            (("z", 2), 2), (("z", 3), 3), (("st", 0), 4), (("st", 1), 5), (("st", 2), 6),
                            (("yd", 0), 7), (("yd", 1), 4), (("yo", 1), 7), (("yd", 2), 5), (("yo", 2), 4),
                            (("yd", 3), 6), (("yo", 3), 5)], S_GROUPS)
        banks.stage("yT", [((t, g), 4 + g) for t in range(NT) for g in range(S_GROUPS)])

        def norm_banks(stage, first=4):
            banks.stage(stage, [((t, h), first + (2 * t + h) % 4) for t in range(NT) for h in range(2)])

        def out_banks(stage):
            banks.stage(stage, [(t, t) for t in range(NT)], NHALF)

        def mlp_banks(i):
            banks.stage(f"mlp{i}", [((kind, m), 4 * (u % 2) + m) for u, kind in enumerate(MLP_UNITS) for m in range(4)], QUARTERS)
            norm_banks(f"norm{i}1", 0)

        def ple_banks(i):
            banks.stage(f"gate{i}", [((h, t), (4, 0)[h] + t) for h in range(NHALF) for t in range(NT)])
            banks.stage(f"proj{i}", [((h, t), (4, 0)[h] + t) for t in range(NT) for h in range(NHALF)])

        out_banks("ssd_out")
        norm_banks("norm00")
        mlp_banks(0)
        ple_banks(0)
        norm_banks("turn0")
        banks.stage("hgrn", [(n, b) for n, b in (("q", 0), ("f", 1), ("vg0", 2), ("vg1", 3))]
                    + [(("lev", n), 4 + n % 2) for n in range(LEVELS + 1)]
                    + [("kt", 6), (("st", 0), 7), (("st", 1), 6), (("st", 2), 7), ("o", 6), ("ot", 7)], H_HEADS)
        banks.stage("hgrn_out", [((h, t), (4, 0)[h] + t) for h in range(NHALF) for t in range(NT)])
        norm_banks("norm10")
        mlp_banks(1)
        ple_banks(1)
        banks.stage("memT", [((m, h), 2 * m + h) for m in range(MT) for h in range(2)])
        banks.stage("memkv", [(("k", c), c) for c in range(2)] + [(("v", m), 2 + m) for m in range(MT)])
        norm_banks("norm_mla")
        banks.stage("cq", [(t, t) for t in range(NT)])
        banks.stage("ckv", [(t, t) for t in range(NT)])
        banks.stage("lora", [(("q", t), 4 + t) for t in range(NT)] + [(("kv", t), 4 + t) for t in range(NT)])
        banks.stage("qm", [(c, c) for c in range(2)])
        banks.stage("mgate", [((h, t), t) for h in range(NHALF) for t in range(NT)])
        banks.stage("uq", [((n, t), t) for n in range(3) for t in range(NT)])
        banks.stage("ukv", [((n, t), 4 + t) for n in range(3) for t in range(NT)])

        def head_banks(name=lambda *n: n, turns=True, scores=True):
            return [(name("next_s", t), t) for t in range(NT) if scores] + ([(name("qt"), 5), (name("kt"), 4)] if turns else []) \
                + [(name("pt", t), 6 + t % 2) for t in range(NT)] + [(name("o"), 4)]

        banks.stage("first_scores", [(("next_s", t), t) for t in range(NT)])
        for h in range(M_HEADS):
            banks.stage(f"mem{h}", head_banks(turns=h >= 2))
        banks.stage("heads", [u for par in range(2) for u in head_banks(lambda *n, par=par: (par,) + n)], A_HEADS // 2 - 1)
        banks.stage("last_head0", head_banks(turns=False))
        banks.stage("last_head1", head_banks(turns=False, scores=False))
        norm_banks("branchT")
        out_banks("mla_out")

        order = [("ssd", 2 * S_GROUPS), ("ssd_out", 4), ("mlp0", 4 * QUARTERS), ("gate0", 2), ("proj0", 1), ("hgrn", H_HEADS),
                 ("hgrn_out", 2), ("mlp1", 4 * QUARTERS), ("gate1", 2), ("proj1", 1), ("mem", 1), ("cq", 1), ("ckv", 1), ("qm", 1),
                 ("mgate", 2), ("uq", 1), ("ukv", 1), ("mla_out", 2)]
        in_parts = ("mlp0", "gate0", "hgrn_out", "mlp1", "gate1")
        unit0, part0, split_units, n_units = {}, {}, [], 0
        for name, n in order:
            unit0[name] = n_units
            n_units += n
            part0[name] = len(split_units)
            if name in in_parts:
                split_units += range(unit0[name], n_units)

        def slot_of(stage, n=0):
            return slots[(unit0[stage] + n) % 2]

        def as_k(s, cols=HALF):
            return s[:, 0:4096 // cols * cols].rearrange("p (k n) -> p k n", n=cols)

        LAND = 4 * 16

        def landed(pe, stage, n=0, i=0, per=0):
            u = unit0[stage] + n
            pe.wait_ge(units_landed[u % 2], LAND * (u // 2 + 1) + i * (LAND * (per // 2)))

        def wait_taken(eng, stage, name, i=0):
            b, n = banks.at(stage, name, i)
            eng.wait_ge(bank_free[b], n + 1)

        def wait_full(eng, stage, name, i=0):
            b, n = banks.at(stage, name, i)
            eng.wait_ge(bank_full[b], n + 1)
            return b

        def wait_filled_before(eng, stage, name, i=0):
            b, n = banks.at(stage, name, i)
            if not isinstance(n, int) or n > 0:
                eng.wait_ge(bank_full[b], n)

        def by_block(ap, t=NT):
            return ap.rearrange("p (t l) -> p t l", t=t)

        block = ctx.enter_context(nc.Block())

        @block.sync
        def _(sp):
            def slot_free(stage, n=0, i=0, per=0):
                u = unit0[stage] + n
                if stage in in_parts and u - 2 in split_units:
                    sp.wait_ge(low_made, (split_units.index(u - 2) + 1) * KD + i * (per * KD))
                    sp.sem_inc(sig("slot_given"), 1)
                elif stage == "mlp0" and n == 1:
                    wait_full(sp, "ssd_out", NT - 1, NHALF - 1)
                elif stage == "hgrn_out" or stage == "hgrn" and per:
                    head = n if stage == "hgrn" else H_HEADS + n
                    sp.wait_ge(sig("cols_low"), 3 * (head - 1) + i * (3 * per))
                    sp.sem_inc(sig("slot_given"), 1)
                elif u >= 2:
                    sp.wait_ge(units_begun, u + i * per)
                    sp.sem_inc(sig("slot_given"), 1)
                return slots[u % 2], units_landed[u % 2]

            def load(view, w, stage, n=0, i=0, per=0):
                s, done = slot_free(stage, n, i, per)
                nk = view[1]
                dst = s[:, 0:nk * view[2]].rearrange("p (k n) -> p k n", k=nk)
                step = nk // 4
                for c in range(4):
                    sp.dma_start(dst[:, c * step:(c + 1) * step, :], w(c * step, step)).then_inc(done, 16)

            def rows_cols(w2, row0, col0, cols):
                def pick(k, n):
                    return w2[ds(row0 + k * P, n * P) if not isinstance(row0, int) else slice(row0 + k * P, row0 + (k + n) * P),
                              ds(col0, cols) if not isinstance(col0, int) else slice(col0, col0 + cols)
                              ].rearrange("(k p) n -> p k n", p=P)
                return pick

            sp.dma_start(con[:], cst).then_inc(con_in, 16)
            for t in range(NT):
                sp.dma_start(res[:, t, :], x[t * P:(t + 1) * P, :]).then_inc(x_in[t], 16)
            sp.dma_start(s_par[0:A_ROWS, 0, :], par_a).then_inc(par_in, 16)
            sp.dma_start(s_par[0:B_ROWS, 1, :], par_b).then_inc(par_in, 16)
            for i in range(DEPTH):
                sp.dma_start(s_p[:, i * NT:(i + 1) * NT, :], p[i].rearrange("(t p) n -> p t n", p=P)).then_inc(p_in, 16)

            sp.dma_start(wdt, w_dt.rearrange("(k p) n -> p k n", p=P)).then_inc(ssd_small_in, 16)
            for dst, src in ((dbias, dt_bias), (aneg, a_log), (dskip, d_skip)):
                sp.dma_start(dst, src.partition_broadcast(P)).then_inc(ssd_small_in, 16)
            w3 = w_ssd.rearrange("(k p) n -> p k n", p=P)
            def load_group(g, first):
                if not first:
                    sp.wait_ge(units_begun, 2 * g)
                    sp.sem_inc(sig("slot_given"), 1)
                for n, c0 in enumerate((S_B, S_C)):
                    sp.dma_start(bc_w[:, :, n * P:(n + 1) * P], w3[:, :, ds(g * S_N + c0, S_N)]).then_inc(bc_in, 16)
                for c in range(4):
                    sp.dma_start(as_k(slots[0])[:, 2 * c:2 * c + 2, :],
                                 w3[:, 2 * c:2 * c + 2, ds(g * HALF + S_X, HALF)]).then_inc(units_landed[0], 16)
                if not first:
                    sp.wait_ge(units_begun, 2 * g + 1)
                    sp.sem_inc(sig("slot_given"), 1)
                for c in range(4):
                    sp.dma_start(as_k(slots[1])[:, 2 * c:2 * c + 2, :],
                                 w3[:, 2 * c:2 * c + 2, ds(g * HALF + S_Z, HALF)]).then_inc(units_landed[1], 16)

            load_group(0, True)
            with sp.Fori(1, S_GROUPS) as g:
                load_group(g, False)
            with sp.Fori(0, NHALF) as h:
                for n in range(2):
                    load((P, KD, HALF), rows_cols(w_ssd_out, n * D, h * HALF, HALF), "ssd_out", n, h, 2)

            def load_mlp(i):
                def up(j, n, q):
                    load((P, KD, HALF), rows_cols(w_mlp1[i], 0, (q + j) * (2 * HALF) + n * HALF, HALF), f"mlp{i}", 4 * j + n, q, 4)

                def down(h, q):
                    load((P, KD, HALF), rows_cols(w_mlp2[i], q * D, h * HALF, HALF), f"mlp{i}", 2 + h, q, 4)

                up(0, 0, 0)
                up(0, 1, 0)
                with sp.Fori(0, QUARTERS - 1) as q:
                    down(0, q)
                    down(1, q)
                    up(1, 0, q)
                    up(1, 1, q)
                down(0, QUARTERS - 1)
                down(1, QUARTERS - 1)

            def load_ple(i):
                for h in range(NHALF):
                    load((P, KD, HALF), rows_cols(w_gate[i], 0, h * HALF, HALF), f"gate{i}", h)
                s, done = slot_free(f"proj{i}")
                dst = s[:, 0:KP * D].rearrange("p (k n) -> p k n", k=KP)
                src = w_proj[i].rearrange("(k p) n -> p k n", p=P)
                for c in range(4):
                    sp.dma_start(dst[:, :, c * 256:(c + 1) * 256], src[:, :, c * 256:(c + 1) * 256]).then_inc(done, 16)

            load_mlp(0)
            load_ple(0)
            wh = w_hgrn.rearrange("(k p) n -> p k n", p=P)
            def load_head(n, i, per):
                s, done = slot_free("hgrn", n, i, per)
                for c in range(4):
                    first = c * D + n * P + (i * (2 * P) if per else 0)
                    sp.dma_start(as_k(s)[:, :, c * P:(c + 1) * P],
                                 wh[:, :, ds(first, P) if per else slice(first, first + P)]).then_inc(done, 16)

            for n in range(2):
                load_head(n, 0, 0)
            with sp.Fori(0, H_HEADS // 2 - 1) as j:
                for n in range(2):
                    load_head(2 + n, j, 2)
            for h in range(NHALF):
                load((P, KD, HALF), rows_cols(w_hgrn_out, 0, h * HALF, HALF), "hgrn_out", h)
            load_mlp(1)
            load_ple(1)
            sp.dma_start(mem_tok, mem.rearrange("(t p) n -> p t n", p=P)).then_inc(sig("mem_in"), 16)
            sp.dma_start(posi[:].bitcast(I32), pos.rearrange("(t p) -> p t", p=P),
                         allow_slow_non_contiguous=True).then_inc(sig("pos_in"), 16)
            load((P, KD, 2 * MEM_W), rows_cols(w_mem, 0, 0, 2 * MEM_W), "mem")
            load((P, KD, Q_LORA), rows_cols(w_mla, 0, 0, Q_LORA), "cq")
            load((P, KD, KV_LORA + ROPE), rows_cols(w_mla, 0, O_KV, KV_LORA + ROPE), "ckv")
            load((P, KD, MEM_W), rows_cols(w_mla, 0, O_QM, MEM_W), "qm")
            for h in range(NHALF):
                load((P, KD, HALF), rows_cols(w_mla, 0, O_GATE + h * HALF, HALF), "mgate", h)
            for name, w, nk, width in (("uq", w_uq, KQ, A_HEADS * QK), ("ukv", w_ukv, KKV, A_HEADS * 2 * NOPE)):
                s, done = slot_free(name)
                dst = s[:, 0:nk * width].rearrange("p (k n) -> p k n", k=nk)
                src = w.rearrange("(k p) n -> p k n", p=P)
                q = width // 4
                for c in range(4):
                    sp.dma_start(dst[:, :, c * q:(c + 1) * q], src[:, :, c * q:(c + 1) * q]).then_inc(done, 16)
            for h in range(NHALF):
                load((P, KD, HALF), rows_cols(w_mla_out, 0, h * HALF, HALF), "mla_out", h)
            for t in range(NT):
                sp.wait_ge(sig("out_ready"), t + 1)
                sp.dma_start(out[t * P:(t + 1) * P, :], res[:, t, :]).then_inc(out_done, 16)
            sp.wait_ge(out_done, 16 * NT)

        @block.tensor
        def _(pe):
            def claim(stage, name, i=0):
                b, n = banks.at(stage, name, i)
                if not isinstance(n, int) or n > 0:
                    pe.wait_ge(bank_free[b], n)
                return b

            def turn(b, cols, src, kp=P, mp=P):
                return pe.transpose(psum[0:mp, b, cols:cols + kp], src, con[0:kp, C_ID:C_ID + kp])

            def turn_rows(stage, src, t, wait_sem, n):
                pe.wait_ge(wait_sem, n)
                for h in range(2):
                    b = claim(stage, (t, h))
                    for c in range(4):
                        m = turn(b, c * P, src[:, t, (4 * h + c) * P:(4 * h + c + 1) * P])
                    m.then_inc(bank_full[b], 1)

            norms = [0]

            def norm_turns(stage, after):
                n = norms[0]
                norms[0] += 1
                for t in range(NT):
                    if after is not None:
                        after(t)
                    if t > 0:
                        turn_rows(stage, rn, t - 1, norm_ready, NT * n + t)
                return lambda: turn_rows(stage, rn, NT - 1, norm_ready, NT * (n + 1))

            def wait_features(stage, name=lambda t, h: (t, h)):
                for t in range(NT):
                    for h in range(2):
                        wait_taken(pe, stage, name(t, h))

            pe.wait_ge(con_in, 16)
            for t in range(NT):
                pe.wait_ge(x_in[t], 16)
                for h in range(2):
                    b = claim("start", ("x", t, h))
                    for c in range(4):
                        m = turn(b, c * P, res[:, t, (4 * h + c) * P:(4 * h + c + 1) * P])
                    m.then_inc(bank_full[b], 1)
            pe.wait_ge(par_in, 32)
            b = claim("start", "par")
            turn(b, 0, s_par[0:A_ROWS, 0, :], A_ROWS).then_inc(bank_full[b], 1)
            b = claim("start", "par_b")
            turn(b, 0, s_par[0:B_ROWS, 1, :], B_ROWS).then_inc(bank_full[b], 1)
            pe.wait_ge(p_in, 16 * DEPTH)
            for i in range(DEPTH):
                for k in range(KP):
                    b = claim("start", ("p", i, k))
                    for t in range(NT):
                        m = turn(b, t * P, s_p[:, i * NT + t, k * P:(k + 1) * P])
                    m.then_inc(bank_full[b], 1)
            wait_features("start", lambda t, h: ("x", t, h))

            pe.wait_ge(ssd_small_in, 64)
            b = claim("dt", "dt")
            for t in range(NT):
                for k in range(KD):
                    m = pe.matmul(psum[:, b, t * S_HEADS:(t + 1) * S_HEADS], fT[:, k, t * P:(t + 1) * P], wdt[:, k, :],
                                  **first_and_last(k, KD))
            m.then_inc(bank_full[b], 1)
            pe.wait_ge(sig("da_ready"), 1)
            for name, left in (("acs", tri), ("tot", ones)):
                b = claim("dt", name)
                for t in range(NT):
                    m = pe.matmul(psum[:, b, t * S_HEADS:(t + 1) * S_HEADS], left, da[:, t, :], start=True, stop=True)
                m.then_inc(bank_full[b], 1)
            b = claim("dt", "acsT")
            for t in range(NT):
                m = pe.matmul(psum[0:S_HEADS, b, t * P:(t + 1) * P], da[:, t, :], tri, start=True, stop=True)
            m.then_inc(bank_full[b], 1)

            with pe.Fori(0, S_GROUPS) as g:
                wx, wz = as_k(slots[0]), as_k(slots[1])
                pe.wait_ge(bc_in, 32 + g * 32)
                for n, name in enumerate(("B", "C")):
                    b = claim("ssd", name, g)
                    for k in range(KD):
                        m = pe.matmul(psum[:, b, :], bc_w[:, k, n * P:(n + 1) * P], fT[:, k, :], **first_and_last(k, KD))
                    m.then_inc(bank_full[b], 1)

                def spread_sums(j):
                    pe.wait_ge(sig("row_ready"), g * S_HPG + (j + 1))
                    b = claim("ssd", ("acs", j), g)
                    pe.matmul(psum[:, b, :], con[0:S_HEADS, C_ONE:C_ONE + P], rows[0:S_HEADS, j % 2, :],
                              start=True, stop=True).then_inc(bank_full[b], 1)

                def x_block(mm_):
                    b = claim("ssd", ("x", mm_), g)
                    for k in range(KD):
                        m = pe.matmul(psum[:, b, :], wx[:, k, mm_ * P:(mm_ + 1) * P], fT[:, k, :], **first_and_last(k, KD))
                        if mm_ == 0 and k == 0:
                            m.then_inc(units_begun, 1)
                    m.then_inc(bank_full[b], 1)

                def x_turn(mm_):
                    pe.wait_ge(sig("conv_silu"), g * 6 + (3 + mm_))
                    b = claim("ssd", ("xt", mm_), g)
                    for t in range(NT):
                        m = turn(b, t * P, cv[:, (mm_ + 2) % 3, t * P:(t + 1) * P])
                    m.then_inc(bank_full[b], 1)

                def z_tile(t):
                    b = claim("ssd", ("z", t), g)
                    for k in range(KD):
                        m = pe.matmul(psum[:, b, :], fT[:, k, t * P:(t + 1) * P], wz[:, k, :], **first_and_last(k, KD))
                        if t == 0 and k == 0:
                            m.then_inc(units_begun, 1)
                    m.then_inc(bank_full[b], 1)

                for j in range(4):
                    spread_sums(j)
                pe.wait_ge(units_landed[0], LAND + g * LAND)
                x_block(0)
                for j in range(4, S_HPG):
                    spread_sums(j)
                x_block(1)
                x_turn(0)
                x_block(2)
                b = claim("ssd", "CB", g)
                for t in range(NT):
                    m = pe.matmul(psum[:, b, t * P:(t + 1) * P], BT[:, t * P:(t + 1) * P], CT[:, t * P:(t + 1) * P],
                                  start=True, stop=True)
                m.then_inc(bank_full[b], 1)
                b = claim("ssd", "BT", g)
                for t in range(NT):
                    m = turn(b, t * P, BT[:, t * P:(t + 1) * P])
                m.then_inc(bank_full[b], 1)
                x_turn(1)
                x_block(3)
                x_turn(2)
                pe.wait_ge(units_landed[1], LAND + g * LAND)
                z_tile(0)
                x_turn(3)
                for t in range(1, NT):
                    z_tile(t)
                wait_taken(pe, "ssd", "BT", g)
                for c in range(NT - 1):
                    if c == 0:
                        pe.wait_ge(sig("xw_ready"), g * 4 + 4)
                    b = claim("ssd", ("st", c), g)
                    pe.matmul(psum[:, b, :], Btok[:, c, :], xw[:, c, :], start=True, stop=True).then_inc(bank_full[b], 1)

                def y_in(c):
                    b = claim("ssd", ("yd", c), g)
                    for j in range(S_HPG):
                        m = pe.matmul(psum[:, b, j * S_P:(j + 1) * S_P], Mh[:, j, c * P:(c + 1) * P],
                                      xdt[:, c, j * S_P:(j + 1) * S_P], start=True, stop=True)
                    m.then_inc(bank_full[b], 1)

                def y_before(c):
                    wait_taken(pe, "ssd", ("st", c - 1), g)
                    b = claim("ssd", ("yo", c), g)
                    pe.matmul(psum[:, b, :], CT[:, c * P:(c + 1) * P], prev[:, c - 1, :],
                              start=True, stop=True).then_inc(bank_full[b], 1)

                pe.wait_ge(sig("M_ready"), g * S_HPG + S_HPG)
                pe.wait_ge(sig("xdt_ready"), g * 4 + 4)
                y_in(0)
                for c in range(1, NT):
                    y_in(c)
                    y_before(c)

            for t in range(NT):
                pe.wait_ge(sig("y_normed"), t + 1)
                for g in range(S_GROUPS):
                    b = claim("yT", (t, g))
                    for c in range(4):
                        m = turn(b, c * P, ys[t][:, (4 * g + c) * P:(4 * g + c + 1) * P])
                    m.then_inc(bank_full[b], 1)
            for t in range(NT):
                for g in range(S_GROUPS):
                    wait_taken(pe, "yT", (t, g))

            def times_out(stage, left, n_units_, h, static=False):
                for n in range(n_units_):
                    last = n == n_units_ - 1
                    landed(pe, stage, h * n_units_ + n)
                    w = as_k(slot_of(stage, h * n_units_ + n))

                    def tile(t, n=n, last=last, w=w):
                        b = t if n else claim(stage, t, h)
                        for k in range(KD):
                            m = pe.matmul(psum[:, b, :], left(n * KD + k, t), w[:, k, :],
                                          start=(n == 0 and k == 0), stop=(last and k == KD - 1))
                            if t == 0 and k == 0:
                                m.then_inc(units_begun, 1)
                        if last:
                            m.then_inc(bank_full[b], 1)
                    if last:
                        return tile
                    for t in range(NT):
                        tile(t)

            def out_and_norm(stage, norm, left, n_units_):
                tile = times_out(stage, left, n_units_, 0)
                for t in range(NT):
                    tile(t)
                return norm_turns(norm, times_out(stage, left, n_units_, 1))

            last_turn = out_and_norm("ssd_out", "norm00", lambda k, t: yT[t][:, k, :], 2)

            inputs_split = [0]

            def next_input():
                before = NT * inputs_split[0]
                inputs_split[0] += 1
                return lambda n: pe.wait_ge(input_low, before + n)

            def times_parts(stage, n, operands, use, i=0, per=0, cs=range(4), begins=True, ends=True, ready=None,
                            cols=None):
                first = (part0[stage] + n) * KD
                bank = {}
                for k in range(KD):
                    if begins:
                        pe.wait_ge(low_made, first + (k + 1) + i * (per * KD))
                    if ready:
                        ready(k)
                    for c in cs:
                        if k == 0:
                            bank[c] = claim(*use(c)) if cols is None or begins else banks.at(*use(c))[0]
                        still_hi, still_lo, moving_hi, moving_lo = operands(c, k)
                        for n_pass, (a, m_) in enumerate(((still_hi, moving_hi), (still_hi, moving_lo), (still_lo, moving_hi))):
                            m = pe.matmul(psum[:, bank[c], cols or slice(0, HALF)], a, m_, start=k == 0 and n_pass == 0,
                                          stop=k == KD - 1 and n_pass == 2)
                            if c == cs[0] and n_pass == 0 and (begins if k == 0 else ends):
                                m.then_inc(blocks_begun, 1)
                            if c == cs[0] and n_pass == 1 and k == 0 and begins:
                                m.then_inc(units_begun, 1)
                        if k == KD - 1 and (cols is None or ends):
                            m.then_inc(bank_full[bank[c]], 1)

            def mlp(i, last_turn):
                stage = f"mlp{i}"
                input_ready = next_input()

                def up(n, q, cols=None, **part):
                    tokens = cols or slice(0, T)
                    times_parts(stage, n, lambda c, k: (w_hi[:, k, c * P:(c + 1) * P], w_lo[:, k, c * P:(c + 1) * P],
                                                        f_hi[:, k, tokens], f_lo[:, k, tokens]),
                                lambda c: (stage, (MLP_UNITS[n], c), q), q, 4, cols=cols, **part)

                def down(h, q, **results):
                    times_parts(stage, 2 + h, lambda t, k: (hid_hi[:, k, t * P:(t + 1) * P], hid_lo[:, k, t * P:(t + 1) * P],
                                                            w_hi[:, k, :], w_lo[:, k, :]),
                                lambda t: (stage, (MLP_UNITS[2 + h], t), q), q, 4,
                                ready=None if h else lambda k: pe.wait_ge(sig("hidden_low"), (KF * i + k + 1) + q * KD), **results)

                input_ready(2)
                up(0, 0, slice(0, T // 2), ends=False)
                last_turn()
                input_ready(NT)
                up(0, 0, slice(T // 2, T), begins=False)
                with pe.Fori(0, QUARTERS - 1) as q:
                    up(1, q)
                    for h in range(NHALF):
                        down(h, q)
                    up(0, q + 1)
                q = QUARTERS - 1
                up(1, q)
                down(0, q)
                return norm_turns(f"norm{i}1", lambda t: down(1, q, cs=(t,), begins=t == 0, ends=t == NT - 1))

            def ple(i, last_turn):
                input_ready = next_input()

                def gate_results(h, **results):
                    times_parts(f"gate{i}", h, lambda t, k: (f_hi[:, k, t * P:(t + 1) * P], f_lo[:, k, t * P:(t + 1) * P],
                                                             w_hi[:, k, :], w_lo[:, k, :]),
                                lambda t: (f"gate{i}", (h, t)), **results)

                for t in range(NT):
                    input_ready(t + 1)
                    gate_results(0, cs=(t,), begins=t == 0, ends=t == NT - 1)
                    if t == 0:
                        last_turn()
                gate_results(1)
                landed(pe, f"proj{i}")
                w = slot_of(f"proj{i}")[:, 0:KP * D].rearrange("p (k n) -> p k n", k=KP)
                for t in range(NT):
                    for h in range(NHALF):
                        b = claim(f"proj{i}", (h, t))
                        for k in range(KP):
                            m = pe.matmul(psum[:, b, :], pT[:, i, k, t * P:(t + 1) * P], w[:, k, h * HALF:(h + 1) * HALF],
                                          **first_and_last(k, KP))
                            if t == 0 and h == 0 and k == 0:
                                m.then_inc(units_begun, 1)
                        m.then_inc(bank_full[b], 1)

            ple(0, mlp(0, last_turn))
            for t in range(NT):
                turn_rows("turn0", res, t, sig("ple_done0"), t + 1)
            next_input()(NT)

            def hgrn_project(par, i, n):
                h = 2 * i + par
                if n < 3:
                    pe.wait_ge(sig("cols_low"), h * 3 + (n + 1))

                def passes(out, hi_lo, k):
                    (still_hi, still_lo), (moving_hi, moving_lo) = hi_lo
                    for n_pass, (a, m_) in enumerate(((still_hi, moving_hi), (still_hi, moving_lo), (still_lo, moving_hi))):
                        m = pe.matmul(out, a, m_, start=k == 0 and n_pass == 0, stop=k == KD - 1 and n_pass == 2)
                        if n == 0 and k == 0 and n_pass == 0:
                            m.then_inc(units_begun, 1)
                    return m

                if n < 2:
                    b = claim("hgrn", "qf"[n], h)
                    cols = slice(n * P, (n + 1) * P)
                    for k in range(KD):
                        m = passes(psum[:, b, :], ((w_hi[:, k, cols], w_lo[:, k, cols]), (f_hi[:, k, :], f_lo[:, k, :])), k)
                    m.then_inc(bank_full[b], 1)
                else:
                    b = claim("hgrn", f"vg{n - 2}", h)
                    cols = slice(2 * P, 4 * P)
                    for tt in range(2):
                        tokens = slice((2 * (n - 2) + tt) * P, (2 * (n - 2) + tt + 1) * P)
                        for k in range(KD):
                            m = passes(psum[:, b, tt * 256:(tt + 1) * 256],
                                       ((f_hi[:, k, tokens], f_lo[:, k, tokens]), (w_hi[:, k, cols], w_lo[:, k, cols])), k)
                    m.then_inc(bank_full[b], 1)

            def hgrn_level(par, i, n):
                h = 2 * i + par
                if n < LEVELS:
                    pe.wait_ge(sig("level_ready"), h * LEVELS + (n + 1))
                else:
                    pe.wait_ge(sig("k_ready"), h + 1)
                b = claim("hgrn", ("lev", n), h)
                for c in range(NT):
                    if n < LEVELS:
                        a = lev[:, n % 2, c * P:(c + 1) * P]
                        m = pe.matmul(psum[:, b, c * P:(c + 1) * P], a, a, start=True, stop=True)
                    else:
                        m = pe.matmul(psum[:, b, c * P:(c + 1) * P], f_k[:, par, c * P:(c + 1) * P],
                                      f_q[:, par, c * P:(c + 1) * P], start=True, stop=True)
                m.then_inc(bank_full[b], 1)

            def hgrn_turn(h):
                wait_taken(pe, "hgrn", "o", h)
                b = claim("hgrn", "ot", h)
                for c in range(NT):
                    m = turn(b, c * P, o_s[:, c, :])
                m.then_inc(bank_full[b], 1)

            def hgrn_core(par, i, first=False, last=False):
                h = 2 * i + par
                nxt = (1 - par, i + par)

                def fill(n):
                    if not last:
                        hgrn_project(*nxt, n)

                fill(0)
                fill(1)
                hgrn_level(par, i, 2)
                hgrn_level(par, i, 3)
                if not first:
                    hgrn_turn(h - 1)
                fill(2)
                hgrn_level(par, i, 4)
                pe.wait_ge(sig("kend_ready"), h + 1)
                b = claim("hgrn", "kt", h)
                for c in range(NT):
                    m = turn(b, c * P, kend[:, c * P:(c + 1) * P])
                m.then_inc(bank_full[b], 1)
                hgrn_level(par, i, 5)
                fill(3)
                hgrn_level(par, i, 6)
                hgrn_level(par, i, LEVELS)
                wait_taken(pe, "hgrn", "kt", h)

                def to_state(c):
                    b = claim("hgrn", ("st", c), h)
                    pe.matmul(psum[:, b, 0:P], ktok[:, c, :], f_v[:, par, c, :],
                              start=True, stop=True).then_inc(bank_full[b], 1)
                to_state(0)
                to_state(1)
                if not last:
                    hgrn_level(*nxt, 0)
                to_state(2)
                if not last:
                    hgrn_level(*nxt, 1)
                wait_taken(pe, "hgrn", ("lev", LEVELS), h)
                wait_taken(pe, "hgrn", ("st", NT - 2), h)
                wait_taken(pe, "hgrn", "vg1", h)
                b = claim("hgrn", "o", h)
                for c in range(NT):
                    m = pe.matmul(psum[:, b, c * P:(c + 1) * P], scT[:, par, c * P:(c + 1) * P], f_v[:, par, c, :],
                                  start=True, stop=(c == 0))
                    if c:
                        m = pe.matmul(psum[:, b, c * P:(c + 1) * P], qe[:, c * P:(c + 1) * P], state[:, c - 1, :],
                                      start=False, stop=True)
                m.then_inc(bank_full[b], 1)

            for n in range(4):
                hgrn_project(0, 0, n)
            hgrn_level(0, 0, 0)
            hgrn_level(0, 0, 1)
            hgrn_core(0, 0, first=True)
            with pe.Fori(0, 2) as i:
                hgrn_core(1, i)
                hgrn_core(0, i + 1)
            hgrn_core(1, 2)
            hgrn_core(0, 3)
            hgrn_core(1, 3, last=True)
            hgrn_turn(H_HEADS - 1)

            def hgrn_out(h, **results):
                times_parts("hgrn_out", h, lambda t, k: (o_hi[:, k, t * P:(t + 1) * P], o_lo[:, k, t * P:(t + 1) * P],
                                                         w_hi[:, k, :], w_lo[:, k, :]),
                            lambda t: ("hgrn_out", (h, t)), ready=None if h else lambda k: pe.wait_ge(sig("o_low"), k + 1), **results)
            hgrn_out(0)
            last_turn = norm_turns("norm10", lambda t: hgrn_out(1, cs=(t,), begins=t == 0, ends=t == NT - 1))
            ple(1, mlp(1, last_turn))

            for m_ in range(MT):
                pe.wait_ge(sig("mem_normed"), m_ + 1)
                for h in range(2):
                    b = claim("memT", (m_, h))
                    for c in range(4):
                        m = turn(b, c * P, mem_tok[:, m_, (4 * h + c) * P:(4 * h + c + 1) * P])
                    m.then_inc(bank_full[b], 1)
            for m_ in range(MT):
                for h in range(2):
                    wait_taken(pe, "memT", (m_, h))
            landed(pe, "mem")
            w = as_k(slot_of("mem"))
            for c in range(2):
                b = claim("memkv", ("k", c))
                for k in range(KD):
                    m = pe.matmul(psum[:, b, 0:NMEM], w[:, k, c * P:(c + 1) * P], memT[:, k, :], **first_and_last(k, KD))
                    if c == 0 and k == 0:
                        m.then_inc(units_begun, 1)
                m.then_inc(bank_full[b], 1)
            for m_ in range(MT):
                b = claim("memkv", ("v", m_))
                for k in range(KD):
                    m = pe.matmul(psum[:, b, 0:MEM_W], memT[:, k, m_ * P:(m_ + 1) * P], w[:, k, MEM_W:2 * MEM_W],
                                  **first_and_last(k, KD))
                m.then_inc(bank_full[b], 1)
            norm_turns("norm_mla", None)()
            wait_features("norm_mla")

            def by_tokens(stage, unit, cols, n=0, name=lambda t: t):
                landed(pe, unit, n)
                w = slot_of(unit, n)[:, 0:KD * cols].rearrange("p (k n) -> p k n", k=KD)
                for t in range(NT):
                    b = claim(stage, name(t))
                    for k in range(KD):
                        m = pe.matmul(psum[:, b, 0:cols], fT[:, k, t * P:(t + 1) * P], w[:, k, :], **first_and_last(k, KD))
                        if t == 0 and k == 0:
                            m.then_inc(units_begun, 1)
                    m.then_inc(bank_full[b], 1)

            by_tokens("cq", "cq", Q_LORA)
            by_tokens("ckv", "ckv", KV_LORA + ROPE)
            landed(pe, "qm")
            w = slot_of("qm")[:, 0:KD * MEM_W].rearrange("p (k n) -> p k n", k=KD)
            for c in range(2):
                b = claim("qm", c)
                for k in range(KD):
                    m = pe.matmul(psum[:, b, :], w[:, k, c * P:(c + 1) * P], fT[:, k, :], **first_and_last(k, KD))
                    if c == 0 and k == 0:
                        m.then_inc(units_begun, 1)
                m.then_inc(bank_full[b], 1)
            for h in range(NHALF):
                by_tokens("mgate", "mgate", HALF, h, lambda t: (h, t))
            for name, src, nk in (("q", cq_n, KQ), ("kv", ckv_n, KKV)):
                for t in range(NT):
                    wait_taken(pe, f"c{name}", t)
                    b = claim("lora", (name, t))
                    for c in range(nk):
                        m = turn(b, c * P, src[:, t, c * P:(c + 1) * P])
                    m.then_inc(bank_full[b], 1)
            for stage, left, nk, cols in (("uq", cqT, KQ, Q_LORA), ("ukv", ckvT, KKV, HALF)):
                for t in range(NT):
                    wait_taken(pe, "lora", (stage[1:], t))
                landed(pe, stage)
                w = slot_of(stage)[:, 0:nk * 3 * cols].rearrange("p (k n) -> p k n", k=nk)
                for n in range(3):
                    for t in range(NT):
                        b = claim(stage, (n, t))
                        for k in range(nk):
                            m = pe.matmul(psum[:, b, 0:cols], left[:, k, t * P:(t + 1) * P],
                                          w[:, k, n * cols:(n + 1) * cols], **first_and_last(k, nk))
                            if n == 0 and t == 0 and k == 0:
                                m.then_inc(units_begun, 1)
                        m.then_inc(bank_full[b], 1)

            def mem_scores(h, t, b):
                r0 = M_HEAD * (h % 2)
                return pe.matmul(psum[:, b, 0:NMEM], qmT[r0:r0 + M_HEAD, h // 2, t * P:(t + 1) * P],
                                 kmT[r0:r0 + M_HEAD, h // 2, :], start=True, stop=True)

            def main_scores(par, t, b):
                return pe.matmul(psum[:, b, :], qhT[0:QK, par, t * P:(t + 1) * P], khT[0:QK, par, :], start=True, stop=True)

            def turn_head(stage, name, i, par, nth):
                pe.wait_ge(sig("head_rows"), nth + 1)
                for src, n in ((hq, "qt"), (hk, "kt")):
                    b = claim(stage, name(n), i)
                    for t in range(NT):
                        m = turn(b, t * P, src[:, par, t, :], P, QK)
                    m.then_inc(bank_full[b], 1)

            def weigh(stage, name, i, nk, values, next_scores=None, turn_next=None, before=None):
                for t in range(NT + 1):
                    if t < NT:
                        if next_scores:
                            bs = claim(stage, name("next_s", t), i)
                        else:
                            wait_taken(pe, before, ("next_s", t))
                        b = claim(stage, name("pt", t), i)
                        for c in range(nk):
                            m = turn(b, c * P, prob[:, t % 2, c * P:(c + 1) * P])
                        m.then_inc(bank_full[b], 1)
                        if t == 0 and turn_next:
                            turn_next()
                        if next_scores:
                            next_scores(t, bs).then_inc(bank_full[bs], 1)
                    if t > 0:
                        wait_taken(pe, stage, name("pt", t - 1), i)
                        b = claim(stage, name("o"), i) if t == 1 else banks.at(stage, name("o"))[0]
                        for c in range(nk):
                            m = pe.matmul(psum[:, b, (t - 1) * V_HEAD:t * V_HEAD], probT[:, (t - 1) % 2, c * P:(c + 1) * P],
                                          values(c), **first_and_last(c, nk))
                        m.then_inc(sig("tile_weighed") if t < NT else bank_full[b], 1)

            for c in range(2):
                wait_taken(pe, "memkv", ("k", c))
                wait_taken(pe, "memkv", ("v", c))
                wait_taken(pe, "qm", c)
            for t in range(NT):
                b = claim("first_scores", ("next_s", t))
                mem_scores(0, t, b).then_inc(bank_full[b], 1)
            for h in range(M_HEADS):
                stage = f"mem{h}"
                weigh(stage, lambda *n: n, 0, MT, lambda c: v_mem[:, c, h * M_HEAD:(h + 1) * M_HEAD],
                      (lambda t, b: mem_scores(h + 1, t, b)) if h + 1 < M_HEADS else (lambda t, b: main_scores(0, t, b)),
                      (lambda: turn_head(stage, lambda n: (n,), 0, h - 2, h - 2)) if h >= 2 else None)
            with pe.Fori(0, A_HEADS // 2 - 1) as i:
                for par in range(2):
                    h = 2 * i + par
                    weigh("heads", lambda *n: (par,) + n, i, NT, lambda c: v_tok[:, c, ds(h * V_HEAD, V_HEAD)],
                          lambda t, b: main_scores(1 - par, t, b),
                          lambda: turn_head("heads", lambda n: (par, n), i, par, h + 2))
            for n in ("qt", "kt"):
                wait_taken(pe, "heads", (1, n), A_HEADS // 2 - 2)
            for par in range(2):
                h = A_HEADS - 2 + par
                weigh(f"last_head{par}", lambda *n: n, 0, NT, lambda c: v_tok[:, c, h * V_HEAD:(h + 1) * V_HEAD],
                      None if par else lambda t, b: main_scores(1, t, b), before="last_head0")
            for t in range(NT):
                turn_rows("branchT", branch, t, sig("branch_gated"), M_HEADS + A_HEADS)
            wait_features("branchT")
            for h in range(NHALF):
                tile = times_out("mla_out", lambda k, t: fT[:, k, t * P:(t + 1) * P], 1, h)
                for t in range(NT):
                    tile(t)

        @block.scalar
        def _(act):
            def full(stage, name, i=0):
                return wait_full(act, stage, name, i)

            def turned_out(stage, t, gain=None, bias=None, name=lambda t, h: (t, h), half=0):
                b = full(stage, name(t, half))
                if gain is None:
                    act.copy(fT[:, 0:4, t * P:(t + 1) * P], by_block(psum[:, b, :])).then_inc(bank_free[b], 1)
                    return
                for c in range(4):
                    k = 4 * half + c
                    src, dst, g = psum[:, b, c * P:(c + 1) * P], fT[:, k, t * P:(t + 1) * P], col_b[:, gain + k:gain + k + 1]
                    if bias is None:
                        m = act.mul(dst, src, g)
                    else:
                        m = act.activation(dst, src, ACT.Identity, scale=g, bias=col_b[:, bias + k:bias + k + 1])
                m.then_inc(bank_free[b], 1)

            for t in range(NT):
                turned_out("start", t, name=lambda t, h: ("x", t, h))
            wait_taken(act, "start", "par")
            wait_taken(act, "start", "par_b")

            wait_taken(act, "dt", "dt")
            act.activation(sp2, sp1, ACT.Abs)
            act.drain()
            act.activation(sp2, sp2, ACT.Exp, scale=-1.0)
            act.drain()
            act.activation(sp2, sp2, ACT.Ln, bias=1.0)
            act.wait_ge(ssd_small_in, 64)
            act.activation(aneg, aneg, ACT.Exp).then_inc(sig("softplus_ln"), 1)
            act.wait_ge(sig("sums_ready"), 1)
            act.activation(decay_end, decay_end, ACT.Exp)
            act.activation(ecs, acs, ACT.Exp)
            act.activation(edec, tot, ACT.Exp).then_inc(sig("decays"), 1)

            with act.Fori(0, S_GROUPS) as g:
                def row(j):
                    if j >= 2:
                        full("ssd", ("acs", j - 2), g)
                    act.mul(rows[0:S_HEADS, j % 2, :], acsT[0:S_HEADS, :], con[0:S_HEADS, ds(g * S_HPG + (C_ID + j), 1)])\
                        .then_inc(sig("row_ready"), 1)

                def conv_start(n, name, blk):
                    act.drain()
                    b = full("ssd", name, g)
                    act.activation(cv[:, n % 3, :], psum[:, b, :], ACT.Identity, scale=col_a[:, ds(blk + (A_CW + 3 * CONV_BLOCKS), 1)],
                                   bias=col_a[:, ds(blk + A_CB, 1)]).then_inc(sig("conv_begun"), 1)

                def silu(n, name, dst):
                    wait_taken(act, "ssd", name, g)
                    act.activation(dst, cv[:, n % 3, :], ACT.Silu).then_inc(sig("conv_silu"), 1)

                def exp_diff(j):
                    act.wait_ge(sig("diff_ready"), g * S_HPG + (j + 1))
                    act.activation(Mh[:, j, :], Mh[:, j, :], ACT.Exp).then_inc(sig("exp_ready"), 1)

                def x_out(m):
                    b = full("ssd", ("xt", m), g)
                    act.copy(xr[:, :, m * P:(m + 1) * P], by_block(psum[:, b, :])).then_inc(bank_free[b], 1)

                row(0)
                row(1)
                conv_start(0, "B", g + 16)
                conv_start(1, "C", g + 20)
                row(2)
                row(3)
                silu(0, "B", BT)
                silu(1, "C", CT)
                row(4)
                row(5)
                conv_start(2, ("x", 0), 4 * g)
                row(6)
                row(7)
                silu(2, ("x", 0), cv[:, 2, :])
                for j in range(4):
                    exp_diff(j)
                conv_start(3, ("x", 1), 4 * g + 1)
                for j in range(4, S_HPG):
                    exp_diff(j)
                silu(3, ("x", 1), cv[:, 0, :])
                x_out(0)
                conv_start(4, ("x", 2), 4 * g + 2)
                silu(4, ("x", 2), cv[:, 1, :])
                b = full("ssd", "BT", g)
                act.copy(Btok, by_block(psum[:, b, :])).then_inc(bank_free[b], 1)
                x_out(1)
                conv_start(5, ("x", 3), 4 * g + 3)
                silu(5, ("x", 3), cv[:, 2, :])
                x_out(2)
                b = full("ssd", ("z", 0), g)
                act.activation(zs[:, 0, :], psum[:, b, :], ACT.Silu).then_inc(bank_free[b], 1)
                x_out(3)
                for t in range(1, NT):
                    b = full("ssd", ("z", t), g)
                    act.activation(zs[:, t, :], psum[:, b, :], ACT.Silu).then_inc(bank_free[b], 1)
                for c in range(NT):
                    act.wait_ge(sig("y_gated"), g * NT + (c + 1))
                    act.activation(zs[:, c, :], ys[c][:, ds(g * HALF, HALF)], ACT.Square,
                                   accum_out=ssq[:, c, ds(g, 1)]).then_inc(sig("ssq_ready"), 1)
            act.wait_ge(sig("sms_ready"), 1)
            act.activation(srs[:, 1, :], srs[:, 0, :], ACT.Sqrt).then_inc(sig("srs_ready"), 1)
            for t in range(NT):
                for g in (0, 2):
                    b = full("yT", (t, g))
                    for c in range(4):
                        k = 4 * g + c
                        m = act.mul(yT[t][:, k, :], psum[:, b, c * P:(c + 1) * P], col_b[:, B_SN + k:B_SN + k + 1])
                    m.then_inc(bank_free[b], 1)

            norms = [0]

            def split_high(stage, n=0, i=0, per=0, follows=True):
                landed(act, stage, n, i, per)
                u = part0[stage] + n
                for k in range(KD):
                    if follows:
                        act.wait_ge(blocks_begun, (u - 1) * KD + (k + 2) + i * (per * KD))
                    act.copy(w_hi[:, k, :], as_k(slot_of(stage, n))[:, k, :]).then_inc(high_made, 1)

            def input_parts(stage, t):
                for h in range(2):
                    wait_taken(act, stage, (t, h))
                tokens = slice(t * P, (t + 1) * P)
                act.copy(f_hi[:, :, tokens], fT[:, :, tokens]).then_inc(input_high, 1)

            def norm(stage=None, gain=None, bias=None, parts=False, meanwhile=None, before_last=None):
                n = norms[0]
                norms[0] += 1
                for t in range(NT + 1):
                    if t == NT - 1 and before_last:
                        before_last()
                    if t < NT:
                        act.wait_ge(var_ready, NT * n + t + 1)
                        act.activation(ms[:, t, 1:2], ms[:, t, 0:1], ACT.Sqrt).then_inc(root_ready, 1)
                    if t > 0 and stage:
                        turned_out(stage, t - 1, gain, bias)
                        if parts:
                            turned_out(stage, t - 1, gain, bias, half=1)
                            input_parts(stage, t - 1)
                    if t == 1 and meanwhile:
                        meanwhile()

            def mlp(i):
                stage = f"mlp{i}"

                def quarter(q, last=False):
                    for n in range(2):
                        done = KF * i + 4 * n

                        def relu(c):
                            if c == 3 or c == 0 and n == 1:
                                act.wait_ge(sig("hidden_low"), done + (1 if c else 0) + q * KD)
                            b = full(stage, (MLP_UNITS[n], c), q)
                            act.activation(sq[:, c % 3, :], psum[:, b, :], ACT.Relu).then_inc(bank_free[b], 1)

                        def high(c):
                            act.wait_ge(sig("squared"), done + (c + 1) + q * KD)
                            act.copy(hid_hi[:, 4 * n + c, :], sq[:, c % 3, :]).then_inc(sig("hidden_high"), 1)

                        for c in range(3):
                            relu(c)
                        high(0)
                        high(1)
                        relu(3)
                        high(2)
                        high(3)
                        split_high(stage, 2 + n, q, 4)
                    if not last:
                        for n in range(2):
                            split_high(stage, 4 + n, q, 4)

                split_high(stage, 1)
                with act.Fori(0, QUARTERS - 1) as q:
                    quarter(q)
                quarter(QUARTERS - 1, last=True)
                norm(f"norm{i}1", B_G + 16 * i + 8, B_B + 16 * i + 8, parts=True, before_last=lambda: split_high(f"gate{i}"))

            def ple(i):
                split_high(f"gate{i}", 1)
                for h in range(NHALF):
                    for t in range(NT):
                        b = full(f"gate{i}", (h, t))
                        act.activation(sg[:, t, h * HALF:(h + 1) * HALF], psum[:, b, :], ACT.Sigmoid).then_inc(bank_free[b], 1)

            norm("norm00", B_G, B_B, parts=True, meanwhile=lambda: split_high("mlp0", follows=False))
            mlp(0)
            ple(0)
            def split_cols_high(par, c):
                cols = slice(c * P, (c + 1 + (c == 2)) * P)
                act.copy(w_hi[:, :, cols], as_k(slot_of("hgrn", par))[:, :, cols]).then_inc(sig("cols_high"), 1)

            for t in range(NT):
                turned_out("turn0", t)
                input_parts("turn0", t)
                if t == 1:
                    landed(act, "hgrn", 0)
                    split_cols_high(0, 0)
            split_cols_high(0, 1)
            split_cols_high(0, 2)

            def gates(par, h):
                b = full("hgrn", "q", h)
                act.copy(f_q[:, par, :], psum[:, b, :]).then_inc(bank_free[b], 1)
                act.drain()
                b = full("hgrn", "f", h)
                act.activation(f_t[:, 0, :], psum[:, b, :], ACT.Abs)
                act.drain()
                act.activation(f_t[:, 0, :], f_t[:, 0, :], ACT.Exp, scale=-1.0)
                act.drain()
                act.activation(f_t[:, 1, :], f_t[:, 0, :], ACT.Ln, bias=1.0).then_inc(sig("ln_ready"), 1)
                wait_taken(act, "hgrn", "f", h)
                act.activation(f_k[:, par, :], f_t[:, 0, :], ACT.Exp).then_inc(sig("k_ready"), 1)

            def values(par, h):
                for n in range(2):
                    b = full("hgrn", f"vg{n}", h)
                    v = psum[:, b, :].rearrange("p (t s l) -> p t s l", t=2, s=2)
                    act.copy(f_v[:, par, 2 * n:2 * n + 2, :], v[:, :, 0, :])
                    act.activation(f_g[:, par, 2 * n:2 * n + 2, :], v[:, :, 1, :], ACT.Silu).then_inc(bank_free[b], 1)

            def ends(par, h):
                b3 = by_block(f_b[:, par, :])
                act.activation(qe, f_b[:, par, :], ACT.Exp)
                for c in range(NT):
                    act.activation(kend[:, c * P:(c + 1) * P], b3[:, c, :], ACT.Exp, scale=-1.0, bias=b3[:, c, P - 1:P])
                act.activation(elast, b3[:, :, P - 1:P].rearrange("p c l -> p (c l)"), ACT.Exp).then_inc(sig("ends_ready"), 1)

            def level_exps(h, n):
                act.wait_ge(sig("dif_ready"), h * LEVELS + (n + 1))
                v = dif[:, n % 2, :].rearrange("p (a s l) -> p a s l", s=2, l=64 >> n)
                act.activation(v[:, :, 0, :], v[:, :, 0, :], ACT.Exp, scale=-1.0)
                act.activation(v[:, :, 1, :], v[:, :, 1, :], ACT.Exp).then_inc(sig("dexp_ready"), 1)

            def out_turned(h):
                b = full("hgrn", "ot", h)
                act.mul(oT[:, ds(h, 1), :].rearrange("p a l -> p (a l)") if not isinstance(h, int) else oT[:, h, :],
                        psum[:, b, :], col_b[:, B_HG:B_HG + 1]).then_inc(bank_free[b], 1)

            def out_root(h):
                b = full("hgrn", "o", h)
                for c in range(NT):
                    act.activation(junk_h[:, c, :], psum[:, b, c * P:(c + 1) * P], ACT.Square, accum_out=hsq[:, 0, c:c + 1])
                act.drain()
                act.activation(hsq[:, 1, :], hsq[:, 0, :], ACT.Sqrt, scale=1.0 / P, bias=eps_h[:, 0:1]).then_inc(sig("oroot_ready"), 1)

            def next_cols(par, i, c):
                if c == 0:
                    landed(act, "hgrn", par, i, 2)
                full("hgrn", ("q", "f", "vg1")[c], 2 * i + (par - 1))
                split_cols_high(par, c)

            def hgrn_head(par, i, first=False, splits=True, last=False):
                h = 2 * i + par
                if not first:
                    out_root(h - 1)
                for n in (2, 3):
                    level_exps(h, n)
                if not first and splits is not None:
                    next_cols(1 - par, i + par, 2)
                values(par, h)
                ends(par, h)
                level_exps(h, 4)
                if not first:
                    out_turned(h - 1)
                if not last:
                    gates(1 - par, h + 1)
                for n in (5, 6):
                    level_exps(h, n)
                if not last:
                    act.wait_ge(sig("b_ready"), h + 2)
                    for n in (0, 1):
                        level_exps(h + 1, n)
                if splits:
                    next_cols(par, i + 1, 0)
                    next_cols(par, i + 1, 1)

            act.wait_ge(sig("eps_set"), 1)
            gates(0, 0)
            act.wait_ge(sig("b_ready"), 1)
            for n in (0, 1):
                level_exps(0, n)
            for c in range(3):
                next_cols(1, 0, c)
            hgrn_head(0, 0, first=True)
            with act.Fori(0, 2) as i:
                hgrn_head(1, i)
                hgrn_head(0, i + 1)
            hgrn_head(1, 2)
            hgrn_head(0, 3, splits=False)
            hgrn_head(1, 3, splits=None, last=True)
            split_high("hgrn_out", follows=False)
            for k in range(H_HEADS):
                if k == H_HEADS - 1:
                    out_root(k)
                    out_turned(k)
                wait_taken(act, "hgrn", "ot", k)
                act.copy(o_hi[:, k, :], oT[:, k, :]).then_inc(sig("o_high"), 1)
            split_high("hgrn_out", 1)
            norm("norm10", B_G + 16, B_B + 16, parts=True, before_last=lambda: split_high("mlp1"))
            mlp(1)
            ple(1)

            for m_ in range(MT):
                act.wait_ge(sig("mem_ms"), m_ + 1)
                act.activation(ms[:, m_, 1:2], ms[:, m_, 0:1], ACT.Sqrt).then_inc(sig("mem_root"), 1)
            for m_ in range(MT):
                b = full("memT", (m_, 0))
                for c in range(4):
                    m = act.mul(memT[:, c, m_ * P:(m_ + 1) * P], psum[:, b, c * P:(c + 1) * P], col_b[:, B_MG + c:B_MG + c + 1])
                m.then_inc(bank_free[b], 1)
            for c in range(2):
                b = full("memkv", ("k", c))
                act.copy(kmT[:, c, :], psum[:, b, 0:NMEM]).then_inc(bank_free[b], 1)
            for m_ in range(MT):
                b = full("memkv", ("v", m_))
                act.copy(v_mem[:, m_, :], psum[:, b, 0:MEM_W]).then_inc(bank_free[b], 1)
            norm("norm_mla", B_NG)
            act.wait_ge(sig("angles_ready"), 1)
            act.activation(sinn, sinn, ACT.Sin)
            act.activation(cosn, cosn, ACT.Sin).then_inc(sig("trig_ready"), 1)
            for name, s in (("cq", 0), ("ckv", 1)):
                for t in range(NT):
                    act.wait_ge(sig(f"{name}_ms"), t + 1)
                    act.activation(rstat[:, s, t, 9:10], rstat[:, s, t, 8:9], ACT.Sqrt).then_inc(sig(f"{name}_root"), 1)
            for c in range(2):
                b = full("qm", c)
                act.copy(qmT[:, c, :], psum[:, b, :]).then_inc(bank_free[b], 1)
            for h in range(NHALF):
                for t in range(NT):
                    b = full("mgate", (h, t))
                    act.activation(gate[:, t, h * HALF:(h + 1) * HALF], psum[:, b, :], ACT.Silu).then_inc(bank_free[b], 1)
            for t in range(NT):
                b = full("lora", ("kv", t))
                for c in range(KKV):
                    m = act.mul(ckvT[:, c, t * P:(t + 1) * P], psum[:, b, c * P:(c + 1) * P], col_b[:, B_KG + c:B_KG + c + 1])
                m.then_inc(bank_free[b], 1)
            for n in range(3):
                for t in range(NT):
                    b = full("uq", (n, t))
                    act.copy(q_tok[:, t, n * Q_LORA:(n + 1) * Q_LORA], psum[:, b, 0:Q_LORA]).then_inc(bank_free[b], 1)

            def exp(nth, par, t, width, scale):
                act.wait_ge(sig("max_ready"), nth * NT + (t + 1))
                act.activation(prob[:, t % 2, 0:width], psum[:, t, 0:width], ACT.Exp, scale=scale,
                               bias=smx[:, par, 1, t:t + 1], accum_out=smx[:, par, 2, t:t + 1]).then_inc(bank_free[t], 1)

            def softmax(stage, name, i, nth, par, this, nxt, turns):
                def prob_turned(t):
                    b = full(stage, name("pt", t), i)
                    if t == 1:
                        wait_filled_before(act, stage, name("o"), i)
                    else:
                        act.wait_ge(sig("tile_weighed"), nth * (NT - 1) + (t - 1))
                    act.copy(probT[:, t % 2, 0:this[0]], psum[:, b, 0:this[0]]).then_inc(bank_free[b], 1)

                full(stage, name("pt", 0), i)
                exp(nth, par, 2, *this)
                if turns:
                    b = full(stage, name("kt"), i)
                    act.copy(khT[0:QK, par, :], psum[0:QK, b, :]).then_inc(bank_free[b], 1)
                prob_turned(1)
                exp(nth, par, 3, *this)
                if nxt:
                    full(stage, name("pt", 2), i)
                    exp(nth + 1, 1 - par, 0, *nxt)
                prob_turned(3)
                if nxt:
                    exp(nth + 1, 1 - par, 1, *nxt)

            of_mem, of_main = (NMEM, M_SCALE), (T, A_SCALE)
            exp(0, 0, 0, *of_mem)
            exp(0, 0, 1, *of_mem)
            for h in range(M_HEADS):
                softmax(f"mem{h}", lambda *n: n, 0, h, h % 2, of_mem, of_mem if h + 1 < M_HEADS else of_main, h >= 2)
            with act.Fori(0, A_HEADS // 2 - 1) as i:
                for par in range(2):
                    softmax("heads", lambda *n, par=par: (par,) + n, i, 2 * i + (par + M_HEADS), par, of_main, of_main, True)
            for par in range(2):
                softmax(f"last_head{par}", lambda *n: n, 0, M_HEADS + A_HEADS - 2 + par, par, of_main,
                        None if par else of_main, False)
            for t in range(NT):
                turned_out("branchT", t)
            norm()

        @block.vector
        def _(dve):
            def full(stage, name, i=0):
                return wait_full(dve, stage, name, i)

            def turned_out(stage, t, gain=None, bias=None, name=lambda t, h: (t, h)):
                b = full(stage, name(t, 1))
                if gain is None:
                    dve.tensor_copy(fT[:, 4:8, t * P:(t + 1) * P], by_block(psum[:, b, :])).then_inc(bank_free[b], 1)
                    return
                for c in range(4, 8):
                    src, dst = psum[:, b, (c - 4) * P:(c - 3) * P], fT[:, c, t * P:(t + 1) * P]
                    m = dve.tensor_scalar(dst, src, col_b[:, gain + c:gain + c + 1],
                                          0.0 if bias is None else col_b[:, bias + c:bias + c + 1], ALU.mult, ALU.add)
                m.then_inc(bank_free[b], 1)

            dve.memset(eps_h[:], RMS_EPS).then_inc(sig("eps_set"), 1)
            for t in range(NT):
                turned_out("start", t, name=lambda t, h: ("x", t, h))
            b = full("start", "par")
            dve.tensor_copy(col_a[:], psum[:, b, 0:A_ROWS]).then_inc(bank_free[b], 1)
            b = full("start", "par_b")
            dve.tensor_copy(col_b[:], psum[:, b, 0:B_ROWS]).then_inc(bank_free[b], 1)
            for i in range(DEPTH):
                for k in range(KP):
                    b = full("start", ("p", i, k))
                    dve.tensor_copy(pT[:, i, k, :], psum[:, b, :]).then_inc(bank_free[b], 1)

            def heads_on_all(v):
                return v.unsqueeze(1).broadcast_to([P, NT, S_HEADS])

            def chunk_heads(b):
                return psum[:, b, 0:NT * S_HEADS].rearrange("p (t h) -> p t h", t=NT)

            dve.wait_ge(ssd_small_in, 64)
            b = full("dt", "dt")
            dve.tensor_tensor(sp1, chunk_heads(b), heads_on_all(dbias), ALU.add).then_inc(bank_free[b], 1)
            dve.wait_ge(sig("softplus_ln"), 1)
            dve.scalar_tensor_tensor(dt_all, sp1, 0.0, sp2, ALU.max, ALU.add)
            dve.tensor_scalar(aneg, aneg, -1.0, None, ALU.mult)
            dve.drain()
            dve.tensor_tensor(da, dt_all, heads_on_all(aneg), ALU.mult).then_inc(sig("da_ready"), 1)
            b = full("dt", "acs")
            dve.tensor_copy(acs, chunk_heads(b)).then_inc(bank_free[b], 1)
            b = full("dt", "tot")
            dve.tensor_copy(tot, chunk_heads(b)).then_inc(bank_free[b], 1)
            b = full("dt", "acsT")
            dve.tensor_copy(acsT[0:S_HEADS, :], psum[0:S_HEADS, b, :]).then_inc(bank_free[b], 1)
            dve.drain()
            dve.tensor_tensor(decay_end, tot, acs, ALU.subtract).then_inc(sig("sums_ready"), 1)

            def by_head(ap, nh):
                return ap.rearrange("p (h d) -> p h d", h=nh)

            with dve.Fori(0, S_GROUPS) as g:
                def taps(n, name, blk):
                    dve.wait_ge(sig("conv_begun"), g * 6 + (n + 1))
                    b = banks.at("ssd", name)[0]
                    for back in range(1, TAPS):
                        m = dve.scalar_tensor_tensor(cv[:, n % 3, back:T], psum[:, b, 0:T - back],
                                                     col_a[:, ds(blk + (A_CW + (3 - back) * CONV_BLOCKS), 1)],
                                                     cv[:, n % 3, back:T], ALU.mult, ALU.add)
                        if back < TAPS - 1:
                            dve.drain()
                    m.then_inc(bank_free[b], 1)

                def diff(j):
                    b = full("ssd", ("acs", j), g)
                    dve.tensor_tensor(by_block(Mh[:, j, :]), by_block(psum[:, b, :]),
                                      acs[:, :, ds(g * S_HPG + j, 1)].broadcast_to([P, NT, P]), ALU.subtract)\
                        .then_inc(bank_free[b], 1)
                    dve.drain()
                    dve.tensor_scalar(Mh[:, j, :], Mh[:, j, :], 0.0, None, ALU.min).then_inc(sig("diff_ready"), 1)

                def weights(j):
                    dve.wait_ge(sig("exp_ready"), g * S_HPG + (j + 1))
                    dve.tensor_tensor(Mh[:, j, :], Mh[:, j, :], CBm[:].rearrange("p t l -> p (t l)"),
                                      ALU.mult).then_inc(sig("M_ready"), 1)

                def x_dt(m):
                    wait_taken(dve, "ssd", ("xt", m), g)
                    dst = xdt[:, :, m * P:(m + 1) * P].rearrange("p t (h d) -> p t h d", h=2)
                    src = xr[:, :, m * P:(m + 1) * P].rearrange("p t (h d) -> p t h d", h=2)
                    dve.tensor_tensor(dst, src, dt_all[:, :, ds(g * S_HPG + 2 * m, 2)].unsqueeze(3)
                                      .broadcast_to([P, NT, 2, S_P]), ALU.mult).then_inc(sig("xdt_ready"), 1)

                taps(0, "B", g + 16)
                taps(1, "C", g + 20)
                for j in range(4):
                    diff(j)
                taps(2, ("x", 0), 4 * g)
                for j in range(4, S_HPG):
                    diff(j)
                taps(3, ("x", 1), 4 * g + 1)
                x_dt(0)
                taps(4, ("x", 2), 4 * g + 2)
                b = full("ssd", "CB", g)
                dve.tensor_tensor(CBm, by_block(psum[:, b, :]), tri.unsqueeze(1).broadcast_to([P, NT, P]), ALU.mult)\
                    .then_inc(bank_free[b], 1)
                dve.drain()
                x_dt(1)
                for j in range(4):
                    weights(j)
                taps(5, ("x", 3), 4 * g + 3)
                x_dt(2)
                for j in range(4, S_HPG):
                    weights(j)
                x_dt(3)
                dve.wait_ge(sig("decays"), 1)
                for c in range(NT - 1):
                    if c:
                        dve.tensor_tensor(by_head(prev[:, c, :], S_HPG), by_head(prev[:, c - 1, :], S_HPG),
                                          edec[:, c, ds(g * S_HPG, S_HPG)].unsqueeze(2).broadcast_to([P, S_HPG, S_P]), ALU.mult)
                        dve.drain()
                    b = full("ssd", ("st", c), g)
                    if c:
                        dve.tensor_tensor(prev[:, c, :], prev[:, c, :], psum[:, b, :], ALU.add).then_inc(bank_free[b], 1)
                    else:
                        dve.tensor_copy(prev[:, c, :], psum[:, b, :]).then_inc(bank_free[b], 1)
                    dve.drain()
                dve.wait_ge(sig("xD_ready"), g * 4 + 4)
                for c in range(NT):
                    if c:
                        dve.drain()
                    b = full("ssd", ("yd", c), g)
                    dve.tensor_tensor(ybuf, psum[:, b, :], xr[:, c, :], ALU.add).then_inc(bank_free[b], 1)
                    if c:
                        b = full("ssd", ("yo", c), g)
                        dve.tensor_tensor(by_head(yoff, S_HPG), by_head(psum[:, b, :], S_HPG),
                                          ecs[:, c, ds(g * S_HPG, S_HPG)].unsqueeze(2).broadcast_to([P, S_HPG, S_P]), ALU.mult)\
                            .then_inc(bank_free[b], 1)
                        dve.drain()
                        dve.tensor_tensor(ybuf, ybuf, yoff, ALU.add)
                    dve.drain()
                    wait_taken(dve, "ssd", ("z", c), g)
                    dve.tensor_tensor(ys[c][:, ds(g * HALF, HALF)], ybuf, zs[:, c, :], ALU.mult).then_inc(sig("y_gated"), 1)
            dve.wait_ge(sig("ssq_ready"), NT * S_GROUPS)
            dve.tensor_scalar(srs[:, 0, :], ssq[:].rearrange("p t g -> p (t g)"), 1.0 / HALF, RMS_EPS, ALU.mult, ALU.add)\
                .then_inc(sig("sms_ready"), 1)
            dve.wait_ge(sig("srs_ready"), 1)
            dve.reciprocal(srs[:, 0, :], srs[:, 1, :])
            dve.drain()

            def y_turned(t):
                for g in (1, 3):
                    b = full("yT", (t, g))
                    for c in range(4):
                        k = 4 * g + c
                        m = dve.tensor_scalar(yT[t][:, k, :], psum[:, b, c * P:(c + 1) * P], col_b[:, B_SN + k:B_SN + k + 1],
                                              None, ALU.mult)
                    m.then_inc(bank_free[b], 1)

            for t in range(NT):
                for g in range(S_GROUPS):
                    n = t * S_GROUPS + g
                    m = dve.tensor_scalar(ys[t][:, g * HALF:(g + 1) * HALF], ys[t][:, g * HALF:(g + 1) * HALF],
                                          srs[:, 0, n:n + 1], None, ALU.mult)
                m.then_inc(sig("y_normed"), 1)
                if t:
                    y_turned(t - 1)
            y_turned(NT - 1)

            norms = [0]

            def stats(src, t, eps, centred):
                for h in range(2):
                    dve.bn_stats(st6[:, t, h, :], src[:, h * HALF:(h + 1) * HALF])
                dve.drain()
                dve.bn_aggr(mv[:, t, :], st6[:, t, :, :].rearrange("p h s -> p (h s)"))
                dve.drain()
                if not centred:
                    dve.scalar_tensor_tensor(mv[:, t, 1:2], mv[:, t, 0:1], mv[:, t, 0:1], mv[:, t, 1:2], ALU.mult, ALU.add)
                    dve.drain()
                return dve.tensor_scalar(ms[:, t, 0:1], mv[:, t, 1:2], eps, None, ALU.add)

            def norm(t, src, dst, eps, centred, gain=None):
                n = NT * norms[0] + t + 1
                stats(src, t, eps, centred).then_inc(var_ready, 1)
                dve.wait_ge(root_ready, n)
                dve.reciprocal(ms[:, t, 2:3], ms[:, t, 1:2])
                dve.drain()
                if centred:
                    return dve.tensor_scalar(dst, src, mv[:, t, 0:1], ms[:, t, 2:3], ALU.subtract, ALU.mult)
                if gain is None:
                    return dve.tensor_scalar(dst, src, ms[:, t, 2:3], None, ALU.mult)
                return dve.scalar_tensor_tensor(dst, src, ms[:, t, 2:3], gain, ALU.mult, ALU.mult)

            inputs_split = [0]

            def split_low(stage, n=0, i=0, per=0):
                first = (part0[stage] + n) * KD
                for k in range(KD):
                    dve.wait_ge(high_made, first + (k + 1) + i * (per * KD))
                    dve.tensor_tensor(w_lo[:, k, :], as_k(slot_of(stage, n))[:, k, :], w_hi[:, k, :].bitcast(F32),
                                      ALU.subtract).then_inc(low_made, 1)

            def input_parts(t):
                dve.wait_ge(input_high, NT * inputs_split[0] + t + 1)
                tokens = slice(t * P, (t + 1) * P)
                dve.tensor_tensor(f_lo[:, :, tokens], fT[:, :, tokens], f_hi[:, :, tokens].bitcast(F32),
                                  ALU.subtract).then_inc(input_low, 1)

            def add_and_norm(add, meanwhile=None, before_last=None):
                for t in range(NT):
                    if t == NT - 1:
                        input_parts(t - 2)
                        if before_last:
                            before_last()
                    add(t)
                    dve.drain()
                    norm(t, rn[:, t, :], rn[:, t, :], LN_EPS, True).then_inc(norm_ready, 1)
                    if 1 < t < NT - 1:
                        input_parts(t - 2)
                    if t == 1 and meanwhile:
                        meanwhile()
                input_parts(NT - 2)
                input_parts(NT - 1)
                norms[0] += 1
                inputs_split[0] += 1

            def mixer_and_norm(out_stage, meanwhile=None, name=lambda h, t: (t, h),
                               before_last=None):
                def add(t, h=1):
                    b = full(out_stage, *name(h, t))
                    cols = slice(h * HALF, (h + 1) * HALF)
                    dve.scalar_tensor_tensor(rn[:, t, cols], res[:, t, cols], ALPHA, psum[:, b, :], ALU.mult, ALU.add)\
                        .then_inc(bank_free[b], 1)

                for t in range(NT):
                    add(t, 0)
                add_and_norm(add, meanwhile, before_last)

            def mlp(i):
                stage = f"mlp{i}"

                def hidden(n, q):
                    def low(c):
                        dve.wait_ge(sig("hidden_high"), (KF * i + 4 * n + c + 1) + q * KD)
                        dve.tensor_tensor(hid_lo[:, 4 * n + c, :], sq[:, c % 3, :], hid_hi[:, 4 * n + c, :].bitcast(F32),
                                          ALU.subtract).then_inc(sig("hidden_low"), 1)
                    for c in range(4):
                        if c == 3:
                            low(0)
                        wait_taken(dve, stage, (MLP_UNITS[n], c), q)
                        a = sq[:, c % 3, :]
                        dve.tensor_tensor(a, a, a, ALU.mult).then_inc(sig("squared"), 1)
                    for c in range(1, 4):
                        low(c)

                def add(t, h, q):
                    b = full(stage, (MLP_UNITS[2 + h], t), q)
                    cols = slice(h * HALF, (h + 1) * HALF)
                    dve.tensor_tensor(rn[:, t, cols], rn[:, t, cols], psum[:, b, :], ALU.add).then_inc(bank_free[b], 1)

                split_low(stage, 1)
                for t in range(NT):
                    dve.wait_ge(res_ready, NT * (2 * i) + t + 1)
                    dve.tensor_scalar(rn[:, t, :], res[:, t, :], ALPHA, None, ALU.mult)
                with dve.Fori(0, QUARTERS - 1) as q:
                    for n in range(2):
                        hidden(n, q)
                        split_low(stage, 2 + n, q, 4)
                    for h in range(NHALF):
                        dve.drain()
                        for t in range(NT):
                            add(t, h, q)
                        split_low(stage, 4 + h, q, 4)
                q = QUARTERS - 1
                for n in range(2):
                    hidden(n, q)
                    split_low(stage, 2 + n, q, 4)
                dve.drain()
                for t in range(NT):
                    add(t, 0, q)
                add_and_norm(lambda t: add(t, 1, q),
                             before_last=lambda: split_low(f"gate{i}"))

            def ple(i):
                split_low(f"gate{i}", 1)
                dve.wait_ge(res_ready, NT * (2 * i + 2))
                for t in range(NT):
                    for h in range(NHALF):
                        cols = slice(h * HALF, (h + 1) * HALF)
                        b = full(f"proj{i}", (h, t))
                        wait_taken(dve, f"gate{i}", (h, t))
                        dve.tensor_tensor(sg[:, t, cols], sg[:, t, cols], psum[:, b, :], ALU.mult).then_inc(bank_free[b], 1)
                    dve.drain()
                    dve.tensor_tensor(res[:, t, :], res[:, t, :], sg[:, t, :], ALU.add).then_inc(sig(f"ple_done{i}"), 1)

            mixer_and_norm("ssd_out", lambda: split_low("mlp0"))
            mlp(0)
            ple(0)
            def split_cols_low(par, h, c):
                dve.wait_ge(sig("cols_high"), h * 3 + (c + 1))
                cols = slice(c * P, (c + 1 + (c == 2)) * P)
                dve.tensor_tensor(w_lo[:, :, cols], as_k(slot_of("hgrn", par))[:, :, cols], w_hi[:, :, cols].bitcast(F32),
                                  ALU.subtract).then_inc(sig("cols_low"), 1)

            for t in range(NT):
                turned_out("turn0", t)
                if t:
                    input_parts(t - 1)
                if t == 2:
                    split_cols_low(0, 0, 0)
            input_parts(NT - 1)
            split_cols_low(0, 0, 1)
            split_cols_low(0, 0, 2)
            inputs_split[0] += 1

            def head_gates(par, h):
                dve.wait_ge(sig("ln_ready"), h + 1)
                b = banks.at("hgrn", "f")[0]
                dve.scalar_tensor_tensor(f_t[:, 1, :], psum[:, b, :], 0.0, f_t[:, 1, :], ALU.min, ALU.subtract)
                dve.drain()
                dve.tensor_tensor(f_t[:, 0, :], f_t[:, 1, :], psum[:, b, :], ALU.subtract).then_inc(bank_free[b], 1)
                for c in range(NT):
                    m = dve.tensor_tensor_scan(f_b[:, par, c * P:(c + 1) * P], ones, f_t[:, 1, c * P:(c + 1) * P], 0.0,
                                               ALU.mult, ALU.add)
                m.then_inc(sig("b_ready"), 1)

            def from_middle(par, h, n):
                half = 64 >> n
                v = dif[:, n % 2, :].rearrange("p (a l) -> p a l", l=2 * half)
                w = f_b[:, par, :].rearrange("p (a l) -> p a l", l=2 * half)
                dve.tensor_tensor(v, w, w[:, :, half - 1:half].broadcast_to([P, T // (2 * half), 2 * half]), ALU.subtract)\
                    .then_inc(sig("dif_ready"), 1)

            def level(par, h, n):
                dve.wait_ge(sig("dexp_ready"), h * LEVELS + (n + 1))

                def halves(ap):
                    return ap.rearrange("p (a s l) -> p a s l", s=2, l=64 >> n)
                e, o = halves(dif[:, n % 2, :]), halves(lev[:, n % 2, :])
                if n == 0:
                    dve.wait_ge(sig("k_ready"), h + 1)
                dve.tensor_tensor(o[:, :, 0, :], e[:, :, 0, :], halves(f_k[:, par, :])[:, :, 0, :], ALU.mult)
                dve.tensor_tensor(o[:, :, 1, :], e[:, :, 1, :], halves(f_q[:, par, :])[:, :, 1, :], ALU.mult)\
                    .then_inc(sig("level_ready"), 1)

            def take(par, h, n):
                b = full("hgrn", ("lev", n), h)
                dve.sem_inc(sig("level_filled"), 1)
                mask = con[:, C_MASK + n * P:C_MASK + (n + 1) * P].bitcast(I32)
                dve.copy_predicated(by_block(scT[:, par, :]), mask.unsqueeze(1).broadcast_to([P, NT, P]),
                                    by_block(psum[:, b, :])).then_inc(bank_free[b], 1)

            def head_out(par, h):
                dve.wait_ge(sig("oroot_ready"), h + 1)
                dve.reciprocal(hsq[:, 0, :], hsq[:, 1, :])
                dve.drain()
                b = banks.at("hgrn", "o")[0]
                for c in range(NT):
                    m = dve.scalar_tensor_tensor(o_s[:, c, :], psum[:, b, c * P:(c + 1) * P], hsq[:, 0, c:c + 1],
                                                 f_g[:, par, c, :], ALU.mult, ALU.mult)
                m.then_inc(bank_free[b], 1)

            def first_levels(par, h):
                for n in (0, 1):
                    level(par, h, n)

            def middle_levels(par, h):
                dve.drain()
                from_middle(par, h, 2)
                from_middle(par, h, 3)
                take(par, h, 0)

            def head_core(par, h, first=False, splits=True, last=False):
                if not first:
                    head_out(1 - par, h - 1)
                    if splits is not None:
                        split_cols_low(1 - par, h + 1, 2)
                for n in range(2, LEVELS):
                    if n == 5 and not last:
                        head_gates(1 - par, h + 1)
                    level(par, h, n)
                    dve.drain()
                    if n + 2 < LEVELS:
                        from_middle(par, h, n + 2)
                    take(par, h, n - 1)
                    if n == 5:
                        b = full("hgrn", "kt", h)
                        dve.tensor_copy(ktok, by_block(psum[:, b, :])).then_inc(bank_free[b], 1)
                if not last:
                    from_middle(1 - par, h + 1, 0)
                    from_middle(1 - par, h + 1, 1)
                dve.drain()
                take(par, h, LEVELS - 1)
                if not last:
                    first_levels(1 - par, h + 1)
                for c in range(NT - 1):
                    b = full("hgrn", ("st", c), h)
                    if c:
                        dve.scalar_tensor_tensor(state[:, c, :], state[:, c - 1, :], elast[:, c:c + 1], psum[:, b, 0:P],
                                                 ALU.mult, ALU.add).then_inc(bank_free[b], 1)
                    else:
                        dve.tensor_copy(state[:, 0, :], psum[:, b, 0:P]).then_inc(bank_free[b], 1)
                    dve.drain()
                take(par, h, LEVELS)
                if not last:
                    middle_levels(1 - par, h + 1)
                if splits:
                    split_cols_low(par, h + 2, 0)
                    split_cols_low(par, h + 2, 1)

            dve.memset(scT[:, 0, :], 0.0)
            dve.memset(scT[:, 1, :], 0.0)
            dve.drain()
            head_gates(0, 0)
            dve.drain()
            for n in (0, 1):
                from_middle(0, 0, n)
            first_levels(0, 0)
            for c in range(3):
                split_cols_low(1, 1, c)
            middle_levels(0, 0)
            head_core(0, 0, first=True)
            with dve.Fori(0, 2) as i:
                head_core(1, 2 * i + 1)
                head_core(0, 2 * i + 2)
            head_core(1, 5)
            head_core(0, 6, splits=False)
            head_core(1, 7, splits=None, last=True)
            head_out(1, 7)
            split_low("hgrn_out")
            for k in range(H_HEADS):
                dve.wait_ge(sig("o_high"), k + 1)
                dve.tensor_tensor(o_lo[:, k, :], oT[:, k, :], o_hi[:, k, :].bitcast(F32), ALU.subtract).then_inc(sig("o_low"), 1)
            split_low("hgrn_out", 1)
            mixer_and_norm("hgrn_out", name=lambda h, t: ((h, t), 0),
                           before_last=lambda: split_low("mlp1"))
            mlp(1)
            ple(1)

            dve.wait_ge(sig("mem_in"), 16)
            for m_ in range(MT):
                stats(mem_tok[:, m_, :], m_, EPS, False).then_inc(sig("mem_ms"), 1)
                dve.wait_ge(sig("mem_root"), m_ + 1)
                dve.reciprocal(ms[:, m_, 2:3], ms[:, m_, 1:2])
                dve.drain()
                dve.tensor_scalar(mem_tok[:, m_, :], mem_tok[:, m_, :], ms[:, m_, 2:3], None, ALU.mult)\
                    .then_inc(sig("mem_normed"), 1)
            for m_ in range(MT):
                b = full("memT", (m_, 1))
                for c in range(4, 8):
                    m = dve.tensor_scalar(memT[:, c, m_ * P:(m_ + 1) * P], psum[:, b, (c - 4) * P:(c - 3) * P],
                                          col_b[:, B_MG + c:B_MG + c + 1], None, ALU.mult)
                m.then_inc(bank_free[b], 1)
            for t in range(NT):
                norm(t, res[:, t, :], rn[:, t, :], EPS, False).then_inc(norm_ready, 1)
                if t:
                    turned_out("norm_mla", t - 1, B_NG)
            turned_out("norm_mla", NT - 1, B_NG)
            norms[0] += 1

            dve.wait_ge(sig("pos_in"), 16)
            dve.tensor_copy(posf, posi[:].bitcast(I32))
            dve.drain()
            freq = con[:, C_FREQ:C_FREQ + HR].unsqueeze(1).broadcast_to([P, NT, HR])
            dve.tensor_tensor(ang, posf.unsqueeze(2).broadcast_to([P, NT, HR]), freq, ALU.mult)
            dve.drain()
            for dst, quarter in ((sinn, 0.0), (cosn, 0.25)):
                dve.tensor_scalar(turns, ang, 1.0 / TWO_PI, quarter, ALU.mult, ALU.add)
                dve.drain()
                dve.tensor_scalar(turns, turns, MAGIC, None, ALU.add)
                dve.drain()
                dve.tensor_scalar(turns, turns, -MAGIC, None, ALU.add)
                dve.drain()
                dve.scalar_tensor_tensor(dst, turns, -PI_A, ang, ALU.mult, ALU.add)
                dve.drain()
                dve.scalar_tensor_tensor(dst, turns, -PI_B, dst, ALU.mult, ALU.add)
                dve.drain()
                dve.scalar_tensor_tensor(dst, turns, -PI_C, dst, ALU.mult, ALU.add)
                dve.drain()
                dve.tensor_scalar(dst, dst, quarter * TWO_PI, None, ALU.add)
                dve.drain()
                m = dve.tensor_scalar(dst, dst, PI_CAP, -PI_CAP, ALU.min, ALU.max)
                if not quarter:
                    dve.drain()
            m.then_inc(sig("angles_ready"), 1)

            def rotate(x1, x2, y1, y2, cos, sin, width):
                shape = list(x1.shape)
                tmp = [rt[:, n, 0:width] if len(shape) == 2 else rt[:, n, 0:width].rearrange("p (h d) -> p h d", d=HR)
                       for n in range(4)]
                for dst, a, w in zip(tmp, (x1, x2, x2, x1), (cos, sin, cos, sin)):
                    dve.tensor_tensor(dst, a, w, ALU.mult)
                dve.drain()
                dve.tensor_tensor(y1, tmp[0], tmp[1], ALU.subtract)
                return dve.tensor_tensor(y2, tmp[2], tmp[3], ALU.add)

            dve.wait_ge(sig("trig_ready"), 1)
            for name, s, width, dst in (("cq", 0, Q_LORA, cq_n), ("ckv", 1, KV_LORA, ckv_n)):
                for t in range(NT):
                    b = full(name, t)
                    r = rstat[:, s, t, :]
                    dve.bn_stats(r[:, 0:6], psum[:, b, 0:width])
                    dve.drain()
                    dve.bn_aggr(r[:, 6:8], r[:, 0:6])
                    dve.drain()
                    dve.scalar_tensor_tensor(r[:, 7:8], r[:, 6:7], r[:, 6:7], r[:, 7:8], ALU.mult, ALU.add)
                    dve.drain()
                    dve.tensor_scalar(r[:, 8:9], r[:, 7:8], EPS, None, ALU.add).then_inc(sig(f"{name}_ms"), 1)
                    if s:
                        m = rotate(psum[:, b, width:width + HR], psum[:, b, width + HR:width + ROPE],
                                   krope[:, t, 0:HR], krope[:, t, HR:ROPE], cosn[:, t, :], sinn[:, t, :], HR)
                        m.then_inc(sig("krope_ready"), 1)
                    dve.wait_ge(sig(f"{name}_root"), t + 1)
                    dve.reciprocal(r[:, 10:11], r[:, 9:10])
                    dve.drain()
                    dve.tensor_scalar(dst[:, t, :], psum[:, b, 0:width], r[:, 10:11], None, ALU.mult).then_inc(bank_free[b], 1)
            for t in range(NT):
                b = full("lora", ("q", t))
                for c in range(KQ):
                    m = dve.tensor_scalar(cqT[:, c, t * P:(t + 1) * P], psum[:, b, c * P:(c + 1) * P],
                                          col_b[:, B_QG + c:B_QG + c + 1], None, ALU.mult)
                m.then_inc(bank_free[b], 1)
            for n in range(3):
                for t in range(NT):
                    b = full("ukv", (n, t))
                    kv = psum[:, b, :].rearrange("p (h s d) -> p h s d", h=4, s=2)
                    k4 = k_tok[:, t, n * 4 * QK:(n + 1) * 4 * QK].rearrange("p (h d) -> p h d", h=4)
                    dve.tensor_copy(k4[:, :, 0:NOPE], kv[:, :, 0, :])
                    dve.tensor_copy(v_tok[:, t, n * 256:(n + 1) * 256].rearrange("p (h d) -> p h d", h=4), kv[:, :, 1, :])\
                        .then_inc(bank_free[b], 1)
            for t in range(NT):
                for n in range(3):
                    wait_taken(dve, "uq", (n, t))
                q3 = q_tok[:, t, :].rearrange("p (h d) -> p h d", h=A_HEADS)
                x1, x2 = q3[:, :, NOPE:NOPE + HR], q3[:, :, NOPE + HR:QK]
                bc = [v[:, t, :].unsqueeze(1).broadcast_to([P, A_HEADS, HR]) for v in (cosn, sinn)]
                rotate(x1, x2, x1, x2, bc[0], bc[1], A_HEADS * HR).then_inc(sig("q_roped"), 1)
                dve.drain()

            def row_max(stage, name, i, par, t, width, scale):
                b = full(stage, name("next_s", t), i)
                dve.tensor_reduce(smx[:, par, 0, t:t + 1], psum[:, b, 0:width], AX.X, ALU.max)
                dve.drain()
                dve.tensor_scalar(smx[:, par, 1, t:t + 1], smx[:, par, 0, t:t + 1], -scale, None, ALU.mult)\
                    .then_inc(sig("max_ready"), 1)

            def softmax(stage, name, i, nth, par, width, nxt, turns, col):
                def prob_turned(t):
                    b = full(stage, name("pt", t), i)
                    weighed = nth * (NT - 1) + (0 if t == 0 else t - 1)
                    if not isinstance(weighed, int) or weighed > 0:
                        dve.wait_ge(sig("tile_weighed"), weighed)
                    dve.tensor_copy(probT[:, t % 2, 0:width], psum[:, b, 0:width]).then_inc(bank_free[b], 1)

                prob_turned(0)
                if turns:
                    b = full(stage, name("qt"), i)
                    dve.tensor_copy(qhT[0:QK, par, :], psum[0:QK, b, :]).then_inc(bank_free[b], 1)
                for t in range(NT):
                    if nxt:
                        row_max(stage, name, i, 1 - par, t, *nxt)
                    if t == 1:
                        prob_turned(2)
                b = full(stage, name("o"), i)
                dve.reciprocal(smx[:, par, 3, :], smx[:, par, 2, :])
                dve.drain()
                dve.tensor_tensor(branch[:, :, col], psum[:, b, 0:NT * V_HEAD].rearrange("p (t d) -> p t d", t=NT),
                                  smx[:, par, 3, :].unsqueeze(2).broadcast_to([P, NT, V_HEAD]), ALU.mult)\
                    .then_inc(bank_free[b], 1)

            of_mem, of_main = (NMEM, M_SCALE), (T, A_SCALE)
            for t in range(NT):
                row_max("first_scores", lambda *n: n, 0, 0, t, *of_mem)
            for h in range(M_HEADS):
                c0 = A_HEADS * V_HEAD + h * V_HEAD
                softmax(f"mem{h}", lambda *n: n, 0, h, h % 2, NMEM, of_mem if h + 1 < M_HEADS else of_main, h >= 2,
                        slice(c0, c0 + V_HEAD))
            with dve.Fori(0, A_HEADS // 2 - 1) as i:
                for par in range(2):
                    softmax("heads", lambda *n, par=par: (par,) + n, i, 2 * i + (par + M_HEADS), par, T, of_main, True,
                            ds(i * (2 * V_HEAD) + par * V_HEAD, V_HEAD))
            for par in range(2):
                h = A_HEADS - 2 + par
                softmax(f"last_head{par}", lambda *n: n, 0, M_HEADS + h, par, T, None if par else of_main, False,
                        slice(h * V_HEAD, (h + 1) * V_HEAD))
            for t in range(NT):
                turned_out("branchT", t)
            dve.wait_ge(gb_in, 16 * 9)
            for h in range(NHALF):
                for t in range(NT):
                    b = full("mla_out", t, h)
                    cols = slice(h * HALF, (h + 1) * HALF)
                    dve.tensor_tensor(rn[:, t, cols], res[:, t, cols], psum[:, b, :], ALU.add).then_inc(bank_free[b], 1)
                    if h == 1:
                        dve.drain()
                        norm(t, rn[:, t, :], res[:, t, :], EPS, False, gb[:, 0, :]).then_inc(sig("out_ready"), 1)

        @block.gpsimd
        def _(pool):
            pool.wait_ge(ssd_small_in, 64)
            pool.wait_ge(sig("decays"), 1)
            with pool.Fori(0, S_GROUPS) as g:
                for m in range(4):
                    pool.wait_ge(sig("xdt_ready"), g * 4 + (m + 1))

                    def heads(ap):
                        return ap[:, :, m * P:(m + 1) * P].rearrange("p t (h d) -> p t h d", h=2)
                    pool.tensor_tensor(heads(xw), heads(xdt), decay_end[:, :, ds(g * S_HPG + 2 * m, 2)].unsqueeze(3)
                                       .broadcast_to([P, NT, 2, S_P]), ALU.mult).then_inc(sig("xw_ready"), 1)
                    pool.tensor_tensor(heads(xr), heads(xr), dskip[:, ds(g * S_HPG + 2 * m, 2)].unsqueeze(1).unsqueeze(3)
                                       .broadcast_to([P, NT, 2, S_P]), ALU.mult).then_inc(sig("xD_ready"), 1)

            def load_gb(n, g, b=None):
                pool.dma_start(gb[:, 0, :], g.partition_broadcast(P)).then_inc(gb_in, 16)
                if b is not None:
                    pool.dma_start(gb[:, 1, :], b.partition_broadcast(P)).then_inc(gb_in, 16)

            def residual(n):
                pool.wait_ge(gb_in, 32 * (n + 1))
                for t in range(NT):
                    pool.wait_ge(norm_ready, NT * n + t + 1)
                    pool.tensor_tensor(res[:, t, :], rn[:, t, :], gb[:, 0, :], ALU.mult).then_inc(sig("res_scaled"), 1)
                    pool.wait_ge(sig("res_scaled"), NT * n + t + 1)
                    pool.tensor_tensor(res[:, t, :], res[:, t, :], gb[:, 1, :], ALU.add).then_inc(res_ready, 1)

            pool.wait_ge(units_begun, 2 * S_GROUPS)
            for n in range(2 * DEPTH):
                if n == 2:
                    with pool.Fori(0, H_HEADS // 2) as i:
                        for par in range(2):
                            h = 2 * i + par
                            pool.wait_ge(sig("ends_ready"), h + 1)
                            pool.wait_ge(sig("k_ready"), h + 1)
                            pool.tensor_tensor(qe, qe, f_q[:, par, :], ALU.mult).then_inc(sig("qe_ready"), 1)
                            pool.tensor_tensor(kend, kend, f_k[:, par, :], ALU.mult).then_inc(sig("kend_ready"), 1)
                if n:
                    pool.wait_ge(res_ready, NT * n)
                load_gb(n, ln_g[n // 2, n % 2], ln_b[n // 2, n % 2])
                residual(n)
            pool.wait_ge(res_ready, NT * 2 * DEPTH)
            load_gb(2 * DEPTH, fin_g)

            for t in range(NT):
                pool.wait_ge(sig("krope_ready"), t + 1)
                k3 = k_tok[:, t, :].rearrange("p (h d) -> p h d", h=A_HEADS)
                pool.tensor_copy(k3[:, :, NOPE:QK], krope[:, t, :].unsqueeze(1).broadcast_to([P, A_HEADS, ROPE]))\
                    .then_inc(sig("k_roped"), 1)
            pool.wait_ge(sig("k_roped"), NT)
            pool.wait_ge(sig("q_roped"), NT)
            for n in range(3):
                for t in range(NT):
                    wait_taken(pool, "ukv", (n, t))

            def head_rows(par, h):
                cols = slice(h * QK, (h + 1) * QK) if isinstance(h, int) else ds(h * QK, QK)
                pool.tensor_copy(hq[:, par, :, :], q_tok[:, :, cols]).then_inc(sig("hq_copied"), 1)
                pool.tensor_copy(hk[:, par, :, :], k_tok[:, :, cols]).then_inc(sig("head_rows"), 1)

            def gated(stage, name, i, col):
                wait_taken(pool, stage, name, i)
                pool.tensor_tensor(branch[:, :, col], branch[:, :, col], gate[:, :, col], ALU.mult)\
                    .then_inc(sig("branch_gated"), 1)

            head_rows(0, 0)
            head_rows(1, 1)
            for h in range(NHALF):
                for t in range(NT):
                    wait_taken(pool, "mgate", (h, t))
            for h in range(M_HEADS):
                if h >= 2:
                    wait_full(pool, f"mem{h}", ("kt",))
                    head_rows(h % 2, h)
                c0 = A_HEADS * V_HEAD + h * V_HEAD
                gated(f"mem{h}", ("o",), 0, slice(c0, c0 + V_HEAD))
            with pool.Fori(0, A_HEADS // 2 - 2) as i:
                for par in range(2):
                    wait_full(pool, "heads", (par, "kt"), i)
                    head_rows(par, 2 * i + (par + 4))
                    gated("heads", (par, "o"), i, ds(i * (2 * V_HEAD) + par * V_HEAD, V_HEAD))
            for h in range(A_HEADS - 4, A_HEADS):
                col = slice(h * V_HEAD, (h + 1) * V_HEAD)
                if h < A_HEADS - 2:
                    gated("heads", (h % 2, "o"), A_HEADS // 2 - 2, col)
                else:
                    gated(f"last_head{h % 2}", ("o",), 0, col)


def kernel(**inputs):
    import concourse.bacc as bacc
    from concourse.bass_utils import run_bass_kernel_spmd

    a = {k: np.asarray(v) for k, v in inputs.items()}
    conv = np.concatenate([a["ssd_conv_w"].reshape(-1, P), a["ssd_conv_b"].reshape(-1, P)])
    par_b = np.concatenate([a[k].reshape(-1, P) for k in
                            ("ln_g", "ln_b", "ssd_norm_w", "norm_g_l0_2", "mem_norm_g_l0_2", "q_norm_g_l0_2",
                             "kv_norm_g_l0_2", "hgrn_norm_w")])
    data = {
        "x": a["x"][0], "p": a["p"][:, 0], "cst": shape_constants(), "par_a": conv, "par_b": par_b,
        "w_ssd": a["ssd_w_in"][0], "w_dt": a["ssd_w_in"][0][:, S_DT:], "dt_bias": a["ssd_dt_bias"][0],
        "a_log": a["ssd_a_log"][0], "d_skip": a["ssd_d"][0], "w_ssd_out": a["ssd_w_out"][0], "w_hgrn": a["hgrn_w_in"][0],
        "w_hgrn_out": a["hgrn_w_out"][0], "ln_g": a["ln_g"], "ln_b": a["ln_b"], "w_mlp1": a["mlp_w1"], "w_mlp2": a["mlp_w2"],
        "w_gate": a["ple_w_gate"], "w_proj": a["ple_w_proj"], "mem": a["mem_2"][0], "pos": a["positions_2"][0],
        "w_mla": a["w_in_l0_2"], "w_uq": a["w_uq_l0_2"], "w_ukv": a["w_ukv_l0_2"], "w_mem": a["w_mem_kv_l0_2"],
        "w_mla_out": a["w_out_l0_2"], "fin_g": a["final_norm_g_2"],
    }
    data = {k: np.ascontiguousarray(v) for k, v in data.items()}
    nc = bacc.Bacc("TRN2", target_bir_lowering=False, num_devices=1)
    args = {k: nc.dram_tensor(f"in_{k}", v.shape, mybir.dt.from_np(v.dtype), kind="ExternalInput").ap() for k, v in data.items()}
    out = nc.dram_tensor("out_rows", (T, D), F32, kind="ExternalOutput").ap()
    build(nc, **args, out=out)
    r = run_bass_kernel_spmd(nc, [{f"in_{k}": v for k, v in data.items()}], core_ids=[0])
    return r.results[0]["out_rows"].reshape(1, T, D)
```
